# Optimizing a Trainium2 kernel written in Bass

```python
import math
import jax
import jax.numpy as jnp
from jax import lax
import numpy as np
import jax, jax.numpy as jnp

D_MODEL = 1024
BATCH = 1
SEQ = 1024
DEPTH = 1

N_MIXERS = 2
EPS = 1e-6

GDN_QK_HEADS = 8
GDN_V_HEADS = 16
GDN_HEAD_DIM = 128
GDN_CONV = 4
GDN_CHUNK = 64
GDN_QK_W = GDN_QK_HEADS * GDN_HEAD_DIM
GDN_V_W = GDN_V_HEADS * GDN_HEAD_DIM
GDN_CONV_W = 2 * GDN_QK_W + GDN_V_W
GDN_IN = GDN_CONV_W + GDN_V_W + 2 * GDN_V_HEADS

NSA_HEADS = 16
NSA_GROUPS = 4
NSA_HPG = NSA_HEADS // NSA_GROUPS
NSA_HEAD_DIM = 64
NSA_CMP_LEN = 32
NSA_CMP_STRIDE = 16
NSA_SLC_LEN = 64
NSA_TOP_K = 8
NSA_WINDOW = 512
NSA_QBLOCK = 128
NSA_Q_W = NSA_HEADS * NSA_HEAD_DIM
NSA_KV_W = NSA_GROUPS * NSA_HEAD_DIM
NSA_IN = 2 * NSA_Q_W + 6 * NSA_KV_W + 3 * NSA_HEADS

REL_BUCKETS = 32
REL_MAX_DIST = 128
NEG_INF = -1e30


def rms_norm(x, g):
    xf = x.astype(jnp.float32)
    y = xf * lax.rsqrt(jnp.mean(xf * xf, axis=-1, keepdims=True) + EPS)
    return (y * g.astype(jnp.float32)).astype(x.dtype)

def l2norm(x):
    return x * lax.rsqrt(jnp.sum(x * x, axis=-1, keepdims=True) + EPS)

def rel_bucket(dist):
    n = jnp.maximum(dist, 0)
    max_exact = REL_BUCKETS // 2
    nf = jnp.maximum(n, 1).astype(jnp.float32)
    large = max_exact + (jnp.log(nf / max_exact) / math.log(REL_MAX_DIST / max_exact)
                         * (REL_BUCKETS - max_exact)).astype(jnp.int32)
    large = jnp.minimum(large, REL_BUCKETS - 1)
    return jnp.where(n < max_exact, n, large)

def head_bias(rel_bias, dist):
    b = rel_bias[rel_bucket(dist)]
    return jnp.transpose(b, (2, 0, 1)).reshape(NSA_GROUPS, NSA_HPG, dist.shape[0], dist.shape[1])

def causal_depthwise_conv(x, w):
    kw, ch = w.shape
    return lax.conv_general_dilated(x, w[:, None, :].astype(x.dtype), window_strides=(1,),
                                    padding=[(kw - 1, 0)], dimension_numbers=('NWC', 'WIO', 'NWC'),
                                    feature_group_count=ch)

def gated_deltanet(h, w_in, conv_w, a_log, dt_bias, norm_w, w_out):
    bsz, t, _ = h.shape
    nh, dh, cs = GDN_V_HEADS, GDN_HEAD_DIM, GDN_CHUNK
    nc = t // cs
    f32 = jnp.float32
    proj = h @ w_in
    qkv, z, b_lin, a_lin = jnp.split(proj, [GDN_CONV_W, GDN_CONV_W + GDN_V_W, GDN_CONV_W + GDN_V_W + nh], axis=-1)
    qkv = jax.nn.silu(causal_depthwise_conv(qkv, conv_w)).astype(f32)
    q, k, v = jnp.split(qkv, [GDN_QK_W, 2 * GDN_QK_W], axis=-1)
    rep = nh // GDN_QK_HEADS
    q = jnp.repeat(l2norm(q.reshape(bsz, t, GDN_QK_HEADS, dh)), rep, axis=2) * (dh ** -0.5)
    k = jnp.repeat(l2norm(k.reshape(bsz, t, GDN_QK_HEADS, dh)), rep, axis=2)
    v = v.reshape(bsz, t, nh, dh)
    beta = jax.nn.sigmoid(b_lin.astype(f32))
    g = -jnp.exp(a_log.astype(f32)) * jax.nn.softplus(a_lin.astype(f32) + dt_bias.astype(f32))
    to_chunks = lambda u: u.reshape(bsz, nc, cs, nh, -1).transpose(0, 3, 1, 2, 4)
    q, k, v = to_chunks(q), to_chunks(k), to_chunks(v)
    beta = to_chunks(beta)[..., 0]
    gc = jnp.cumsum(to_chunks(g)[..., 0], axis=-1)
    idx = jnp.arange(cs)
    lower = idx[:, None] >= idx[None, :]
    strict = idx[:, None] > idx[None, :]
    decay = jnp.exp(jnp.where(lower, gc[..., :, None] - gc[..., None, :], -jnp.inf))
    kb = k * beta[..., None]
    a_mat = jnp.where(strict, jnp.einsum('bhncd,bhnsd->bhncs', kb, k) * decay, 0.0)
    eye = jnp.eye(cs, dtype=f32)
    l_mat = a_mat + eye
    t_mat = lax.linalg.triangular_solve(l_mat, jnp.broadcast_to(eye, l_mat.shape), left_side=True,
                                        lower=True, unit_diagonal=True)
    u = jnp.einsum('bhncs,bhnsd->bhncd', t_mat, v * beta[..., None])
    w = jnp.einsum('bhncs,bhnsd->bhncd', t_mat, kb * jnp.exp(gc)[..., None])
    qk = jnp.where(lower, jnp.einsum('bhncd,bhnsd->bhncs', q, k) * decay, 0.0)
    g_last = gc[..., -1]
    k_dec = k * jnp.exp(g_last[..., None] - gc)[..., None]
    q_dec = q * jnp.exp(gc)[..., None]
    xs = tuple(jnp.moveaxis(a, 2, 0) for a in (q_dec, qk, u, w, k_dec, jnp.exp(g_last)))

    def step(state, inp):
        qd, qkc, uc, wc, kd, gl = inp
        v_new = uc - jnp.einsum('bhcd,bhde->bhce', wc, state)
        o = jnp.einsum('bhcd,bhde->bhce', qd, state) + jnp.einsum('bhcs,bhse->bhce', qkc, v_new)
        state = state * gl[..., None, None] + jnp.einsum('bhcd,bhce->bhde', kd, v_new)
        return state, o

    s0 = jnp.zeros((bsz, nh, dh, dh), f32)
    _, o = lax.scan(step, s0, xs)
    o = o.transpose(1, 0, 3, 2, 4).reshape(bsz, t, nh, dh)
    o = rms_norm(o, norm_w) * jax.nn.silu(z.reshape(bsz, t, nh, dh).astype(f32))
    return o.reshape(bsz, t, nh * dh).astype(h.dtype) @ w_out

def native_sparse_attention(h, w_in, cmp_pos, cmp_w1, cmp_w2, rel_bias, w_out):
    bsz, t, _ = h.shape
    nh, ng, hpg, dh = NSA_HEADS, NSA_GROUPS, NSA_HPG, NSA_HEAD_DIM
    f32 = jnp.float32
    proj = h @ w_in
    q = proj[..., :NSA_Q_W].reshape(bsz, t, ng, hpg, dh).transpose(0, 2, 3, 1, 4) * (dh ** -0.5)
    kv = proj[..., NSA_Q_W:NSA_Q_W + 6 * NSA_KV_W].reshape(bsz, t, 6, ng, dh)
    kc, vc, ks, vs, kw, vw = [kv[:, :, i] for i in range(6)]
    off = NSA_Q_W + 6 * NSA_KV_W
    gates = jax.nn.sigmoid(proj[..., off:off + 3 * nh].astype(f32)).reshape(bsz, t, ng, hpg, 3)
    gates = gates.transpose(0, 2, 3, 1, 4)
    z = proj[..., off + 3 * nh:]

    n_cmp = (t - NSA_CMP_LEN) // NSA_CMP_STRIDE + 1
    tok = jnp.arange(n_cmp)[:, None] * NSA_CMP_STRIDE + jnp.arange(NSA_CMP_LEN)[None, :]

    def compress(xk, i):
        blk = xk[:, tok] + cmp_pos[i][None, None, :, None, :]
        blk = blk.transpose(0, 1, 3, 2, 4).reshape(bsz, n_cmp, ng, NSA_CMP_LEN * dh)
        return (jax.nn.silu(blk @ cmp_w1[i]) @ cmp_w2[i]).transpose(0, 2, 1, 3)

    k_cmp = compress(kc, 0)
    v_cmp = compress(vc, 1)
    cmp_end = jnp.arange(n_cmp) * NSA_CMP_STRIDE + NSA_CMP_LEN - 1

    n_slc = t // NSA_SLC_LEN
    k_sel = min(NSA_TOP_K, n_slc)
    c_start = jnp.arange(n_cmp)[:, None] * NSA_CMP_STRIDE
    s_start = jnp.arange(n_slc)[None, :] * NSA_SLC_LEN
    overlap = (jnp.clip(jnp.minimum(c_start + NSA_CMP_LEN, s_start + NSA_SLC_LEN) - jnp.maximum(c_start, s_start), 0)
               .astype(f32) / NSA_CMP_LEN)
    ks_blk = ks.reshape(bsz, n_slc, NSA_SLC_LEN, ng, dh).transpose(0, 3, 1, 2, 4)
    vs_blk = vs.reshape(bsz, n_slc, NSA_SLC_LEN, ng, dh).transpose(0, 3, 1, 2, 4)
    gather = jax.vmap(jax.vmap(lambda kb, ix: kb[ix]))
    tbl = rel_bias.T.reshape(ng, hpg, REL_BUCKETS)
    gi = jnp.arange(ng)[None, :, None, None, None]
    hi = jnp.arange(hpg)[None, None, :, None, None]
    blk_id = jnp.arange(n_slc)

    pad = ((0, 0), (0, 0), (NSA_WINDOW, 0), (0, 0))
    kw_p = jnp.pad(kw.transpose(0, 2, 1, 3), pad)
    vw_p = jnp.pad(vw.transpose(0, 2, 1, 3), pad)

    def query_block(bi):
        q0 = bi * NSA_QBLOCK
        qb = lax.dynamic_slice_in_dim(q, q0, NSA_QBLOCK, axis=3)
        gb = lax.dynamic_slice_in_dim(gates, q0, NSA_QBLOCK, axis=3)
        tq = q0 + jnp.arange(NSA_QBLOCK)
        dist = tq[:, None] - cmp_end[None, :]
        valid = dist >= 0
        s = jnp.einsum('bghqd,bgkd->bghqk', qb, k_cmp).astype(f32) + head_bias(rel_bias, dist)
        s = jnp.where(valid, s, NEG_INF)
        p_cmp = jax.nn.softmax(s, axis=-1) * jnp.any(valid, axis=-1)[:, None].astype(f32)
        o_cmp = jnp.einsum('bghqk,bgkd->bghqd', p_cmp.astype(v_cmp.dtype), v_cmp)
        imp = jnp.einsum('bghqk,ks->bgqs', p_cmp, overlap)
        cur = tq // NSA_SLC_LEN
        forced = (blk_id[None, :] == 0) | (blk_id[None, :] == cur[:, None]) | (blk_id[None, :] == cur[:, None] - 1)
        causal_blk = blk_id[None, :] * NSA_SLC_LEN <= tq[:, None]
        imp = jnp.where(forced, jnp.inf, jnp.where(causal_blk, imp, -jnp.inf))
        _, sel = lax.top_k(imp, k_sel)
        n_s = k_sel * NSA_SLC_LEN
        k_g = gather(ks_blk, sel).reshape(bsz, ng, NSA_QBLOCK, n_s, dh)
        v_g = gather(vs_blk, sel).reshape(bsz, ng, NSA_QBLOCK, n_s, dh)
        pos = (sel[..., None] * NSA_SLC_LEN + jnp.arange(NSA_SLC_LEN)).reshape(bsz, ng, NSA_QBLOCK, n_s)
        dist_s = tq[None, None, :, None] - pos
        s = jnp.einsum('bghqd,bgqsd->bghqs', qb, k_g).astype(f32) + tbl[gi, hi, rel_bucket(dist_s)[:, :, None]]
        s = jnp.where((dist_s >= 0)[:, :, None], s, NEG_INF)
        o_slc = jnp.einsum('bghqs,bgqsd->bghqd', jax.nn.softmax(s, axis=-1).astype(v_g.dtype), v_g)
        kwb = lax.dynamic_slice_in_dim(kw_p, q0, NSA_WINDOW + NSA_QBLOCK, axis=2)
        vwb = lax.dynamic_slice_in_dim(vw_p, q0, NSA_WINDOW + NSA_QBLOCK, axis=2)
        tk = q0 - NSA_WINDOW + jnp.arange(NSA_WINDOW + NSA_QBLOCK)
        dist_w = tq[:, None] - tk[None, :]
        valid_w = (dist_w >= 0) & (dist_w < NSA_WINDOW) & (tk[None, :] >= 0)
        s = jnp.einsum('bghqd,bgkd->bghqk', qb, kwb).astype(f32) + head_bias(rel_bias, dist_w)
        s = jnp.where(valid_w, s, NEG_INF)
        o_win = jnp.einsum('bghqk,bgkd->bghqd', jax.nn.softmax(s, axis=-1).astype(vwb.dtype), vwb)
        return (gb[..., 0:1] * o_cmp.astype(f32) + gb[..., 1:2] * o_slc.astype(f32)
                + gb[..., 2:3] * o_win.astype(f32))

    outs = lax.map(query_block, jnp.arange(t // NSA_QBLOCK))
    o = outs.transpose(1, 0, 4, 2, 3, 5).reshape(bsz, t, nh * dh)
    o = o * jax.nn.silu(z.astype(f32))
    return o.astype(h.dtype) @ w_out

def first_inputs(seed: int = 0) -> dict:
    key = jax.random.key(seed)
    ks = jax.random.split(key, 20)
    n_a = (DEPTH + N_MIXERS - 1) // N_MIXERS
    n_b = DEPTH // N_MIXERS
    nrm = lambda k, shape, scale: jax.random.normal(k, shape, jnp.float32) * scale
    dt = jnp.exp(jax.random.uniform(ks[7], (n_a, GDN_V_HEADS), jnp.float32, math.log(1e-3), math.log(1e-1)))
    return {
        'x': nrm(ks[0], (BATCH, SEQ, D_MODEL), 1.0),
        'c': nrm(ks[1], (BATCH, D_MODEL), 1.0),
        'ada_w': nrm(ks[2], (DEPTH, D_MODEL, 3 * D_MODEL), D_MODEL ** -0.5),
        'ada_b': nrm(ks[3], (DEPTH, 3 * D_MODEL), 0.01),
        'norm_g': 1.0 + nrm(ks[4], (DEPTH, D_MODEL), 0.05),
        'gdn_w_in': nrm(ks[5], (n_a, D_MODEL, GDN_IN), D_MODEL ** -0.5),
        'gdn_conv_w': nrm(ks[6], (n_a, GDN_CONV, GDN_CONV_W), GDN_CONV ** -0.5),
        'gdn_a_log': jnp.log(jax.random.uniform(ks[8], (n_a, GDN_V_HEADS), jnp.float32, 1.0, 16.0)),
        'gdn_dt_bias': dt + jnp.log(-jnp.expm1(-dt)),
        'gdn_norm_w': 1.0 + nrm(ks[9], (n_a, GDN_HEAD_DIM), 0.05),
        'gdn_w_out': nrm(ks[10], (n_a, GDN_V_W, D_MODEL), GDN_V_W ** -0.5),
        'nsa_w_in': nrm(ks[11], (n_b, D_MODEL, NSA_IN), D_MODEL ** -0.5),
        'nsa_cmp_pos': nrm(ks[12], (n_b, 2, NSA_CMP_LEN, NSA_HEAD_DIM), 0.1),
        'nsa_cmp_w1': nrm(ks[13], (n_b, 2, NSA_CMP_LEN * NSA_HEAD_DIM, NSA_HEAD_DIM), (NSA_CMP_LEN * NSA_HEAD_DIM) ** -0.5),
        'nsa_cmp_w2': nrm(ks[14], (n_b, 2, NSA_HEAD_DIM, NSA_HEAD_DIM), NSA_HEAD_DIM ** -0.5),
        'nsa_w_out': nrm(ks[15], (n_b, NSA_Q_W, D_MODEL), NSA_Q_W ** -0.5),
        'rel_bias': nrm(ks[16], (REL_BUCKETS, NSA_HEADS), 0.5),
        'final_g': 1.0 + nrm(ks[17], (D_MODEL,), 0.05),
    }

def first_block(x, c, ada_w, ada_b, norm_g, gdn_w_in, gdn_conv_w, gdn_a_log, gdn_dt_bias, gdn_norm_w, gdn_w_out,
              nsa_w_in, nsa_cmp_pos, nsa_cmp_w1, nsa_cmp_w2, nsa_w_out, rel_bias, final_g):
    cond = jax.nn.silu(c)
    for i in range(DEPTH):
        mod = cond @ ada_w[i] + ada_b[i]
        shift, scale, gate = jnp.split(mod, 3, axis=-1)
        hdn = rms_norm(x, norm_g[i]) * (1.0 + scale[:, None, :]) + shift[:, None, :]
        j = i // N_MIXERS
        if i % N_MIXERS == 0:
            y = gated_deltanet(hdn, gdn_w_in[j], gdn_conv_w[j], gdn_a_log[j], gdn_dt_bias[j], gdn_norm_w[j], gdn_w_out[j])
        else:
            y = native_sparse_attention(hdn, nsa_w_in[j], nsa_cmp_pos[j], nsa_cmp_w1[j], nsa_cmp_w2[j], rel_bias, nsa_w_out[j])
        x = x + gate[:, None, :] * y
    return rms_norm(x, final_g)


N_HEADS_A = 4
HEAD_DIM_A = 64
W_A = N_HEADS_A * 2 * HEAD_DIM_A
N_HEADS_B = 4
HEAD_DIM_B = D_MODEL // 8
W_B = N_HEADS_B * HEAD_DIM_B
CONV_W = 4
Q_BLOCK = 128
MLSTM_CHUNK = 64
N_IN = 4 * W_A + 5 * W_B + 2 * N_HEADS_B + 2 * D_MODEL


def _rmsnorm(x, g):
    xf = x.astype(jnp.float32)
    y = xf * lax.rsqrt(jnp.mean(xf * xf, axis=-1, keepdims=True) + EPS)
    return (y * g.astype(jnp.float32)).astype(x.dtype)

def _split(t, sizes):
    idx = np.cumsum(sizes)[:-1].tolist()
    return jnp.split(t, idx, axis=-1)

def _causal_conv(x, w):
    S = x.shape[1]
    xp = jnp.pad(x, ((0, 0), (CONV_W - 1, 0), (0, 0)))
    y = xp[:, 0:S] * w[0]
    for k in range(1, CONV_W):
        y = y + xp[:, k:k + S] * w[k]
    return y

def _alibi_slopes(n_heads):
    return 2.0 ** (-8.0 * jnp.arange(1, n_heads + 1, dtype=jnp.float32) / n_heads)

def _diff_attention(q, k, v, lam):
    B, S, _ = q.shape
    H, d = N_HEADS_A, HEAD_DIM_A
    qh = q.reshape(B, S, H, 2, d).transpose(0, 2, 3, 1, 4)
    kh = k.reshape(B, S, H, 2, d).transpose(0, 2, 3, 1, 4)
    vh = v.reshape(B, S, H, 2 * d).transpose(0, 2, 1, 3)
    nb = S // Q_BLOCK
    q_blocks = qh.reshape(B, H, 2, nb, Q_BLOCK, d).transpose(3, 0, 1, 2, 4, 5)
    slopes = _alibi_slopes(H)
    s_pos = jnp.arange(S)
    scale = d ** -0.5

    def block(args):
        q_blk, i = args
        t_pos = i * Q_BLOCK + jnp.arange(Q_BLOCK)
        dist = (t_pos[:, None] - s_pos[None, :]).astype(jnp.float32)
        bias = jnp.where(dist >= 0, -slopes[:, None, None] * dist, -jnp.inf)
        scores = jnp.einsum('bhcqd,bhcsd->bhcqs', q_blk, kh,
                            preferred_element_type=jnp.float32) * scale + bias[None, :, None]
        p = jax.nn.softmax(scores, axis=-1)
        p = p[:, :, 0] - lam * p[:, :, 1]
        return jnp.einsum('bhqs,bhse->bhqe', p.astype(vh.dtype), vh)

    out = lax.map(block, (q_blocks, jnp.arange(nb)))
    return out.transpose(1, 0, 3, 2, 4).reshape(B, S, H, 2 * d)

def _mlstm(q, k, v, ig, fg):
    B, S, _ = q.shape
    H, d, L = N_HEADS_B, HEAD_DIM_B, MLSTM_CHUNK
    nc = S // L

    def heads(t):
        return t.astype(jnp.float32).reshape(B, nc, L, H, d).transpose(1, 0, 3, 2, 4)

    def gates(t):
        return t.astype(jnp.float32).reshape(B, nc, L, H).transpose(1, 0, 3, 2)

    qc, kc, vc = heads(q), heads(k) * (d ** -0.5), heads(v)
    igc = gates(ig)
    lfc = jax.nn.log_sigmoid(gates(fg))
    causal = jnp.tril(jnp.ones((L, L), dtype=bool))

    def body(carry, xs):
        C, n, m = carry
        qj, kj, vj, ij, lj = xs
        b = jnp.cumsum(lj, axis=-1)
        logD = b[..., :, None] - b[..., None, :] + ij[..., None, :]
        logD = jnp.where(causal, logD, -jnp.inf)
        inter = b + m[..., None]
        m_row = jnp.maximum(inter, jnp.max(logD, axis=-1))
        Dm = jnp.exp(logD - m_row[..., None])
        w_inter = jnp.exp(inter - m_row)
        Sm = jnp.einsum('bhjd,bhsd->bhjs', qj, kj) * Dm
        num = jnp.einsum('bhjs,bhse->bhje', Sm, vj) + w_inter[..., None] * jnp.einsum('bhjd,bhde->bhje', qj, C)
        den = jnp.sum(Sm, axis=-1) + w_inter * jnp.einsum('bhjd,bhd->bhj', qj, n)
        h = num / jnp.maximum(jnp.abs(den), jnp.exp(-m_row))[..., None]
        bL = b[..., -1]
        a = bL[..., None] - b + ij
        m_new = jnp.maximum(bL + m, jnp.max(a, axis=-1))
        decay = jnp.exp(bL + m - m_new)
        wk = jnp.exp(a - m_new[..., None])
        C_new = decay[..., None, None] * C + jnp.einsum('bhs,bhsd,bhse->bhde', wk, kj, vj)
        n_new = decay[..., None] * n + jnp.einsum('bhs,bhsd->bhd', wk, kj)
        return (C_new, n_new, m_new), h

    init = (jnp.zeros((B, H, d, d), jnp.float32), jnp.zeros((B, H, d), jnp.float32),
            jnp.zeros((B, H), jnp.float32))
    _, hs = lax.scan(body, init, (qc, kc, vc, igc, lfc))
    return hs.transpose(1, 0, 3, 2, 4).reshape(B, S, H, d)

def second_inputs(seed: int = 0) -> dict:
    key = jax.random.key(seed)
    ks = jax.random.split(key, 14)
    nrm = jax.random.normal
    x = nrm(ks[0], (BATCH, SEQ, D_MODEL), jnp.float32)
    norm_pre = 1.0 + 0.05 * nrm(ks[1], (DEPTH, D_MODEL), jnp.float32)
    norm_post = 1.0 + 0.05 * nrm(ks[2], (DEPTH, D_MODEL), jnp.float32)
    w_in = nrm(ks[3], (DEPTH, D_MODEL, N_IN), jnp.float32) * D_MODEL ** -0.5
    b_i = 0.1 * nrm(ks[4], (DEPTH, N_HEADS_B), jnp.float32)
    b_f = jnp.linspace(3.0, 6.0, N_HEADS_B, dtype=jnp.float32)[None, :] + 0.01 * nrm(ks[5], (DEPTH, N_HEADS_B), jnp.float32)
    b_if = jnp.concatenate([b_i, b_f], axis=-1)
    conv_qk = nrm(ks[6], (DEPTH, CONV_W, 2 * W_B), jnp.float32) * CONV_W ** -0.5
    lambda_qk = 0.1 * nrm(ks[7], (DEPTH, 4, HEAD_DIM_A), jnp.float32)
    norm_a = 1.0 + 0.05 * nrm(ks[8], (DEPTH, W_A), jnp.float32)
    norm_b = 1.0 + 0.05 * nrm(ks[9], (DEPTH, W_B), jnp.float32)
    w_a = nrm(ks[10], (DEPTH, W_A, D_MODEL), jnp.float32) * W_A ** -0.5
    w_b = nrm(ks[11], (DEPTH, W_B, D_MODEL), jnp.float32) * W_B ** -0.5
    w_out = nrm(ks[12], (DEPTH, D_MODEL, D_MODEL), jnp.float32) * D_MODEL ** -0.5
    return {"x": x, "norm_pre": norm_pre, "norm_post": norm_post, "w_in": w_in,
            "b_if": b_if, "conv_qk": conv_qk, "lambda_qk": lambda_qk,
            "norm_a": norm_a, "norm_b": norm_b, "w_a": w_a, "w_b": w_b, "w_out": w_out}

def second_block(x, norm_pre, norm_post, w_in, b_if, conv_qk, lambda_qk, norm_a, norm_b, w_a, w_b, w_out):
    B, S, _ = x.shape
    H_A, H_B = N_HEADS_A, N_HEADS_B
    sizes = [W_A, W_A, W_A, W_A, W_B, W_B, W_B, W_B, W_B, H_B, H_B, D_MODEL, D_MODEL]
    for l in range(DEPTH):
        h = _rmsnorm(x, norm_pre[l])
        proj = jnp.einsum('bsd,dn->bsn', h, w_in[l])
        qa, ka, va, za, qb, kb, vb, ob, zb, igb, fgb, ga, gb = _split(proj, sizes)

        lam_init = 0.8 - 0.6 * math.exp(-0.3 * l)
        lq = lambda_qk[l].astype(jnp.float32)
        lam = jnp.exp(jnp.sum(lq[0] * lq[1])) - jnp.exp(jnp.sum(lq[2] * lq[3])) + lam_init
        oa = _diff_attention(qa, ka, va, lam)
        oa = _rmsnorm(oa, norm_a[l].reshape(H_A, 2 * HEAD_DIM_A)) * (1.0 - lam_init)
        ya = oa.reshape(B, S, W_A) * jax.nn.silu(za)

        qk = jax.nn.silu(_causal_conv(jnp.concatenate([qb, kb], axis=-1), conv_qk[l]))
        qb_c, kb_c = qk[..., :W_B], qk[..., W_B:]
        ig = igb + b_if[l, :H_B]
        fg = fgb + b_if[l, H_B:]
        hb = _mlstm(qb_c, kb_c, vb, ig, fg)
        hb = jax.nn.sigmoid(ob.astype(jnp.float32)).reshape(B, S, H_B, HEAD_DIM_B) * hb
        hb = _rmsnorm(hb, norm_b[l].reshape(H_B, HEAD_DIM_B)).astype(x.dtype)
        yb = hb.reshape(B, S, W_B) * jax.nn.silu(zb)

        merged = (jax.nn.sigmoid(ga) * jnp.einsum('bsw,wd->bsd', ya, w_a[l])
                  + jax.nn.sigmoid(gb) * jnp.einsum('bsw,wd->bsd', yb, w_b[l]))
        out = jnp.einsum('bsd,de->bse', merged, w_out[l])
        x = x + _rmsnorm(out, norm_post[l])
    return x


def setup_inputs(seed=0):
    out = dict(first_inputs(seed))
    for name, value in second_inputs(seed + 1).items():
        if name != "x":
            out[name + "_2"] = value
    return out


def reference(
    x, c, ada_w, ada_b, norm_g, gdn_w_in, gdn_conv_w, gdn_a_log, gdn_dt_bias, gdn_norm_w,
    gdn_w_out, nsa_w_in, nsa_cmp_pos, nsa_cmp_w1, nsa_cmp_w2, nsa_w_out, rel_bias, final_g,
    norm_pre_2, norm_post_2, w_in_2, b_if_2, conv_qk_2, lambda_qk_2, norm_a_2, norm_b_2, w_a_2,
    w_b_2, w_out_2,
):
    x = first_block(
        x, c, ada_w, ada_b, norm_g, gdn_w_in, gdn_conv_w, gdn_a_log, gdn_dt_bias, gdn_norm_w,
        gdn_w_out, nsa_w_in, nsa_cmp_pos, nsa_cmp_w1, nsa_cmp_w2, nsa_w_out, rel_bias, final_g,
    )
    return second_block(
        x, norm_pre_2, norm_post_2, w_in_2, b_if_2, conv_qk_2, lambda_qk_2, norm_a_2, norm_b_2,
        w_a_2, w_b_2, w_out_2,
    )


_drawn_inputs = setup_inputs


def setup_inputs(seed=0):
    import zlib

    import numpy as np

    out = dict(_drawn_inputs(seed))
    spreads = {}
    factors = {'ada_b': 3.06}
    for name, (base, spread) in spreads.items():
        noise = np.random.default_rng([zlib.crc32(name.encode()), seed]).standard_normal(out[name].shape)
        drawn = base * np.exp(spread * noise) if base else spread * noise
        out[name] = jnp.asarray(drawn.astype(out[name].dtype))
    for name, factor in factors.items():
        out[name] = (out[name] * factor).astype(out[name].dtype)
    return out
```

```python
from contextlib import ExitStack

import numpy as np

import concourse.bass as bass
from concourse import mybir

F32 = mybir.dt.float32
F32R = mybir.dt.float32r
ALU = mybir.AluOpType
ACT = mybir.ActivationFunctionType
AX = mybir.AxisListType.X

P = 128
D = 1024
T = 1024
KD = D // P
NT = T // P
HALF = 512
EPS = 1e-6
QK_HEADS = 8
V_HEADS = 16
DH = 128
LEVELS = 7
HA, DA = 4, 64
HB = 4
TAPS = 4
NEG = -1.0e30


def bc(ap, axis, n):
    ap = ap.unsqueeze(axis)
    shape = list(ap.shape)
    shape[axis] = n
    return ap.broadcast_to(shape)


def stage_norm(nc, ctx, io, keep):
    def sb(name, shape, dt=F32):
        return own.enter_context(nc.sbuf_tensor(name, shape, dt))

    own = ExitStack()
    with own:
        sem = lambda name: ctx.enter_context(nc.semaphore(name))
        x_sb = sb("x_sb", [P, KD, T])
        ada = sb("ada", [P, 4, KD * P])
        c_col = sb("c_col", [P, KD])
        cond = sb("cond", [P, KD])
        ada_b = sb("ada_b", [P, 3 * KD])
        g_col = sb("g_col", [P, KD])
        mod = sb("mod", [P, 3 * KD])
        gain = sb("gain", [P, KD])
        sq = sb("sq", [P, 2, T])
        rinv = sb("rinv", [P, T])
        xn = sb("xn", [P, 2, T])
        h = sb("h", [P, 2, T])
        ps_ss = [own.enter_context(nc.psum_tensor(f"ps_ss{i}", [P, HALF], F32)) for i in range(2)]
        ps_mod = own.enter_context(nc.psum_tensor("ps_mod", [P, HALF], F32))
        h_hi, h_lo = keep["h_hi"], keep["h_lo"]

        small_in = sem("a_small_in")
        x_in = [sem(f"a_x_in{i}") for i in range(KD)]
        ada_in = [sem(f"a_ada_in{i}") for i in range(4)]
        const_in = keep["const_in"]
        eps_set = keep["eps_set"]
        cond_done = sem("a_cond_done")
        sq_done = sem("a_sq_done")
        ss_done = sem("a_ss_done")
        ln_done = sem("a_ln_done")
        rinv_done = sem("a_rinv_done")
        mod_tile = sem("a_mod_tile")
        mod_done = sem("a_mod_done")
        xn_done = sem("a_xn_done")
        h_done = sem("a_h_done")
        hi_done = sem("a_hi_done")
        lo_done = sem("a_lo_done")

        with nc.Block() as block:
            @block.sync
            def _(sp):
                for dst, src in ((c_col, io["c"]), (ada_b, io["ada_b"]), (g_col, io["norm_g"])):
                    sp.dma_start(dst[:], src).then_inc(small_in, 16)
                for dst, src in ((keep["ones"], io["ones"]), (keep["ident"], io["ident"])):
                    sp.dma_start(dst[:], src).then_inc(const_in, 16)
                for k in range(KD):
                    sp.dma_start(x_sb[:, k, :], io["xT"][:, k, :]).then_inc(x_in[k], 16)
                for n in range(3 * KD):
                    if n >= 4:
                        sp.wait_ge(mod_tile, n - 3)
                    sp.dma_start(ada[:, n % 4, :], io["ada_w"][n]).then_inc(ada_in[n % 4], 16)
                sp.wait_ge(lo_done, KD)

            @block.gpsimd
            def _(pool):
                for k in range(KD):
                    pool.wait_ge(hi_done, k + 1)
                    nc.gpsimd.tensor_tensor(h_lo[:, k, :], h[:, k % 2, :],
                                            h_hi[:, k, :].bitcast(F32), ALU.subtract).then_inc(lo_done, 1)

            @block.scalar
            def _(act):
                act.wait_ge(small_in, 48)
                nc.scalar.activation(cond[:], c_col[:], ACT.Silu).then_inc(cond_done, 1)
                for k in range(KD):
                    act.wait_ge(x_in[k], 16)
                    if k >= 2:
                        act.wait_ge(ss_done, k - 1)
                    nc.scalar.activation(sq[:, k % 2, :], x_sb[:, k, :], ACT.Square).then_inc(sq_done, 1)
                act.wait_ge(ss_done, KD)
                act.wait_ge(eps_set, 1)
                for i in range(2):
                    nc.scalar.activation(rinv[:, i * HALF:(i + 1) * HALF], ps_ss[i][:], ACT.Ln,
                                         scale=1.0 / D, bias=keep["eps"][:, 0:1]).then_inc(ln_done, 1)
                act.wait_ge(ln_done, 2)
                nc.scalar.activation(rinv[:], rinv[:], ACT.Exp, scale=-0.5).then_inc(rinv_done, 1)
                act.wait_ge(mod_done, 4)
                for k in range(KD):
                    act.wait_ge(xn_done, k + 1)
                    if k >= 2:
                        act.wait_ge(lo_done, k - 1)
                    nc.scalar.activation(h[:, k % 2, :], xn[:, k % 2, :], ACT.Identity,
                                         scale=gain[:, k:k + 1], bias=mod[:, k:k + 1]).then_inc(h_done, 1)

            @block.tensor
            def _(pe):
                pe.wait_ge(const_in, 32)
                for k in range(KD):
                    pe.wait_ge(sq_done, k + 1)
                    for i in range(2):
                        last = nc.tensor.matmul(ps_ss[i][:], keep["ones"][:], sq[:, k % 2, i * HALF:(i + 1) * HALF],
                                                start=(k == 0), stop=(k == KD - 1))
                    last.then_inc(ss_done, 1)
                pe.wait_ge(cond_done, 1)
                for n in range(3 * KD):
                    pe.wait_ge(ada_in[n % 4], 16 * (n // 4 + 1))
                    for k in range(KD):
                        last = nc.tensor.matmul(ps_mod[:, n:n + 1], ada[:, n % 4, k * P:(k + 1) * P],
                                                cond[:, k:k + 1], start=(k == 0), stop=(k == KD - 1))
                    last.then_inc(mod_tile, 1)

            @block.vector
            def _(dve):
                nc.vector.memset(keep["eps"][:], EPS).then_inc(eps_set, 1)
                dve.wait_ge(rinv_done, 1)
                for k in range(2):
                    nc.vector.tensor_tensor(xn[:, k, :], x_sb[:, k, :], rinv[:], ALU.mult).then_inc(xn_done, 1)
                dve.wait_ge(mod_tile, 3 * KD)
                nc.vector.tensor_tensor(mod[:], ps_mod[:, 0:3 * KD], ada_b[:], ALU.add).then_inc(mod_done, 1)
                dve.wait_ge(mod_done, 1)
                nc.vector.tensor_scalar_add(gain[:], mod[:, KD:2 * KD], 1.0).then_inc(mod_done, 1)
                nc.vector.tensor_copy(keep["gate"][:], mod[:, 2 * KD:3 * KD]).then_inc(mod_done, 1)
                dve.wait_ge(mod_done, 3)
                nc.vector.tensor_tensor(gain[:], gain[:], g_col[:], ALU.mult).then_inc(mod_done, 1)
                for k in range(KD):
                    dve.wait_ge(h_done, k + 1)
                    nc.vector.tensor_copy(h_hi[:, k, :], h[:, k % 2, :]).then_inc(hi_done, 1)
                    if k + 2 < KD:
                        nc.vector.tensor_tensor(xn[:, k % 2, :], x_sb[:, k + 2, :], rinv[:],
                                                ALU.mult).then_inc(xn_done, 1)


JOBS = 6


def plan(projects, recurs):
    slices = [("slice", j, h, k) for j in range(JOBS) for h in range(2) for k in range(KD)] if projects else []
    steps = []
    if recurs:
        steps += [("decay", b) for b in range(4)]
        steps += [("edge",), ("queries",)]
        for b in range(4):
            steps += [("gram", b), ("vcols", b), ("kcols", b)]
        steps += [("bcast",)]

        def level(pair, l):
            out = []
            if l == 0:
                out += [("part", b, 0) for b in pair] + [("unit", b) for b in pair]
            else:
                out += [("right", b, l) for b in pair] + [("left", b, l) for b in pair]
            if l < LEVELS - 1:
                out += [("part", b, l + 1) for b in pair] + [("turn", b, l) for b in pair]
            return out

        def chunk(c):
            return [("read", c), ("solve", c), ("write", c)]

        for l in range(LEVELS):
            steps += level((0, 1), l)
        first = [s for l in range(LEVELS) for s in level((2, 3), l)]
        second = [s for c in range(4) for s in chunk(c)]
        n = len(first) // len(second)
        for i, s in enumerate(second):
            steps += first[i * n:(i + 1) * n] + [s]
        steps += first[len(second) * n:]
        steps += [s for c in range(4, NT) for s in chunk(c)]
    else:
        steps += [("bcast",)]
    on_pe = ("gram", "vcols", "kcols", "right", "left", "turn", "read", "solve", "write")
    total = sum(s[0] in on_pe for s in steps)
    out, sent, passed = [], 0, 0

    def send(upto):
        nonlocal sent
        while sent < min(upto, len(slices)):
            s = slices[sent]
            if s[2:] == (0, 0):
                out.append(("weights", s[1]))
            out.append(s)
            sent += 1
            if s[3] == KD - 1:
                out.append(("evac", s[1], s[2]))
                if s[2] == 1 and s[1] < 4:
                    out.append(("conv", s[1]))
                if s[2] == 1 and s[1] >= 4:
                    out.append(("zstore", s[1]))
                if s[1:3] == (4, 0):
                    out.append(("silu",))
                if s[1:3] == (4, 1):
                    out.extend([("norm", 0, 0), ("norm", 0, 1)])
                if s[1:3] == (5, 0):
                    out.extend([("norm", 1, 0), ("norm", 1, 1)])

    send(2)
    for s in steps:
        out.append(s)
        if s[0] in on_pe:
            passed += 1
            send(2 + passed * (len(slices) - 2) // total)
    send(len(slices))
    return out


def ordinals(steps):
    seen, out = {}, {}
    for s in steps:
        out[s] = seen.get(s[0], 0)
        seen[s[0]] = out[s] + 1
    return out, seen


def stage_deltanet(nc, ctx, io, keep):
    own = ExitStack()
    with own:
        def sb(name, shape, dt=F32):
            return own.enter_context(nc.sbuf_tensor(name, shape, dt))

        def ps(name):
            return own.enter_context(nc.psum_tensor(name, [P, HALF], F32))

        sem = nc.alloc_semaphore
        h_hi, h_lo, ident, ones = keep["h_hi"], keep["h_lo"], keep["ident"], keep["ones"]

        w_raw = sb("w_raw", [P, KD * P])
        w_hi = sb("w_hi", [P, 2, KD * P], F32R)
        w_lo = sb("w_lo", [P, 2, KD * P], F32R)
        pre = sb("pre", [P, TAPS - 1 + T])
        conv_w = sb("conv_w", [P, QK_HEADS, 4, TAPS])
        qv = sb("qv", [P, 3, T])
        kT = sb("kT", [P, 2, T])
        nsq = sb("nsq", [P, HALF])
        nrm = sb("nrm", [P, HALF])
        rows = sb("rows", [P, 2, 2, T])
        qd = sb("qd", [P, 2, T])
        gam = sb("gam", [P, NT, 2, P])
        at = sb("at", [P, NT, 2, P])
        vb = sb("vb", [P, NT, 2, P])
        kd = sb("kd", [P, NT, 2, P])
        U = sb("U", [P, NT, 2, P])
        Ti = sb("Ti", [P, 2, HALF])
        Pr = sb("Pr", [P, 2, HALF])
        X = sb("X", [P, 2, 2, HALF])
        S = sb("S", [P, 2, P])
        Dl = sb("Dl", [P, 2, P])
        vn = sb("vn", [P, 2, P])
        oT = sb("oT", [P, 2, 2, P])
        tri = sb("tri", [P, P])
        lev = sb("lev", [P, LEVELS, P])
        cols = sb("cols", [P, NT, 64])
        eg = sb("eg", [P, NT, V_HEADS])
        nbe = sb("nbe", [P, NT, V_HEADS])
        edl = sb("edl", [P, NT, 2])
        gl = sb("gl", [P, NT, 2])
        adt = sb("adt", [P, 2])
        qbias = sb("qbias", [P, 2])

        p_job = [ps("p_job0"), ps("p_job1")]
        p_right, p_left, p_turn, p_pre = ps("p_right"), ps("p_left"), ps("p_turn"), ps("p_pre")
        p_read, p_write = ps("p_read"), ps("p_write")

        grow = vb[:].rearrange("p a b c -> p (a b c)")[:, 0:T]
        gt0 = vb[:].rearrange("p a b c -> p (a b c)")[:, T:2 * T]
        gt1 = kd[:].rearrange("p a b c -> p (a b c)")[:, 0:T]

        N_IT = QK_HEADS + 1
        plans = [plan(True, False)] + [plan(True, True)] * (QK_HEADS - 1) + [plan(False, True)]
        order = [ordinals(p) for p in plans]

        cst = sem("b_cst")
        w_in = sem("b_w_in"); w_hi_done = sem("b_w_hi"); w_lo_done = sem("b_w_lo")
        half_done = sem("b_half"); evac_done = sem("b_evac"); conv_step = sem("b_conv")
        pad_set = sem("b_pad"); silu_done = sem("b_silu")
        nsq_done = sem("b_nsq"); nss_done = sem("b_nss"); nln = sem("b_nln"); nexp = sem("b_nexp"); nmul = sem("b_nmul")
        z_stored = sem("b_zst")
        g_act = sem("b_gact"); g_dve = sem("b_gdve"); g_pe = sem("b_gpe"); g_out = sem("b_gout")
        rows_in = sem("b_rows")
        diff_done = sem("b_diff"); mask_done = sem("b_mask"); decay_done = sem("b_decay"); dbeta_done = sem("b_dbeta")
        edge_dve = sem("b_edged"); edge_act = sem("b_edgea"); qexp = sem("b_qexp"); qd_done = sem("b_qd")
        gram_ready = sem("b_gram"); gram_used = sem("b_gramu")
        v_ready = sem("b_vr"); vb_done = sem("b_vb"); k_ready = sem("b_kr"); kd_done = sem("b_kd")
        part_done = sem("b_part"); right_ready = sem("b_right"); right_cp = sem("b_rightc")
        left_ready = sem("b_left"); u_done = sem("b_u"); turn_ready = sem("b_turn"); turn_cp = sem("b_turnc")
        read_ready = sem("b_read"); d_done = sem("b_d"); solve_ready = sem("b_solve"); vn_done = sem("b_vn")
        write_ready = sem("b_write"); s_done = sem("b_s"); o_done = sem("b_o")
        o_stored = [sem("b_os0"), sem("b_os1")]

        N_PART, N_LVL = 4 * LEVELS, 4 * (LEVELS - 1)

        def job(i, j):
            return 1 + JOBS * i + j

        def conv_dst(i, j):
            return (qv[:, 0, :], kT[:, i % 2, :], qv[:, 1, :], qv[:, 2, :])[j]

        def unit(t, b):
            return t[:, 2 * b:2 * b + 2, :, :].rearrange("p a b c -> p (a b c)")

        def u_ord(b, l):
            return b // 2 * 2 * LEVELS + 2 * l + b % 2

        with nc.Block() as block:
            @block.sync
            def _(sp):
                for dst, src in ((tri[:], io["tri"]), (lev[:], io["lev"]), (conv_w[:], io["conv_w"]),
                                 (adt[32:48, :], io["adt"])):
                    sp.dma_start(dst, src).then_inc(cst, 16)

                def load(J):
                    if J >= 1:
                        sp.wait_ge(w_lo_done, J)
                    sp.dma_start(w_raw[:], io["w1"][J]).then_inc(w_in, 16)

                load(0)
                for i in range(N_IT):
                    o, n = order[i]
                    for s in plans[i]:
                        if s[0] == "weights":
                            load(job(i, s[1]))
                        elif s[0] == "bcast" and i < QK_HEADS:
                            if i == 0:
                                sp.wait_ge(g_dve, 13)
                                sp.dma_start(io["grows"][0:V_HEADS, :], grow[0:V_HEADS, :]).then_inc(g_out, 16)
                                sp.dma_start(io["grows"][V_HEADS:2 * V_HEADS, :], grow[32:48, :]).then_inc(g_out, 16)
                                sp.wait_ge(g_out, 32)
                            else:
                                sp.wait_ge(dbeta_done, 4 * i)
                                sp.wait_ge(qexp, i)
                                sp.wait_ge(edge_dve, i)
                                sp.wait_ge(edge_act, 2 * i)
                            for kind in range(2):
                                for a in range(2):
                                    r = kind * V_HEADS + 2 * i + a
                                    sp.dma_start(rows[:, kind, a, :], io["grows"][r:r + 1, :].broadcast_to([P, T])
                                                 ).then_inc(rows_in, 16)
                        elif s[0] == "zstore":
                            J = job(i, s[1])
                            sp.wait_ge(evac_done, 2 * J + 2)
                            sp.dma_start(io["z_scr"][2 * i + s[1] - 4], pre[:, TAPS - 1:]).then_inc(z_stored, 16)
                        elif s[0] == "write":
                            g, c = i - 1, s[1]
                            sp.wait_ge(o_done, NT * g + c + 1)
                            sp.dma_start(io["o_scr"][2 * g:2 * g + 2, :, c * P:(c + 1) * P].rearrange("a p t -> p a t"),
                                         oT[:, c % 2]).then_inc(o_stored[c % 2], 16)
                sp.wait_ge(z_stored, 16 * V_HEADS)
                for q in range(2):
                    sp.wait_ge(o_stored[q], 16 * QK_HEADS * NT // 2)

            @block.gpsimd
            def _(pool):
                def split_lo(J):
                    pool.wait_ge(w_hi_done, J + 1)
                    nc.gpsimd.tensor_tensor(w_lo[:, J % 2, :], w_raw[:], w_hi[:, J % 2, :].bitcast(F32),
                                            ALU.subtract).then_inc(w_lo_done, 1)

                pool.wait_ge(cst, 64)
                split_lo(0)
                for i in range(N_IT):
                    g = i - 1
                    o, n = order[i]
                    for s in plans[i]:
                        if s[0] == "weights":
                            split_lo(job(i, s[1]))
                        elif s[0] == "decay":
                            b = s[1]
                            pool.wait_ge(diff_done, 4 * g + b + 1)
                            x = gam[:, 2 * b:2 * b + 2].rearrange("p a b c -> p (a b) c")
                            nc.gpsimd.tensor_tensor(x, x, bc(tri[:], 1, 4), ALU.add).then_inc(mask_done, 1)
                            pool.wait_ge(decay_done, 4 * g + b + 1)
                            if g >= 1:
                                pool.wait_ge(part_done, N_PART * g)
                            else:
                                pool.wait_ge(rows_in, 64)
                            for a in range(2):
                                last = nc.gpsimd.tensor_tensor(
                                    at[:, 2 * b:2 * b + 2, a, :], gam[:, 2 * b:2 * b + 2, a, :],
                                    rows[:, 0, a, 2 * b * P:(2 * b + 2) * P].rearrange("p (c t) -> p c t", c=2),
                                    ALU.mult)
                                if a == 1:
                                    last.then_inc(dbeta_done, 1)
                        elif s[0] == "queries":
                            pool.wait_ge(qexp, g + 1)
                            pool.wait_ge(nmul, 4 * (g + 1))
                            nc.gpsimd.tensor_tensor(qd[:], qd[:], bc(qv[:, 0, :], 1, 2), ALU.mult).then_inc(qd_done, 1)
                        elif s[0] == "part":
                            b, l = s[1:]
                            pool.wait_ge(gram_used, 2 * (4 * g + b) + 2)
                            if l > 2:
                                pool.wait_ge(right_ready, N_LVL * g + o[("right", b, l - 2)] + 1)
                            elif l == 2:
                                pool.wait_ge(u_done, N_PART * g + u_ord(b, 0) + 1)
                            elif l == 0 and b >= 2:
                                pool.wait_ge(right_ready, N_LVL * g + o[("right", b - 2, LEVELS - 1)] + 1)
                            elif l == 0 and g >= 1:
                                pool.wait_ge(right_ready, N_LVL * g)
                            nc.gpsimd.tensor_tensor(
                                X[:, b % 2, l % 2, :].rearrange("p (u t) -> p u t", u=4),
                                unit(at, b).rearrange("p (u t) -> p u t", u=4), bc(lev[:, l, :], 1, 4),
                                ALU.mult).then_inc(part_done, 1)

            @block.scalar
            def _(act):
                def evac(J, h, func=ACT.Copy):
                    act.wait_ge(half_done, 2 * J + h + 1)
                    nc.scalar.activation(pre[:, TAPS - 1 + h * HALF:TAPS - 1 + (h + 1) * HALF], p_job[h][:],
                                         func).then_inc(evac_done, 1)

                act.wait_ge(cst, 64)
                nc.scalar.activation(adt[32:48, 0:1], adt[32:48, 0:1], ACT.Exp).then_inc(g_act, 1)
                act.wait_ge(pad_set, 4)
                evac(0, 0)
                evac(0, 1)
                act.wait_ge(evac_done, 2)
                nc.scalar.activation(gt0[0:16, :], pre[0:16, TAPS - 1:], ACT.Exp, scale=-1.0).then_inc(g_act, 1)
                nc.scalar.activation(gt0[32:48, :], pre[32:48, TAPS - 1:], ACT.Identity,
                                     bias=adt[32:48, 1:2]).then_inc(g_act, 1)
                act.wait_ge(g_dve, 3)
                nc.scalar.activation(gt1[32:48, :], gt1[32:48, :], ACT.Exp).then_inc(g_act, 1)
                act.wait_ge(g_act, 4)
                nc.scalar.activation(gt1[32:48, :], gt1[32:48, :], ACT.Ln, bias=1.0).then_inc(g_act, 1)
                act.wait_ge(g_pe, 1)
                nc.scalar.activation(cols[:].rearrange("p a b -> p (a b)"), p_turn[:], ACT.Copy).then_inc(g_act, 1)
                act.wait_ge(g_act, 6)
                nc.scalar.activation(eg[:], cols[:, :, 32:48], ACT.Exp).then_inc(g_act, 1)

                for i in range(N_IT):
                    g = i - 1
                    o, n = order[i]
                    for s in plans[i]:
                        if s[0] == "evac":
                            j, h = s[1:]
                            J = job(i, j)
                            if h == 0:
                                if j == 0:
                                    act.wait_ge(z_stored, 16 * 2 * i) if i else act.wait_ge(g_act, 3)
                                elif j <= 4:
                                    act.wait_ge(conv_step, 16 * i + 4 * j)
                                else:
                                    act.wait_ge(z_stored, 16 * (2 * i + 1))
                            evac(J, h, ACT.Silu if j >= 4 else ACT.Copy)
                        elif s[0] == "silu":
                            act.wait_ge(conv_step, 16 * (i + 1))
                            nc.scalar.activation(qv[:], qv[:], ACT.Silu).then_inc(silu_done, 1)
                            nc.scalar.activation(kT[:, i % 2, :], kT[:, i % 2, :], ACT.Silu).then_inc(silu_done, 1)
                        elif s[0] == "norm":
                            w, h = s[1:]
                            m = 4 * i + 2 * w + h
                            src = (qv[:, 0, :] if w == 0 else kT[:, i % 2, :])[:, h * HALF:(h + 1) * HALF]
                            act.wait_ge(silu_done, 2 * i + 2)
                            if m >= 1:
                                act.wait_ge(nss_done, m)
                            nc.scalar.activation(nsq[:], src, ACT.Square).then_inc(nsq_done, 1)
                            act.wait_ge(nss_done, m + 1)
                            if m >= 1:
                                act.wait_ge(nmul, m)
                            nc.scalar.activation(nrm[:], p_pre[:], ACT.Ln, bias=keep["eps"][:, 0:1]).then_inc(nln, 1)
                            act.wait_ge(nln, m + 1)
                            nc.scalar.activation(nrm[:], nrm[:], ACT.Exp, scale=-0.5,
                                                 bias=qbias[:, w:w + 1]).then_inc(nexp, 1)
                        elif s[0] == "decay":
                            b = s[1]
                            act.wait_ge(mask_done, 4 * g + b + 1)
                            nc.scalar.activation(unit(gam, b), unit(gam, b), ACT.Exp).then_inc(decay_done, 1)
                        elif s[0] == "edge":
                            act.wait_ge(edge_dve, g + 1)
                            nc.scalar.activation(edl[:], edl[:], ACT.Exp).then_inc(edge_act, 1)
                            if g >= 1:
                                act.wait_ge(s_done, 17 * g)
                            nc.scalar.activation(gl[:], rows[:, 1, :, P - 1::P].rearrange("p a c -> p c a"),
                                                 ACT.Exp).then_inc(edge_act, 1)
                        elif s[0] == "queries":
                            if g >= 1:
                                act.wait_ge(write_ready, NT * g)
                            act.wait_ge(rows_in, 64 * (g + 1))
                            nc.scalar.activation(qd[:], rows[:, 1, :, :], ACT.Exp).then_inc(qexp, 1)
                        elif s[0] == "right":
                            m = N_LVL * g + o[s]
                            b = s[1]
                            act.wait_ge(right_ready, m + 1)
                            if m >= 2:
                                act.wait_ge(left_ready, m - 1)
                            nc.scalar.activation(Pr[:, b % 2, :], p_right[:], ACT.Copy).then_inc(right_cp, 1)
                        elif s[0] == "turn":
                            m = N_LVL * g + o[s]
                            b = s[1]
                            act.wait_ge(turn_ready, m + 1)
                            if m >= 2:
                                act.wait_ge(right_ready, m - 1)
                            nc.scalar.activation(Ti[:, b % 2, :], p_turn[:], ACT.Copy).then_inc(turn_cp, 1)
                        elif s[0] == "solve":
                            m = NT * g + s[1]
                            act.wait_ge(solve_ready, m + 1)
                            if m >= 1:
                                act.wait_ge(write_ready, m)
                            nc.scalar.activation(vn[:].rearrange("p a c -> p (a c)"), p_read[:, 256:512],
                                                 ACT.Copy).then_inc(vn_done, 1)
                        elif s[0] == "write":
                            c = s[1]
                            m = NT * g + c
                            act.wait_ge(write_ready, m + 1)
                            if m >= 2:
                                act.wait_ge(o_stored[c % 2], 16 * (m // 2))
                            nc.scalar.activation(oT[:, c % 2].rearrange("p a c -> p (a c)"), p_read[:, 0:256],
                                                 ACT.Copy).then_inc(o_done, 1)

            @block.tensor
            def _(pe):
                def piece(J, h, k):
                    if h == 0 and k == 0:
                        pe.wait_ge(w_lo_done, J + 1)
                    if k == 0 and J >= 1:
                        pe.wait_ge(evac_done, 2 * (J - 1) + h + 1)
                    cut = slice(h * HALF, (h + 1) * HALF)
                    hi, lo = w_hi[:, J % 2, k * P:(k + 1) * P], w_lo[:, J % 2, k * P:(k + 1) * P]
                    nc.tensor.matmul(p_job[h][:], hi, h_hi[:, k, cut], start=(k == 0), stop=False)
                    nc.tensor.matmul(p_job[h][:], hi, h_lo[:, k, cut], start=False, stop=False)
                    last = nc.tensor.matmul(p_job[h][:], lo, h_hi[:, k, cut], start=False, stop=(k == KD - 1))
                    if k == KD - 1:
                        last.then_inc(half_done, 1)

                for h in range(2):
                    for k in range(KD):
                        piece(0, h, k)
                pe.wait_ge(g_dve, 13)
                for t in range(NT):
                    last = nc.tensor.transpose(p_turn[:, 64 * t:64 * (t + 1)], grow[0:64, t * P:(t + 1) * P],
                                               ident[0:64, 0:64])
                last.then_inc(g_pe, 1)

                for i in range(N_IT):
                    g = i - 1
                    o, n = order[i]
                    for s in plans[i]:
                        if s[0] == "slice":
                            piece(job(i, s[1]), s[2], s[3])
                        elif s[0] == "norm":
                            m = 4 * i + 2 * s[1] + s[2]
                            pe.wait_ge(nsq_done, m + 1)
                            if m >= 1:
                                pe.wait_ge(nln, m)
                            if g >= 0:
                                pe.wait_ge(kd_done, 4 * (g + 1))
                            nc.tensor.matmul(p_pre[:], ones[:], nsq[:], start=True, stop=True).then_inc(nss_done, 1)
                        elif s[0] == "gram":
                            b = s[1]
                            pe.wait_ge(nmul, 4 * (g + 1))
                            if b >= 1:
                                pe.wait_ge(kd_done, 4 * g + b)
                            for t in range(2):
                                c = slice((2 * b + t) * P, (2 * b + t + 1) * P)
                                nc.tensor.matmul(p_pre[:, 256 * t:256 * t + P], kT[:, g % 2, c], kT[:, g % 2, c],
                                                 start=True, stop=True)
                                last = nc.tensor.matmul(p_pre[:, 256 * t + P:256 * t + 2 * P], kT[:, g % 2, c],
                                                        qv[:, 0, c], start=True, stop=True)
                            last.then_inc(gram_ready, 1)
                        elif s[0] == "vcols":
                            b = s[1]
                            if b >= 1:
                                pe.wait_ge(vb_done, 4 * g + b)
                            elif g >= 1:
                                pe.wait_ge(turn_cp, N_LVL * g)
                            else:
                                pe.wait_ge(g_act, 6)
                            for t in range(2):
                                for a in range(2):
                                    last = nc.tensor.transpose(
                                        p_turn[:, (2 * t + a) * P:(2 * t + a + 1) * P],
                                        qv[:, 1 + a, (2 * b + t) * P:(2 * b + t + 1) * P], ident[:])
                            last.then_inc(v_ready, 1)
                        elif s[0] == "kcols":
                            b = s[1]
                            pe.wait_ge(gram_used, 2 * (4 * g + b) + 2)
                            for t in range(2):
                                last = nc.tensor.transpose(p_pre[:, t * P:(t + 1) * P],
                                                           kT[:, g % 2, (2 * b + t) * P:(2 * b + t + 1) * P], ident[:])
                            last.then_inc(k_ready, 1)
                        elif s[0] == "right":
                            b, l = s[1:]
                            m = N_LVL * g + o[s]
                            pe.wait_ge(part_done, N_PART * g + o[("part", b, l)] + 1)
                            pe.wait_ge(turn_cp, N_LVL * g + o[("turn", b, l - 1)] + 1)
                            if m >= 1:
                                pe.wait_ge(right_cp, m)
                            for u in range(4):
                                c = slice(u * P, (u + 1) * P)
                                last = nc.tensor.matmul(p_right[:, c], X[:, b % 2, l % 2, c], Ti[:, b % 2, c],
                                                        start=True, stop=True)
                            last.then_inc(right_ready, 1)
                        elif s[0] == "left":
                            b, l = s[1:]
                            m = N_LVL * g + o[s]
                            pe.wait_ge(right_cp, N_LVL * g + o[("right", b, l)] + 1)
                            pe.wait_ge(u_done, N_PART * g + u_ord(b, l))
                            for u in range(4):
                                c = slice(u * P, (u + 1) * P)
                                last = nc.tensor.matmul(p_left[:, c], Pr[:, b % 2, c], unit(U, b)[:, c],
                                                        start=True, stop=True)
                            last.then_inc(left_ready, 1)
                        elif s[0] == "turn":
                            b, l = s[1:]
                            m = N_LVL * g + o[s]
                            pe.wait_ge(u_done, N_PART * g + u_ord(b, l) + 1)
                            if o[s] >= 1:
                                pe.wait_ge(turn_cp, m)
                            else:
                                pe.wait_ge(vb_done, 4 * (g + 1))
                            for u in range(4):
                                c = slice(u * P, (u + 1) * P)
                                last = nc.tensor.transpose(p_turn[:, c], unit(U, b)[:, c], ident[:])
                            last.then_inc(turn_ready, 1)
                        elif s[0] == "read":
                            c = s[1]
                            m = NT * g + c
                            pe.wait_ge(s_done, 17 * g + 1 + 2 * c)
                            if m >= 1:
                                pe.wait_ge(o_done, m)
                            nc.tensor.matmul(p_read[:, 0:256], kT[:, g % 2, c * P:(c + 1) * P],
                                             S[:].rearrange("p a c -> p (a c)"), start=True, stop=True
                                             ).then_inc(read_ready, 1)
                        elif s[0] == "solve":
                            c = s[1]
                            m = NT * g + c
                            pe.wait_ge(d_done, 2 * m + 2)
                            pe.wait_ge(u_done, N_PART * g + u_ord(c // 2, LEVELS - 1) + 1)
                            for a in range(2):
                                last = nc.tensor.matmul(p_read[:, 256 + a * P:256 + (a + 1) * P], U[:, c, a, :],
                                                        Dl[:, a, :], start=True, stop=True)
                            last.then_inc(solve_ready, 1)
                        elif s[0] == "write":
                            c = s[1]
                            m = NT * g + c
                            pe.wait_ge(vn_done, m + 1)
                            pe.wait_ge(qd_done, g + 1)
                            pe.wait_ge(kd_done, 4 * (g + 1))
                            if m >= 1:
                                pe.wait_ge(s_done, 17 * g + 1 + 2 * c)
                            for a in range(2):
                                nc.tensor.matmul(p_write[:, a * P:(a + 1) * P], kd[:, c, a, :], vn[:, a, :],
                                                 start=True, stop=True)
                            for a in range(2):
                                nc.tensor.matmul(p_read[:, a * P:(a + 1) * P], S[:, a, :],
                                                 qd[:, a, c * P:(c + 1) * P], start=True, stop=False)
                                last = nc.tensor.matmul(p_read[:, a * P:(a + 1) * P], vn[:, a, :], gam[:, c, a, :],
                                                        start=False, stop=True)
                            last.then_inc(write_ready, 1)

            @block.vector
            def _(dve):
                def split_hi(J):
                    dve.wait_ge(w_in, 16 * (J + 1))
                    if J >= 2:
                        dve.wait_ge(half_done, 2 * (J - 1))
                    nc.vector.tensor_copy(w_hi[:, J % 2, :], w_raw[:]).then_inc(w_hi_done, 1)

                nc.vector.memset(pre[:, 0:TAPS - 1], 0.0).then_inc(pad_set, 1)
                nc.vector.memset(qbias[:, 0:1], float(np.log(DH ** -0.5))).then_inc(pad_set, 1)
                nc.vector.memset(qbias[:, 1:2], 0.0).then_inc(pad_set, 1)
                nc.vector.memset(grow, 0.0).then_inc(pad_set, 1)
                dve.wait_ge(cst, 64)
                split_hi(0)

                dve.wait_ge(g_act, 2)
                nc.vector.tensor_scalar_add(gt0[0:16, :], gt0[0:16, :], 1.0).then_inc(g_dve, 1)
                dve.wait_ge(g_dve, 1)
                dve.wait_ge(pad_set, 4)
                nc.vector.reciprocal(grow[0:16, :], gt0[0:16, :]).then_inc(g_dve, 1)
                dve.wait_ge(g_act, 3)
                nc.vector.scalar_tensor_tensor(gt1[32:48, :], gt0[32:48, :], -1.0, gt0[32:48, :],
                                               ALU.mult, ALU.min).then_inc(g_dve, 1)
                dve.wait_ge(g_act, 5)
                nc.vector.scalar_tensor_tensor(gt0[32:48, :], gt0[32:48, :], 0.0, gt1[32:48, :],
                                               ALU.max, ALU.add).then_inc(g_dve, 1)
                dve.wait_ge(g_dve, 4)
                nc.vector.tensor_scalar(gt0[32:48, :], gt0[32:48, :], adt[32:48, 0:1], -1.0,
                                        ALU.mult, ALU.mult).then_inc(g_dve, 1)
                dve.wait_ge(g_dve, 5)
                for t in range(NT):
                    c = slice(t * P, (t + 1) * P)
                    nc.vector.tensor_tensor_scan(grow[32:48, c], ones[32:48, :], gt0[32:48, c], 0.0,
                                                 ALU.mult, ALU.add).then_inc(g_dve, 1)
                dve.wait_ge(g_act, 7)
                nc.vector.scalar_tensor_tensor(nbe[:], cols[:, :, 0:16], -1.0, eg[:],
                                               ALU.mult, ALU.mult).then_inc(g_dve, 1)

                for i in range(N_IT):
                    g = i - 1
                    o, n = order[i]
                    for s in plans[i]:
                        if s[0] == "weights":
                            split_hi(job(i, s[1]))
                        elif s[0] == "conv":
                            j = s[1]
                            base = 16 * i + 4 * j
                            dst = conv_dst(i, j)
                            dve.wait_ge(evac_done, 2 * job(i, j) + 2)
                            if g >= 0:
                                dve.wait_ge(gram_ready, 4 * (g + 1))
                                dve.wait_ge(qd_done, g + 1)
                                dve.wait_ge(v_ready, 4 * (g + 1))
                            if i >= 2 and j == 1:
                                dve.wait_ge(read_ready, NT * (i - 1))
                            nc.vector.tensor_scalar(dst, pre[:, 0:T], conv_w[:, i, j, 0:1], None,
                                                    ALU.mult).then_inc(conv_step, 1)
                            for q in range(1, TAPS):
                                dve.wait_ge(conv_step, base + q)
                                nc.vector.scalar_tensor_tensor(dst, pre[:, q:q + T], conv_w[:, i, j, q:q + 1], dst,
                                                               ALU.mult, ALU.add).then_inc(conv_step, 1)
                        elif s[0] == "norm":
                            w, h = s[1:]
                            m = 4 * i + 2 * w + h
                            src = (qv[:, 0, :] if w == 0 else kT[:, i % 2, :])[:, h * HALF:(h + 1) * HALF]
                            dve.wait_ge(nexp, m + 1)
                            nc.vector.tensor_tensor(src, src, nrm[:], ALU.mult).then_inc(nmul, 1)
                        elif s[0] == "decay":
                            b = s[1]
                            dve.wait_ge(rows_in, 64 * (g + 1))
                            if g >= 1:
                                dve.wait_ge(write_ready, NT * g)
                            else:
                                dve.wait_ge(g_act, 6)
                            for a in range(2):
                                last = nc.vector.tensor_tensor(
                                    gam[:, 2 * b:2 * b + 2, a, :],
                                    rows[:, 1, a, 2 * b * P:(2 * b + 2) * P].rearrange("p (c t) -> p c t", c=2),
                                    bc(cols[:, 2 * b:2 * b + 2, 32 + 2 * g + a], 2, P), ALU.subtract)
                            last.then_inc(diff_done, 1)
                        elif s[0] == "edge":
                            if g >= 1:
                                dve.wait_ge(kd_done, 4 * g)
                                dve.wait_ge(s_done, 17 * g)
                                dve.wait_ge(write_ready, NT * g)
                            nc.vector.tensor_tensor(
                                edl[:], rows[:, 1, :, P - 1::P].rearrange("p a c -> p c a"),
                                cols[:, :, 32 + 2 * g:34 + 2 * g], ALU.subtract).then_inc(edge_dve, 1)
                            nc.vector.memset(S[:], 0.0).then_inc(s_done, 1)
                        elif s[0] == "gram":
                            b = s[1]
                            dve.wait_ge(gram_ready, 4 * g + b + 1)
                            dve.wait_ge(dbeta_done, 4 * g + b + 1)
                            pk = p_pre[:].rearrange("p (t k c) -> p t k c", t=2, k=2)
                            nc.vector.tensor_tensor(at[:, 2 * b:2 * b + 2], bc(pk[:, :, 0, :], 2, 2),
                                                    at[:, 2 * b:2 * b + 2], ALU.mult).then_inc(gram_used, 1)
                            nc.vector.tensor_tensor(gam[:, 2 * b:2 * b + 2], bc(pk[:, :, 1, :], 2, 2),
                                                    gam[:, 2 * b:2 * b + 2], ALU.mult).then_inc(gram_used, 1)
                        elif s[0] == "vcols":
                            b = s[1]
                            dve.wait_ge(v_ready, 4 * g + b + 1)
                            if g == 0:
                                dve.wait_ge(g_out, 32)
                            nc.vector.tensor_tensor(
                                vb[:, 2 * b:2 * b + 2], p_turn[:].rearrange("p (t a c) -> p t a c", t=2, a=2),
                                bc(cols[:, 2 * b:2 * b + 2, 2 * g:2 * g + 2], 3, P), ALU.mult).then_inc(vb_done, 1)
                        elif s[0] == "kcols":
                            b = s[1]
                            dve.wait_ge(k_ready, 4 * g + b + 1)
                            dve.wait_ge(edge_act, 2 * g + 1)
                            nc.vector.tensor_tensor(
                                kd[:, 2 * b:2 * b + 2],
                                bc(p_pre[:, 0:256].rearrange("p (t c) -> p t c", t=2), 2, 2),
                                bc(edl[:, 2 * b:2 * b + 2, :], 3, P), ALU.mult).then_inc(kd_done, 1)
                        elif s[0] == "unit":
                            b = s[1]
                            dve.wait_ge(part_done, N_PART * g + o[("part", b, 0)] + 1)
                            if g >= 1:
                                dve.wait_ge(solve_ready, NT * g)
                            nc.vector.tensor_tensor(unit(U, b).rearrange("p (u t) -> p u t", u=4), bc(ident[:], 1, 4),
                                                    X[:, b % 2, 0, :].rearrange("p (u t) -> p u t", u=4),
                                                    ALU.subtract).then_inc(u_done, 1)
                        elif s[0] == "left":
                            b, l = s[1:]
                            dve.wait_ge(left_ready, N_LVL * g + o[s] + 1)
                            nc.vector.tensor_tensor(unit(U, b), unit(U, b), p_left[:], ALU.subtract).then_inc(u_done, 1)
                        elif s[0] == "read":
                            c = s[1]
                            m = NT * g + c
                            dve.wait_ge(read_ready, m + 1)
                            dve.wait_ge(vb_done, 4 * (g + 1))
                            dve.wait_ge(g_dve, 14)
                            if m >= 1:
                                dve.wait_ge(solve_ready, m)
                            for a in range(2):
                                hd = 2 * g + a
                                nc.vector.scalar_tensor_tensor(Dl[:, a, :], p_read[:, a * P:(a + 1) * P],
                                                               nbe[:, c, hd:hd + 1], vb[:, c, a, :],
                                                               ALU.mult, ALU.add).then_inc(d_done, 1)
                        elif s[0] == "write":
                            c = s[1]
                            m = NT * g + c
                            dve.wait_ge(write_ready, m + 1)
                            dve.wait_ge(edge_act, 2 * g + 2)
                            dve.wait_ge(s_done, 17 * g + 1 + 2 * c)
                            for a in range(2):
                                nc.vector.scalar_tensor_tensor(S[:, a, :], S[:, a, :], gl[:, c, a:a + 1],
                                                               p_write[:, a * P:(a + 1) * P],
                                                               ALU.mult, ALU.add).then_inc(s_done, 1)


CH_PASS = (3, 3, 2)


def stage_out(nc, ctx, io, keep):
    own = ExitStack()
    with own:
        def sb(name, shape, dt=F32):
            return own.enter_context(nc.sbuf_tensor(name, shape, dt))

        sem = lambda name: ctx.enter_context(nc.semaphore(name))
        h_hi, h_lo, ones, eps = keep["h_hi"], keep["h_lo"], keep["ones"], keep["eps"]
        y2_hi = sb("y2_hi", [P, V_HEADS - KD, T], F32R)
        y2_lo = sb("y2_lo", [P, V_HEADS - KD, T], F32R)
        x1 = sb("x1", [P, KD, T])
        W3 = 3 * P
        w_raw = sb("wo_raw", [P, 2, W3])
        w_hi = sb("wo_hi", [P, 2, W3], F32R)
        w_lo = sb("wo_lo", [P, 2, W3], F32R)
        ob = sb("ob", [P, 2, T])
        zb = sb("zb", [P, 2, T])
        sq = sb("sq3", [P, T])
        rinv = sb("rinv3", [P, T])
        nw = sb("nw", [P, 1])
        fg = sb("fg", [P, KD])
        np_col = sb("np_col", [P, KD])
        p_out = [own.enter_context(nc.psum_tensor(f"p_out{i}", [P, HALF], F32)) for i in range(6)]
        p_ss = [own.enter_context(nc.psum_tensor(f"p_ss{i}", [P, HALF], F32)) for i in range(2)]

        def y(part, n):
            low, high = ((h_hi, y2_hi), (h_lo, y2_lo))[part]
            return low[:, n, :] if n < KD else high[:, n - KD, :]

        cst = sem("c_cst"); x_in = sem("c_x"); oz_in = [sem("c_oz0"), sem("c_oz1")]
        sq_done = sem("c_sq"); ss_done = sem("c_ss"); ln_done = sem("c_ln"); rinv_done = sem("c_rinv")
        gz_done = sem("c_gz"); y_done = sem("c_y"); yhi_done = sem("c_yhi"); ylo_done = sem("c_ylo")
        w_in = [sem("c_w0"), sem("c_w1")]; whi_done = sem("c_whi"); wlo_done = sem("c_wlo"); w_used = sem("c_wu")
        pass_done = sem("c_pass"); bank_used = sem("c_bank")
        sq2 = sem("c_sq2"); ss2 = sem("c_ss2"); ln2 = sem("c_ln2"); ri2 = sem("c_ri2"); xn2 = sem("c_xn2")
        hh = sem("c_hh"); hhi = sem("c_hhi"); hlo = sem("c_hlo"); x1_out = sem("c_x1o")
        steps = [(q, n) for q in range(len(CH_PASS)) for n in range(V_HEADS)]
        first_ch = [sum(CH_PASS[:q]) for q in range(len(CH_PASS))]

        with nc.Block() as block:
            @block.sync
            def _(sp):
                for dst, src in ((nw, io["norm_w"]), (fg, io["final_g"]), (np_col, io["norm_pre"])):
                    sp.dma_start(dst[:], src).then_inc(cst, 16)

                def load_w(m):
                    q, n = steps[m]
                    c0, cn = first_ch[q] * P, CH_PASS[q] * P
                    if m >= 2:
                        sp.wait_ge(wlo_done, m - 1)
                    sp.dma_start(w_raw[:, m % 2, 0:cn], io["w_out"][n * P:(n + 1) * P, c0:c0 + cn]
                                 ).then_inc(w_in[m % 2], 16)

                for m in range(len(steps)):
                    if m < V_HEADS:
                        if m >= 2:
                            sp.wait_ge(ylo_done, m - 1)
                        sp.dma_start(ob[:, m % 2, :], io["o_scr"][m]).then_inc(oz_in[m % 2], 16)
                        sp.dma_start(zb[:, m % 2, :], io["z_scr"][m]).then_inc(oz_in[m % 2], 16)
                    if m == 2:
                        sp.dma_start(x1[:], io["xT"]).then_inc(x_in, 16)
                    load_w(m)
                for k in range(KD):
                    sp.wait_ge(xn2, k + 1)
                    sp.dma_start(io["x1_scr"][k], x1[:, k, :]).then_inc(x1_out, 16)
                sp.wait_ge(x1_out, 16 * KD)
                sp.wait_ge(hlo, KD)

            @block.gpsimd
            def _(pool):
                for m, (q, n) in enumerate(steps):
                    cn = CH_PASS[q] * P
                    if q == 0:
                        pool.wait_ge(yhi_done, n + 1)
                        nc.gpsimd.tensor_tensor(y(1, n), zb[:, n % 2, :], y(0, n).bitcast(F32),
                                                ALU.subtract).then_inc(ylo_done, 1)
                    pool.wait_ge(whi_done, m + 1)
                    nc.gpsimd.tensor_tensor(w_lo[:, m % 2, 0:cn], w_raw[:, m % 2, 0:cn],
                                            w_hi[:, m % 2, 0:cn].bitcast(F32), ALU.subtract).then_inc(wlo_done, 1)
                for k in range(KD):
                    pool.wait_ge(hhi, k + 1)
                    nc.gpsimd.tensor_tensor(h_lo[:, k, :], zb[:, k % 2, :], h_hi[:, k, :].bitcast(F32),
                                            ALU.subtract).then_inc(hlo, 1)

            @block.scalar
            def _(act):
                def norm_row(base, scale, ln_sem, out_sem, n):
                    for i in range(2):
                        nc.scalar.activation(rinv[:, i * HALF:(i + 1) * HALF], p_ss[i][:], ACT.Ln, scale=scale,
                                             bias=eps[:, 0:1]).then_inc(ln_sem, 1)
                    act.wait_ge(ln_sem, 2 * n + 2)
                    nc.scalar.activation(rinv[:], rinv[:], ACT.Exp, scale=-0.5).then_inc(out_sem, 1)

                for n in range(V_HEADS):
                    act.wait_ge(oz_in[n % 2], 32 * (n // 2 + 1))
                    if n >= 1:
                        act.wait_ge(ss_done, n)
                    nc.scalar.activation(sq[:], ob[:, n % 2, :], ACT.Square).then_inc(sq_done, 1)
                    act.wait_ge(ss_done, n + 1)
                    if n >= 1:
                        act.wait_ge(y_done, n)
                    norm_row(n, 1.0 / DH, ln_done, rinv_done, n)
                for r in range(2):
                    for k in range(KD):
                        if r == 0:
                            act.wait_ge(bank_used, 2 * (k + 1))
                            if k == 0:
                                act.wait_ge(ss_done, V_HEADS)
                        else:
                            act.wait_ge(xn2, k + 1)
                        if r or k:
                            act.wait_ge(ss2, KD * r + k)
                        nc.scalar.activation(sq[:], x1[:, k, :], ACT.Square).then_inc(sq2, 1)
                    act.wait_ge(ss2, KD * (r + 1))
                    if r == 0:
                        act.wait_ge(y_done, V_HEADS)
                    else:
                        act.wait_ge(xn2, KD)
                    norm_row(r, 1.0 / D, ln2, ri2, r)

            @block.tensor
            def _(pe):
                def sums(n):
                    pe.wait_ge(sq_done, n + 1)
                    if n >= 1:
                        pe.wait_ge(ln_done, 2 * n)
                    for i in range(2):
                        last = nc.tensor.matmul(p_ss[i][:], ones[:], sq[:, i * HALF:(i + 1) * HALF],
                                                start=True, stop=True)
                    last.then_inc(ss_done, 1)

                sums(0)
                for m, (q, n) in enumerate(steps):
                    if q == 0 and n + 1 < V_HEADS:
                        sums(n + 1)
                    pe.wait_ge(ylo_done, n + 1)
                    pe.wait_ge(wlo_done, m + 1)
                    for c in range(CH_PASS[q]):
                        hi, lo = w_hi[:, m % 2, c * P:(c + 1) * P], w_lo[:, m % 2, c * P:(c + 1) * P]
                        for i in range(2):
                            bank = p_out[2 * c + i]
                            if q and n == 0:
                                pe.wait_ge(bank_used, 2 * first_ch[q - 1] + 2 * c + i + 1)
                            cut = slice(i * HALF, (i + 1) * HALF)
                            nc.tensor.matmul(bank[:], hi, y(0, n)[:, cut], start=(n == 0), stop=False)
                            nc.tensor.matmul(bank[:], hi, y(1, n)[:, cut], start=False, stop=False)
                            last = nc.tensor.matmul(bank[:], lo, y(0, n)[:, cut], start=False,
                                                    stop=(n == V_HEADS - 1))
                    last.then_inc(w_used, 1)
                for r in range(2):
                    for k in range(KD):
                        pe.wait_ge(sq2, KD * r + k + 1)
                        if k == 0:
                            pe.wait_ge(ln2, 2) if r else pe.wait_ge(ln_done, 2 * V_HEADS)
                        for i in range(2):
                            last = nc.tensor.matmul(p_ss[i][:], ones[:], sq[:, i * HALF:(i + 1) * HALF],
                                                    start=(k == 0), stop=(k == KD - 1))
                        last.then_inc(ss2, 1)

            @block.vector
            def _(dve):
                def drain(q):
                    dve.wait_ge(w_used, V_HEADS * (q + 1))
                    dve.wait_ge(x_in, 16)
                    for c in range(CH_PASS[q]):
                        ch = first_ch[q] + c
                        for i in range(2):
                            cut = slice(i * HALF, (i + 1) * HALF)
                            nc.vector.scalar_tensor_tensor(x1[:, ch, cut], p_out[2 * c + i][:],
                                                           keep["gate"][:, ch:ch + 1], x1[:, ch, cut],
                                                           ALU.mult, ALU.add).then_inc(bank_used, 1)

                dve.wait_ge(cst, 48)
                for m, (q, n) in enumerate(steps):
                    cn = CH_PASS[q] * P
                    if q and n == 0:
                        drain(q - 1)
                    dve.wait_ge(w_in[m % 2], 16 * (m // 2 + 1))
                    if m >= 2:
                        dve.wait_ge(w_used, m - 1)
                    nc.vector.tensor_copy(w_hi[:, m % 2, 0:cn], w_raw[:, m % 2, 0:cn]).then_inc(whi_done, 1)
                    if q == 0:
                        dve.wait_ge(oz_in[n % 2], 32 * (n // 2 + 1))
                        nc.vector.scalar_tensor_tensor(zb[:, n % 2, :], ob[:, n % 2, :], nw[:, 0:1], zb[:, n % 2, :],
                                                       ALU.mult, ALU.mult).then_inc(gz_done, 1)
                        dve.wait_ge(gz_done, n + 1)
                        dve.wait_ge(rinv_done, n + 1)
                        nc.vector.tensor_tensor(zb[:, n % 2, :], zb[:, n % 2, :], rinv[:], ALU.mult).then_inc(y_done, 1)
                        dve.wait_ge(y_done, n + 1)
                        nc.vector.tensor_copy(y(0, n), zb[:, n % 2, :]).then_inc(yhi_done, 1)
                drain(len(CH_PASS) - 1)
                dve.wait_ge(ri2, 1)
                dve.wait_ge(bank_used, 2 * KD)
                for k in range(KD):
                    nc.vector.scalar_tensor_tensor(x1[:, k, :], x1[:, k, :], fg[:, k:k + 1], rinv[:],
                                                   ALU.mult, ALU.mult).then_inc(xn2, 1)
                dve.wait_ge(ri2, 2)
                dve.wait_ge(ylo_done, V_HEADS)
                for k in range(KD):
                    if k >= 2:
                        dve.wait_ge(hlo, k - 1)
                    nc.vector.scalar_tensor_tensor(zb[:, k % 2, :], x1[:, k, :], np_col[:, k:k + 1], rinv[:],
                                                   ALU.mult, ALU.mult).then_inc(hh, 1)
                    dve.wait_ge(hh, k + 1)
                    nc.vector.tensor_copy(h_hi[:, k, :], zb[:, k % 2, :]).then_inc(hhi, 1)


MIX_JOBS = ("qa", "ka", "va", "qb", "kb", "vb", "za", "ob", "zb")


def mix_plan(projects, recurs):
    nj = len(MIX_JOBS)
    slices = [("slice", j, h, k) for j in range(nj) for h in range(2) for k in range(KD)] if projects else []
    steps = []
    if recurs:
        steps += [("edge",), ("gaps",)]
        steps += [("cols", w, h) for w in range(3) for h in range(2)]
        steps += [("score", 0, 0), ("score", 0, 1), ("sim", 0)]
        for i in range(NT):
            steps += [("blend", i)]
            if i + 1 < NT:
                steps += [("score", i + 1, 0), ("score", i + 1, 1)]
            steps += [("update", i)]
            steps += [("turn", i, q) for q in range((i + 4) // 4)]
            steps += [("apply", i), ("out", i)]
            if i + 1 < NT:
                steps += [("sim", i + 1)]
        steps += [("store",)]
    steps += [("bcast",)]
    on_pe = ("cols", "score", "sim", "update", "turn", "apply", "out")
    total = sum(s[0] in on_pe for s in steps)
    out, sent, passed = [], 0, 0

    def send(upto):
        nonlocal sent
        while sent < min(upto, len(slices)):
            s = slices[sent]
            if s[2:] == (0, 0):
                out.append(("weights", s[1]))
            out.append(s)
            sent += 1
            if s[3] == KD - 1:
                out.append(("evac", s[1], s[2]))
                if s[2] == 1:
                    if MIX_JOBS[s[1]] in ("qb", "kb"):
                        out.append(("conv", s[1] - 3))
                    if MIX_JOBS[s[1]] in ("za", "ob", "zb"):
                        out.append(("gstore", s[1] - 6))
                    if MIX_JOBS[s[1]] == "vb":
                        out.append(("silu",))

    if not recurs:
        send(4 * KD)
    for s in steps:
        out.append(s)
        if s[0] in on_pe:
            passed += 1
            send(passed * len(slices) // total)
    send(len(slices))
    return out


def stage_mix(nc, ctx, io, keep):
    own = ExitStack()
    with own:
        def sb(name, shape, dt=F32):
            return own.enter_context(nc.sbuf_tensor(name, shape, dt))

        def ps(name, n=HALF):
            return own.enter_context(nc.psum_tensor(name, [P, n], F32))

        sem = lambda name: ctx.enter_context(nc.semaphore(name))
        h_hi, h_lo, ident, ones = keep["h_hi"], keep["h_lo"], keep["ident"], keep["ones"]
        DV = DH + 1

        w_raw = sb("m_raw", [P, KD * P])
        w_hi = sb("m_hi", [P, 2, KD * P], F32R)
        w_lo = sb("m_lo", [P, 2, KD * P], F32R)
        pre = sb("m_pre", [P, TAPS - 1 + T])
        conv_w = sb("m_conv_w", [P, HB, 2, TAPS])
        qa = sb("qa", [P, 2, T])
        ka = sb("ka", [P, 2, T])
        vaT = sb("vaT", [P, T])
        qb = sb("qb", [P, 2, T])
        kb = sb("kb", [P, 2, T])
        vbT = sb("vbT", [P, T])
        gt = sb("m_gt", [P, T])
        va = sb("va", [P, NT, P])
        v1 = sb("v1", [P, NT, DV])
        kw = sb("kw", [P, NT, P])
        alibi = sb("alibi", [P, T])
        sc = sb("sc", [P, 2, 2, T])
        mn = sb("mn", [P, 2, 2])
        ls = sb("ls", [P, 2, 2])
        rl = sb("rl", [P, 2, 2])
        r1 = sb("r1", [P, 2])
        PT = sb("PT", [P, NT, P])
        oA = sb("oA", [P, T])
        rows = sb("m_rows", [P, 2, T])
        dm = sb("dm", [P, NT, P])
        qw = sb("qw", [P, T])
        sm = sb("sm", [P, P])
        C = sb("C", [P, DV])
        hb = sb("hb", [P, P])
        hT = sb("hT", [P, T])
        tri = sb("m_tri", [P, P])
        den = sb("den", [P, 2])
        wk = sb("wk", [P, NT])
        dec = sb("dec", [P, NT])
        cols = sb("m_cols", [P, 2, NT, HB])
        bif = sb("bif", [P, 2])
        lq = sb("lq", [P, 4, DA])
        lp = sb("lp", [P, 2, DA])
        ld = sb("ld", [P, 2])
        nlam = sb("nlam", [P, 1])
        lnd = sb("lnd", [P, 1])

        p_job = [ps("m_job0"), ps("m_job1")]
        p_sc = ps("p_sc", T)
        p_t, p_a, p_s, p_u = ps("p_t"), ps("p_a"), ps("p_s"), ps("p_u")

        flat = sc[:].rearrange("p a b c -> p (a b) c")
        r_lf, r_i, r_b, r_m = (flat[:, q, :] for q in range(4))
        r_t, r_w = oA, hT

        N_IT = HB + 1
        plans = [mix_plan(True, False)] + [mix_plan(True, True)] * (HB - 1) + [mix_plan(False, True)]
        order = [ordinals(p) for p in plans]
        nj = len(MIX_JOBS)
        NTURN = sum((i + 4) // 4 for i in range(NT))

        cst = sem("d_cst"); lq_in = sem("d_lq")
        w_in = sem("d_w"); w_hi_done = sem("d_whi"); w_lo_done = sem("d_wlo")
        half_done = sem("d_half"); evac_done = sem("d_evac"); conv_step = sem("d_conv"); silu_done = sem("d_silu")
        set_up = sem("d_set"); g_store = sem("d_gst")
        g_act = sem("d_gact"); g_dve = sem("d_gdve"); g_pe = sem("d_gpe"); g_dma = sem("d_gdma"); i_moved = sem("d_im")
        lam = sem("d_lam"); lam_a = sem("d_lama")
        rows_in = sem("d_rows"); alibi_in = sem("d_alibi")
        edge_dve = sem("d_edged"); edge_act = sem("d_edgea")
        gap_dve = sem("d_gap"); gap_exp = sem("d_gape"); qw_done = sem("d_qw")
        cols_ready = sem("d_cr"); cols_done = sem("d_cd")
        sc_ready = sem("d_sr"); sc_used = sem("d_su"); exp_done = sem("d_exp")
        rl_done = sem("d_rl"); p1_done = sem("d_p1"); blend_done = sem("d_bl")
        turn_ready = sem("d_tr"); turn_cp = sem("d_tc"); app_ready = sem("d_ar"); app_cp = sem("d_ac")
        sim_ready = sem("d_simr"); sim_done = sem("d_simd"); up_ready = sem("d_upr"); c_done = sem("d_c")
        den_done = sem("d_den"); hb_done = sem("d_hb"); out_ready = sem("d_or"); out_cp = sem("d_oc")
        a_stored = sem("d_as")

        def job(i, j):
            return 1 + nj * i + j

        with nc.Block() as block:
            @block.sync
            def _(sp):
                for dst, src in ((tri[:], io["tri"]), (conv_w[:], io["conv_w2"]), (bif[0:4, :], io["bif"])):
                    sp.dma_start(dst, src).then_inc(cst, 16)
                sp.dma_start(lq[:].rearrange("p a d -> p (a d)"), io["lq"].broadcast_to([P, 4 * DA])).then_inc(lq_in, 16)
                sp.dma_start(alibi[:], io["alibi"][:, 0, :]).then_inc(alibi_in, 16)

                def load(J):
                    if J >= 1:
                        sp.wait_ge(w_lo_done, J)
                    sp.dma_start(w_raw[:], io["w2"][J]).then_inc(w_in, 16)

                load(0)
                sp.wait_ge(evac_done, 2)
                sp.dma_start(r_i[0:4, :], pre[32:36, TAPS - 1:]).then_inc(i_moved, 16)
                for i in range(N_IT):
                    g = i - 1
                    for s in plans[i]:
                        if s[0] == "weights":
                            load(job(i, s[1]))
                        elif s[0] == "bcast" and i < HB:
                            if i == 0:
                                sp.wait_ge(g_dve, 24)
                                sp.dma_start(io["mrows"][0:4, :], r_t[0:4, :]).then_inc(g_dma, 16)
                                sp.dma_start(io["mrows"][4:8, :], r_w[0:4, :]).then_inc(g_dma, 16)
                                sp.wait_ge(g_dma, 32)
                            else:
                                sp.wait_ge(gap_dve, NT * i)
                                sp.wait_ge(edge_dve, 2 * i)
                                sp.wait_ge(edge_act, 2 * i)
                                sp.wait_ge(qw_done, 2 * i)
                                sp.wait_ge(sc_used, 2 * NT * i)
                                sp.dma_start(alibi[:], io["alibi"][:, i, :]).then_inc(alibi_in, 16)
                            for q in range(2):
                                sp.dma_start(rows[:, q, :], io["mrows"][4 * q + i:4 * q + i + 1, :].broadcast_to([P, T])
                                             ).then_inc(rows_in, 16)
                        elif s[0] == "gstore":
                            sp.wait_ge(evac_done, 2 * job(i, 6 + s[1]) + 2)
                            sp.dma_start(io["g_scr"][3 * i + s[1]], gt[:]).then_inc(g_store, 16)
                        elif s[0] == "store":
                            sp.wait_ge(app_cp, NT * i)
                            sp.dma_start(io["a_scr"][g], oA[:]).then_inc(a_stored, 16)
                            sp.wait_ge(out_cp, NT * i)
                            sp.dma_start(io["a_scr"][HA + g], hT[:]).then_inc(a_stored, 16)
                sp.wait_ge(g_store, 16 * 3 * HB)
                sp.wait_ge(a_stored, 32 * HB)

            @block.gpsimd
            def _(pool):
                def split_lo(J):
                    pool.wait_ge(w_hi_done, J + 1)
                    nc.gpsimd.tensor_tensor(w_lo[:, J % 2, :], w_raw[:], w_hi[:, J % 2, :].bitcast(F32),
                                            ALU.subtract).then_inc(w_lo_done, 1)

                split_lo(0)
                for i in range(N_IT):
                    g = i - 1
                    for s in plans[i]:
                        if s[0] == "weights":
                            split_lo(job(i, s[1]))
                        elif s[0] == "gaps":
                            pool.wait_ge(qw_done, 2 * g + 1)
                            pool.wait_ge(silu_done, 2 * (g + 1))
                            nc.gpsimd.tensor_tensor(qw[:], qw[:], qb[:, g % 2, :], ALU.mult).then_inc(qw_done, 1)

            @block.scalar
            def _(act):
                def evac(J, h, out, func=ACT.Copy, scale=1.0):
                    act.wait_ge(half_done, 2 * J + h + 1)
                    nc.scalar.activation(out[:, h * HALF:(h + 1) * HALF], p_job[h][:], func,
                                         scale=scale).then_inc(evac_done, 1)

                evac(0, 0, pre[:, TAPS - 1:])
                evac(0, 1, pre[:, TAPS - 1:])
                act.wait_ge(g_dve, 2)
                nc.scalar.activation(r_w[0:4, :], r_w[0:4, :], ACT.Exp).then_inc(g_act, 1)
                act.wait_ge(g_act, 1)
                nc.scalar.activation(r_w[0:4, :], r_w[0:4, :], ACT.Ln, bias=1.0).then_inc(g_act, 1)
                act.wait_ge(lam, 2)
                nc.scalar.activation(ld[:], ld[:], ACT.Exp).then_inc(lam_a, 1)
                act.wait_ge(g_pe, 1)
                nc.scalar.activation(cols[:, 0], p_t[:, 0:32].rearrange("p (t h) -> p t h", h=HB),
                                     ACT.Copy).then_inc(g_act, 1)
                nc.scalar.activation(cols[:, 1], p_t[:, 32:64].rearrange("p (t h) -> p t h", h=HB),
                                     ACT.Exp, scale=-1.0).then_inc(g_act, 1)

                for i in range(N_IT):
                    g = i - 1
                    o, n = order[i]
                    for s in plans[i]:
                        if s[0] == "evac":
                            j, h = s[1:]
                            J = job(i, j)
                            name = MIX_JOBS[j]
                            if name == "qa":
                                if h == 0 and i >= 2:
                                    act.wait_ge(sc_ready, 2 * NT * (i - 1))
                                evac(J, h, qa[:, i % 2, :], ACT.Copy, -(DA ** -0.5))
                            elif name == "ka":
                                evac(J, h, ka[:, i % 2, :])
                            elif name == "va":
                                if h == 0 and i >= 1:
                                    act.wait_ge(cols_ready, 6 * i)
                                evac(J, h, vaT)
                            elif name == "vb":
                                evac(J, h, vbT)
                            elif name in ("qb", "kb"):
                                if h == 0:
                                    if i or name == "kb":
                                        act.wait_ge(conv_step, 8 * i + (4 if name == "kb" else 0))
                                    else:
                                        act.wait_ge(i_moved, 16)
                                        act.wait_ge(g_dve, 1)
                                evac(J, h, pre[:, TAPS - 1:])
                            else:
                                if h == 0 and (i or name != "za"):
                                    act.wait_ge(g_store, 16 * (3 * i + j - 6))
                                evac(J, h, gt, ACT.Sigmoid if name == "ob" else ACT.Silu)
                        elif s[0] == "silu":
                            act.wait_ge(conv_step, 8 * (i + 1))
                            nc.scalar.activation(qb[:, i % 2, :], qb[:, i % 2, :], ACT.Silu).then_inc(silu_done, 1)
                            nc.scalar.activation(kb[:, i % 2, :], kb[:, i % 2, :], ACT.Silu).then_inc(silu_done, 1)
                        elif s[0] == "edge":
                            act.wait_ge(edge_dve, 2 * g + 1)
                            nc.scalar.activation(wk[:], wk[:], ACT.Exp).then_inc(edge_act, 1)
                            if g >= 1:
                                act.wait_ge(c_done, (NT + 1) * g)
                            nc.scalar.activation(dec[:], rows[:, 1, P - 1::P], ACT.Exp).then_inc(edge_act, 1)
                        elif s[0] == "gaps":
                            if g >= 1:
                                act.wait_ge(up_ready, NT * g)
                            act.wait_ge(rows_in, 32 * (g + 1))
                            act.wait_ge(set_up, 4)
                            nc.scalar.activation(qw[:], rows[:, 1, :], ACT.Exp, bias=lnd[:, 0:1]).then_inc(qw_done, 1)
                            act.wait_ge(gap_dve, NT * (g + 1))
                            nc.scalar.activation(dm[:], dm[:], ACT.Exp, bias=lnd[:, 0:1]).then_inc(gap_exp, 1)
                        elif s[0] == "score":
                            t, c = s[1:]
                            m = 2 * NT * g + 2 * t + c
                            w = (t + 1) * P
                            act.wait_ge(sc_used, m + 1)
                            if m >= 4:
                                act.wait_ge(rl_done, 2 * (m // 2) - 2)
                            nc.scalar.activation(sc[:, t % 2, c, 0:w], sc[:, t % 2, c, 0:w], ACT.Exp, scale=-1.0,
                                                 bias=mn[:, t % 2, c:c + 1], accum_out=ls[:, t % 2, c:c + 1]
                                                 ).then_inc(exp_done, 1)
                        elif s[0] == "blend":
                            t = s[1]
                            w = (t + 1) * P
                            m = NT * g + t
                            act.wait_ge(rl_done, 2 * m + 2)
                            nc.scalar.activation(sc[:, t % 2, 1, 0:w], sc[:, t % 2, 1, 0:w], ACT.Copy,
                                                 scale=r1[:, t % 2:t % 2 + 1]).then_inc(p1_done, 1)
                        elif s[0] == "cols":
                            w, h = s[1:]
                            m = 6 * g + o[s]
                            act.wait_ge(cols_ready, m + 1)
                            src = p_t[:].rearrange("p (t c) -> p t c", c=P)
                            cut = slice(4 * h, 4 * h + 4)
                            if w == 0:
                                if g >= 1:
                                    act.wait_ge(app_ready, NT * g)
                                nc.scalar.activation(va[:, cut, :], src, ACT.Copy).then_inc(cols_done, 1)
                            elif w == 1:
                                if g >= 1:
                                    act.wait_ge(up_ready, NT * g)
                                act.wait_ge(set_up, 4)
                                nc.scalar.activation(v1[:, cut, 0:P], src, ACT.Copy).then_inc(cols_done, 1)
                            else:
                                act.wait_ge(edge_act, 2 * g + 1)
                                for t in range(4):
                                    last = nc.scalar.activation(kw[:, 4 * h + t, :], p_t[:, t * P:(t + 1) * P], ACT.Copy,
                                                                scale=wk[:, 4 * h + t:4 * h + t + 1])
                                last.then_inc(cols_done, 1)
                        elif s[0] == "turn":
                            t, q = s[1:]
                            m = NTURN * g + o[s]
                            nb = min(4, t + 1 - 4 * q)
                            act.wait_ge(turn_ready, m + 1)
                            if q == 0 and NT * g + t >= 1:
                                act.wait_ge(app_ready, NT * g + t)
                            nc.scalar.activation(PT[:, 4 * q:4 * q + nb, :].rearrange("p b c -> p (b c)"),
                                                 p_t[:, 0:nb * P], ACT.Copy).then_inc(turn_cp, 1)
                        elif s[0] == "update":
                            c = s[1]
                            m = NT * g + c
                            act.wait_ge(den_done, 3 * m + 3)
                            if m >= 1:
                                act.wait_ge(out_ready, m)
                            nc.scalar.activation(hb[:], p_u[:, 0:P], ACT.Copy, scale=den[:, 1:2]).then_inc(hb_done, 1)
                        elif s[0] == "out":
                            c = s[1]
                            m = NT * g + c
                            act.wait_ge(out_ready, m + 1)
                            if c == 0 and g >= 1:
                                act.wait_ge(a_stored, 32 * g)
                            elif g == 0 and c == 0:
                                act.wait_ge(g_dma, 32)
                            nc.scalar.activation(hT[:, c * P:(c + 1) * P], p_u[:, 256:256 + P],
                                                 ACT.Copy).then_inc(out_cp, 1)

            @block.tensor
            def _(pe):
                def piece(J, h, k):
                    if h == 0 and k == 0:
                        pe.wait_ge(w_lo_done, J + 1)
                    if k == 0 and J >= 1:
                        pe.wait_ge(evac_done, 2 * (J - 1) + h + 1)
                    cut = slice(h * HALF, (h + 1) * HALF)
                    hi, lo = w_hi[:, J % 2, k * P:(k + 1) * P], w_lo[:, J % 2, k * P:(k + 1) * P]
                    nc.tensor.matmul(p_job[h][:], hi, h_hi[:, k, cut], start=(k == 0), stop=False)
                    nc.tensor.matmul(p_job[h][:], hi, h_lo[:, k, cut], start=False, stop=False)
                    last = nc.tensor.matmul(p_job[h][:], lo, h_hi[:, k, cut], start=False, stop=(k == KD - 1))
                    if k == KD - 1:
                        last.then_inc(half_done, 1)

                for h in range(2):
                    for k in range(KD):
                        piece(0, h, k)
                pe.wait_ge(g_dve, 24)
                for q, r in ((0, r_i), (1, r_m)):
                    for t in range(NT):
                        at = 32 * q + HB * t
                        last = nc.tensor.transpose(p_t[:, at:at + HB], r[0:HB, t * P:(t + 1) * P], ident[0:HB, 0:HB])
                last.then_inc(g_pe, 1)

                for i in range(N_IT):
                    g = i - 1
                    o, n = order[i]
                    for s in plans[i]:
                        if s[0] == "slice":
                            piece(job(i, s[1]), s[2], s[3])
                        elif s[0] == "cols":
                            w, h = s[1:]
                            m = 6 * g + o[s]
                            pe.wait_ge(evac_done, 2 * job(g, 5) + 2)
                            pe.wait_ge(silu_done, 2 * (g + 1))
                            if o[s]:
                                pe.wait_ge(cols_done, m)
                            elif g:
                                pe.wait_ge(turn_cp, NTURN * g)
                            else:
                                pe.wait_ge(g_act, 4)
                            src = (vaT[:], vbT[:], kb[:, g % 2, :])[w]
                            for t in range(4):
                                last = nc.tensor.transpose(p_t[:, t * P:(t + 1) * P],
                                                           src[:, (4 * h + t) * P:(4 * h + t + 1) * P], ident[:])
                            last.then_inc(cols_ready, 1)
                        elif s[0] == "score":
                            t, c = s[1:]
                            m = 2 * NT * g + 2 * t + c
                            pe.wait_ge(evac_done, 2 * job(g, 1) + 2)
                            if m >= 1:
                                pe.wait_ge(sc_used, m)
                            w = (t + 1) * P
                            half = slice(DA * c, DA * (c + 1))
                            for a in range(0, w, HALF):
                                e = min(a + HALF, w)
                                last = nc.tensor.matmul(p_sc[:, a:e], qa[half, g % 2, t * P:(t + 1) * P],
                                                        ka[half, g % 2, a:e], start=True, stop=True)
                            last.then_inc(sc_ready, 1)
                        elif s[0] == "turn":
                            t, q = s[1:]
                            m = NTURN * g + o[s]
                            pe.wait_ge(blend_done, NT * g + t + 1)
                            if o[s]:
                                pe.wait_ge(turn_cp, m)
                            else:
                                pe.wait_ge(cols_done, 6 * (g + 1))
                            nb = min(4, t + 1 - 4 * q)
                            for b in range(nb):
                                last = nc.tensor.transpose(p_t[:, b * P:(b + 1) * P],
                                                           sc[:, t % 2, 0, (4 * q + b) * P:(4 * q + b + 1) * P], ident[:])
                            last.then_inc(turn_ready, 1)
                        elif s[0] == "apply":
                            t = s[1]
                            m = NT * g + t
                            pe.wait_ge(turn_cp, NTURN * g + o[("turn", t, t // 4)] + 1)
                            if m >= 1:
                                pe.wait_ge(app_cp, m)
                            for b in range(t + 1):
                                last = nc.tensor.matmul(p_a[:, 0:P], va[:, b, :], PT[:, b, :], start=(b == 0), stop=(b == t))
                            last.then_inc(app_ready, 1)
                        elif s[0] == "sim":
                            c = s[1]
                            m = NT * g + c
                            if m >= 1:
                                pe.wait_ge(c_done, (NT + 1) * g + 1 + c)
                            pe.wait_ge(silu_done, 2 * (g + 1))
                            cut = slice(c * P, (c + 1) * P)
                            nc.tensor.matmul(p_s[:, 0:P], kb[:, g % 2, cut], qb[:, g % 2, cut], start=True, stop=True
                                             ).then_inc(sim_ready, 1)
                        elif s[0] == "update":
                            c = s[1]
                            m = NT * g + c
                            pe.wait_ge(sim_done, m + 1)
                            pe.wait_ge(c_done, (NT + 1) * g + 1 + c)
                            pe.wait_ge(qw_done, 2 * g + 2)
                            pe.wait_ge(cols_done, 6 * (g + 1))
                            if m >= 1:
                                pe.wait_ge(out_cp, m)
                            nc.tensor.matmul(p_u[:, 0:DV], qw[:, c * P:(c + 1) * P], C[:], start=True, stop=False)
                            nc.tensor.matmul(p_u[:, 0:DV], sm[:], v1[:, c, :], start=False, stop=True)
                            nc.tensor.matmul(p_s[:, 256:256 + DV], kw[:, c, :], v1[:, c, :], start=True, stop=True
                                             ).then_inc(up_ready, 1)
                        elif s[0] == "out":
                            c = s[1]
                            m = NT * g + c
                            pe.wait_ge(hb_done, m + 1)
                            nc.tensor.transpose(p_u[:, 256:256 + P], hb[:], ident[:]).then_inc(out_ready, 1)

            @block.vector
            def _(dve):
                def split_hi(J):
                    dve.wait_ge(w_in, 16 * (J + 1))
                    if J >= 2:
                        dve.wait_ge(half_done, 2 * (J - 1))
                    nc.vector.tensor_copy(w_hi[:, J % 2, :], w_raw[:]).then_inc(w_hi_done, 1)

                nc.vector.memset(pre[:, 0:TAPS - 1], 0.0).then_inc(set_up, 1)
                nc.vector.memset(v1[:, :, P:DV], 1.0).then_inc(set_up, 1)
                nc.vector.memset(lnd[:], float(np.log(DH ** -0.5))).then_inc(set_up, 1)
                nc.vector.memset(nlam[:], 0.0).then_inc(set_up, 1)
                split_hi(0)
                dve.wait_ge(lq_in, 16)
                nc.vector.tensor_tensor(lp[:], lq[:, 0::2, :], lq[:, 1::2, :], ALU.mult).then_inc(lam, 1)
                dve.wait_ge(lam, 1)
                nc.vector.reduce_sum(ld[:], lp[:], axis=AX).then_inc(lam, 1)

                dve.wait_ge(cst, 48)
                dve.wait_ge(evac_done, 2)
                nc.vector.tensor_scalar(r_lf[0:4, :], pre[0:4, TAPS - 1:], bif[0:4, 0:1], None, ALU.add
                                        ).then_inc(g_dve, 1)
                dve.wait_ge(g_dve, 1)
                nc.vector.scalar_tensor_tensor(r_w[0:4, :], r_lf[0:4, :], -1.0, r_lf[0:4, :], ALU.mult, ALU.min
                                               ).then_inc(g_dve, 1)
                dve.wait_ge(g_act, 2)
                nc.vector.scalar_tensor_tensor(r_lf[0:4, :], r_lf[0:4, :], 0.0, r_w[0:4, :], ALU.min, ALU.subtract
                                               ).then_inc(g_dve, 1)
                dve.wait_ge(i_moved, 16)
                nc.vector.tensor_scalar(r_i[0:4, :], r_i[0:4, :], bif[0:4, 1:2], None, ALU.add).then_inc(g_dve, 1)
                dve.wait_ge(g_dve, 4)
                nc.vector.tensor_tensor_scan(r_m[0:4, :], r_lf[0:4, :], r_i[0:4, :], 0.0, ALU.add, ALU.max
                                             ).then_inc(g_dve, 1)
                for t in range(NT):
                    c = slice(t * P, (t + 1) * P)
                    nc.vector.tensor_tensor_scan(r_b[0:4, c], ones[0:4, :], r_lf[0:4, c], 0.0, ALU.mult, ALU.add
                                                 ).then_inc(g_dve, 1)
                dve.wait_ge(g_dve, 13)
                nc.vector.tensor_tensor(r_t[0:4, :], r_b[0:4, :], r_m[0:4, :], ALU.subtract).then_inc(g_dve, 1)
                nc.vector.tensor_tensor(r_i[0:4, :], r_i[0:4, :], r_b[0:4, :], ALU.subtract).then_inc(g_dve, 1)
                dve.wait_ge(g_dve, 14)
                nc.vector.tensor_copy(r_w[0:4, 0:P], r_t[0:4, 0:P]).then_inc(g_dve, 1)
                for t in range(1, NT):
                    c = slice(t * P, (t + 1) * P)
                    nc.vector.tensor_scalar(r_w[0:4, c], r_t[0:4, c], r_m[0:4, t * P - 1:t * P], None, ALU.add
                                            ).then_inc(g_dve, 1)
                dve.wait_ge(g_dve, 23)
                dve.wait_ge(lam_a, 1)
                nc.vector.tensor_tensor(nlam[:], ld[:, 1:2], ld[:, 0:1], ALU.subtract).then_inc(lam, 1)
                dve.wait_ge(lam, 3)
                nc.vector.tensor_scalar_add(nlam[:], nlam[:], -0.2).then_inc(g_dve, 1)

                for i in range(N_IT):
                    g = i - 1
                    o, n = order[i]
                    for s in plans[i]:
                        if s[0] == "weights":
                            split_hi(job(i, s[1]))
                        elif s[0] == "conv":
                            j = s[1]
                            base = 8 * i + 4 * j
                            dst = (qb, kb)[j][:, i % 2, :]
                            dve.wait_ge(evac_done, 2 * job(i, 3 + j) + 2)
                            if i >= 2:
                                dve.wait_ge(sim_ready, NT * (i - 1))
                            nc.vector.tensor_scalar(dst, pre[:, 0:T], conv_w[:, i, j, 0:1], None,
                                                    ALU.mult).then_inc(conv_step, 1)
                            for q in range(1, TAPS):
                                dve.wait_ge(conv_step, base + q)
                                nc.vector.scalar_tensor_tensor(dst, pre[:, q:q + T], conv_w[:, i, j, q:q + 1], dst,
                                                               ALU.mult, ALU.add).then_inc(conv_step, 1)
                        elif s[0] == "edge":
                            dve.wait_ge(rows_in, 32 * (g + 1))
                            dve.wait_ge(g_act, 4)
                            if g >= 1:
                                dve.wait_ge(cols_done, 6 * g)
                                dve.wait_ge(up_ready, NT * g)
                                dve.wait_ge(c_done, (NT + 1) * g)
                            nc.vector.tensor_tensor(wk[:], rows[:, 0, P - 1::P], cols[:, 0, :, g], ALU.add
                                                    ).then_inc(edge_dve, 1)
                            nc.vector.memset(C[:], 0.0).then_inc(c_done, 1)
                            nc.vector.memset(den[:], 0.0).then_inc(edge_dve, 1)
                        elif s[0] == "gaps":
                            if g >= 1:
                                dve.wait_ge(sim_done, NT * g)
                            for t in range(NT):
                                nc.vector.scalar_tensor_tensor(dm[:, t, :], rows[:, 0, t * P:(t + 1) * P],
                                                               cols[:, 0, t, g:g + 1], tri[:], ALU.add, ALU.add
                                                               ).then_inc(gap_dve, 1)
                        elif s[0] == "score":
                            t, c = s[1:]
                            m = 2 * NT * g + 2 * t + c
                            w = (t + 1) * P
                            dve.wait_ge(sc_ready, m + 1)
                            dve.wait_ge(alibi_in, 16 * (g + 1))
                            if NT * g + t >= 2:
                                dve.wait_ge(turn_ready, NTURN * g + o[("turn", t - 2, (t - 2) // 4)] + 1 if t >= 2
                                            else NTURN * (g - 1) + o[("turn", NT - 2 + t, 1)] + 1)
                            else:
                                dve.wait_ge(g_pe, 1)
                            nc.vector.tensor_tensor_reduce(
                                out=sc[:, t % 2, c, 0:w], in0=p_sc[:, 0:w], in1=alibi[:, T - w:], scale=1.0,
                                scalar=3.0e38, op0=ALU.add, op1=ALU.min, accum_out=mn[:, t % 2, c:c + 1]
                            ).then_inc(sc_used, 1)
                        elif s[0] == "blend":
                            t = s[1]
                            w = (t + 1) * P
                            m = NT * g + t
                            dve.wait_ge(exp_done, 2 * m + 2)
                            if m >= 2:
                                dve.wait_ge(blend_done, m - 1)
                            nc.vector.reciprocal(rl[:, t % 2, :], ls[:, t % 2, :]).then_inc(rl_done, 1)
                            dve.wait_ge(rl_done, 2 * m + 1)
                            if m >= 2:
                                dve.wait_ge(p1_done, m - 1)
                            nc.vector.tensor_tensor(r1[:, t % 2:t % 2 + 1], rl[:, t % 2, 1:2], nlam[:], ALU.mult
                                                    ).then_inc(rl_done, 1)
                            dve.wait_ge(p1_done, m + 1)
                            nc.vector.scalar_tensor_tensor(sc[:, t % 2, 0, 0:w], sc[:, t % 2, 0, 0:w],
                                                           rl[:, t % 2, 0:1], sc[:, t % 2, 1, 0:w],
                                                           ALU.mult, ALU.add).then_inc(blend_done, 1)
                        elif s[0] == "apply":
                            t = s[1]
                            m = NT * g + t
                            dve.wait_ge(app_ready, m + 1)
                            if t == 0 and g >= 1:
                                dve.wait_ge(a_stored, 32 * g)
                            elif t == 0:
                                dve.wait_ge(g_dma, 32)
                            nc.vector.tensor_copy(oA[:, t * P:(t + 1) * P], p_a[:, 0:P]).then_inc(app_cp, 1)
                        elif s[0] == "sim":
                            c = s[1]
                            m = NT * g + c
                            dve.wait_ge(sim_ready, m + 1)
                            dve.wait_ge(gap_exp, g + 1)
                            if m >= 1:
                                dve.wait_ge(up_ready, m)
                            nc.vector.tensor_tensor(sm[:], p_s[:, 0:P], dm[:, c, :], ALU.mult).then_inc(sim_done, 1)
                        elif s[0] == "update":
                            c = s[1]
                            m = NT * g + c
                            dve.wait_ge(up_ready, m + 1)
                            dve.wait_ge(edge_act, 2 * g + 2)
                            if m >= 1:
                                dve.wait_ge(hb_done, m)
                            dve.wait_ge(edge_dve, 2 * g + 2)
                            nc.vector.scalar_tensor_tensor(den[:, 0:1], p_u[:, P:DV], -1.0, cols[:, 1, c, g:g + 1],
                                                           ALU.mult, ALU.max).then_inc(den_done, 1)
                            dve.wait_ge(den_done, 3 * m + 1)
                            nc.vector.tensor_tensor(den[:, 0:1], p_u[:, P:DV], den[:, 0:1], ALU.max
                                                    ).then_inc(den_done, 1)
                            dve.wait_ge(den_done, 3 * m + 2)
                            nc.vector.reciprocal(den[:, 1:2], den[:, 0:1]).then_inc(den_done, 1)
                            dve.wait_ge(c_done, (NT + 1) * g + 1 + c)
                            nc.vector.scalar_tensor_tensor(C[:], C[:], dec[:, c:c + 1], p_s[:, 256:256 + DV],
                                                           ALU.mult, ALU.add).then_inc(c_done, 1)


def stage_merge(nc, ctx, io, keep):
    own = ExitStack()
    with own:
        def sb(name, shape, dt=F32):
            return own.enter_context(nc.sbuf_tensor(name, shape, dt))

        def ps(name):
            return own.enter_context(nc.psum_tensor(name, [P, HALF], F32))

        sem = lambda name: ctx.enter_context(nc.semaphore(name))
        h_hi, h_lo, ident, ones, eps = (keep[n] for n in ("h_hi", "h_lo", "ident", "ones", "eps"))
        NY = HA + HB
        y_hi = sb("y_hi", [P, NY, T], F32R)
        y_lo = sb("y_lo", [P, NY, T], F32R)
        w_raw = sb("e_raw", [P, KD * P])
        w_hi = sb("e_hi", [P, 2, KD * P], F32R)
        w_lo = sb("e_lo", [P, 2, KD * P], F32R)
        mg = sb("mg", [P, KD, T])
        ab = sb("ab", [P, T])
        g1 = sb("g1", [P, T])
        sq = sb("e_sq", [P, T])
        rinv = sb("e_rinv", [P, T])
        ny = sb("ny", [P, NY])
        sga, sgb = sb("sga", [P, T]), ab
        banks = [ps(f"e_b{i}") for i in range(8)]
        p_ss = banks[6:8]

        cst = sem("e_cst"); nys = sem("e_nys"); in_a = sem("e_ina"); in_g = sem("e_ing")
        ob_done = sem("e_ob"); sq_done = sem("e_sq"); ss_done = sem("e_ss"); ln_done = sem("e_ln"); ri_done = sem("e_ri")
        gz = sem("e_gz"); yb = sem("e_y"); yh = sem("e_yh"); yl = sem("e_yl")
        w_in = sem("e_w"); w_hi_done = sem("e_whi"); w_lo_done = sem("e_wlo"); job_done = sem("e_job")
        sg_done = sem("e_sg"); m1 = sem("e_m1"); m2 = sem("e_m2"); m3 = sem("e_m3")
        wo_in = sem("e_wo"); wo_hi = sem("e_wohi"); wo_lo = sem("e_wolo"); mg_hi = sem("e_mh"); mg_lo = sem("e_ml")
        x_in = [sem("e_x0"), sem("e_x1")]; o_ready = sem("e_or"); x_ready = sem("e_xr")
        r_sq = sem("e_rsq"); r_ln = sem("e_rln"); r_done = sem("e_rd"); t_done = sem("e_t"); f_done = sem("e_f")
        stored = [sem("e_st0"), sem("e_st1")]
        NJ = 3 * KD

        with nc.Block() as block:
            @block.sync
            def _(sp):
                sp.dma_start(ny[:], io["norm_y"]).then_inc(cst, 16)

                def load(J):
                    if J >= 1:
                        sp.wait_ge(w_lo_done, J)
                    sp.dma_start(w_raw[:], io["w3"][J]).then_inc(w_in, 16)

                load(0)
                load(1)
                load(2)
                for n in range(NY):
                    if n >= 1:
                        sp.wait_ge(yl, n)
                    sp.dma_start(ab[:], io["a_scr"][n]).then_inc(in_a, 16)
                    if n >= HA:
                        sp.dma_start(g1[:], io["g_scr"][3 * (n - HA) + 1]).then_inc(in_g, 16)
                        sp.wait_ge(ob_done, n - HA + 1)
                        sp.dma_start(g1[:], io["g_scr"][3 * (n - HA) + 2]).then_inc(in_g, 16)
                    else:
                        sp.dma_start(g1[:], io["g_scr"][3 * n]).then_inc(in_g, 16)
                for J in range(3, NJ):
                    load(J)

            @block.gpsimd
            def _(pool):
                def split_lo(J):
                    pool.wait_ge(w_hi_done, J + 1)
                    nc.gpsimd.tensor_tensor(w_lo[:, J % 2, :], w_raw[:], w_hi[:, J % 2, :].bitcast(F32),
                                            ALU.subtract).then_inc(w_lo_done, 1)

                split_lo(0)
                split_lo(1)
                for n in range(NY):
                    pool.wait_ge(yh, n + 1)
                    nc.gpsimd.tensor_tensor(y_lo[:, n, :], ab[:], y_hi[:, n, :].bitcast(F32),
                                            ALU.subtract).then_inc(yl, 1)
                for J in range(2, NJ):
                    split_lo(J)

            @block.scalar
            def _(act):
                for n in range(NY):
                    if n < HA:
                        act.wait_ge(in_a, 16 * (n + 1))
                    else:
                        act.wait_ge(ob_done, n - HA + 1)
                    if n >= 1:
                        act.wait_ge(ss_done, n)
                    nc.scalar.activation(sq[:], ab[:], ACT.Square).then_inc(sq_done, 1)
                    act.wait_ge(ss_done, n + 1)
                    if n >= 1:
                        act.wait_ge(yb, n)
                    for i in range(2):
                        nc.scalar.activation(rinv[:, i * HALF:(i + 1) * HALF], p_ss[i][:], ACT.Ln, scale=1.0 / P,
                                             bias=eps[:, 0:1]).then_inc(ln_done, 1)
                    act.wait_ge(ln_done, 2 * n + 2)
                    nc.scalar.activation(rinv[:], rinv[:], ACT.Exp, scale=-0.5).then_inc(ri_done, 1)
                act.wait_ge(yl, NY)
                for c in range(KD):
                    for q, dst in enumerate((sga, sgb)):
                        act.wait_ge(job_done, 3 * c + q + 1)
                        if c >= 1:
                            act.wait_ge((m1, m2)[q], c)
                        for i in range(2):
                            nc.scalar.activation(dst[:, i * HALF:(i + 1) * HALF], banks[2 * q + i][:],
                                                 ACT.Sigmoid).then_inc(sg_done, 1)

            @block.tensor
            def _(pe):
                def sums(n):
                    pe.wait_ge(sq_done, n + 1)
                    if n >= 1:
                        pe.wait_ge(ln_done, 2 * n)
                    for i in range(2):
                        last = nc.tensor.matmul(p_ss[i][:], ones[:], sq[:, i * HALF:(i + 1) * HALF],
                                                start=True, stop=True)
                    last.then_inc(ss_done, 1)

                def three(bank, J, k, hi_rhs, lo_rhs, first, final):
                    hi, lo = w_hi[:, J % 2, k * P:(k + 1) * P], w_lo[:, J % 2, k * P:(k + 1) * P]
                    nc.tensor.matmul(bank, hi, hi_rhs, start=first, stop=False)
                    nc.tensor.matmul(bank, hi, lo_rhs, start=False, stop=False)
                    return nc.tensor.matmul(bank, lo, hi_rhs, start=False, stop=final)

                def gate_job(c, q):
                    J = 3 * c + q
                    pe.wait_ge(w_lo_done, J + 1)
                    if c >= 1:
                        pe.wait_ge(sg_done, 4 * (c - 1) + 2 * q + 2)
                    for i in range(2):
                        cut = slice(i * HALF, (i + 1) * HALF)
                        for k in range(KD):
                            last = three(banks[2 * q + i][:], J, k, h_hi[:, k, cut], h_lo[:, k, cut],
                                         k == 0, k == KD - 1)
                    last.then_inc(job_done, 1)

                gate_job(0, 0)
                sums(0)
                sums(1)
                gate_job(0, 1)
                for n in range(2, NY):
                    sums(n)
                for c in range(KD):
                    if c >= 1:
                        gate_job(c, 0)
                        gate_job(c, 1)
                    J = 3 * c + 2
                    pe.wait_ge(w_lo_done, J + 1)
                    if c == 0:
                        pe.wait_ge(yl, NY)
                        pe.wait_ge(ln_done, 2 * NY)
                    else:
                        pe.wait_ge(m2, c)
                    for q in range(2):
                        for i in range(2):
                            cut = slice(i * HALF, (i + 1) * HALF)
                            for k in range(HA):
                                n = HA * q + k
                                last = three(banks[4 + 2 * q + i][:], J, n, y_hi[:, n, cut], y_lo[:, n, cut],
                                             k == 0, k == HA - 1)
                    last.then_inc(job_done, 1)

            @block.vector
            def _(dve):
                def split_hi(J):
                    dve.wait_ge(w_in, 16 * (J + 1))
                    if J >= 2:
                        dve.wait_ge(job_done, J - 1)
                    nc.vector.tensor_copy(w_hi[:, J % 2, :], w_raw[:]).then_inc(w_hi_done, 1)

                split_hi(0)
                split_hi(1)
                dve.wait_ge(cst, 16)
                nc.vector.tensor_scalar(ny[:, 0:HA], ny[:, 0:HA], 0.8, None, ALU.mult).then_inc(nys, 1)
                dve.wait_ge(nys, 1)
                for n in range(NY):
                    dve.wait_ge(in_a, 16 * (n + 1))
                    if n >= HA:
                        dve.wait_ge(in_g, 16 * (HA + 2 * (n - HA) + 1))
                        nc.vector.tensor_tensor(ab[:], ab[:], g1[:], ALU.mult).then_inc(ob_done, 1)
                        dve.wait_ge(ob_done, n - HA + 1)
                        dve.wait_ge(in_g, 16 * (HA + 2 * (n - HA) + 2))
                    else:
                        dve.wait_ge(in_g, 16 * (n + 1))
                    nc.vector.scalar_tensor_tensor(g1[:], ab[:], ny[:, n:n + 1], g1[:], ALU.mult, ALU.mult
                                                   ).then_inc(gz, 1)
                    dve.wait_ge(gz, n + 1)
                    dve.wait_ge(ri_done, n + 1)
                    nc.vector.tensor_tensor(ab[:], g1[:], rinv[:], ALU.mult).then_inc(yb, 1)
                    dve.wait_ge(yb, n + 1)
                    nc.vector.tensor_copy(y_hi[:, n, :], ab[:]).then_inc(yh, 1)
                for c in range(KD):
                    for q in range(3):
                        J = 3 * c + q
                        if J >= 2:
                            split_hi(J)
                    dve.wait_ge(job_done, 3 * c + 3)
                    dve.wait_ge(sg_done, 4 * c + 4)
                    for i in range(2):
                        cut = slice(i * HALF, (i + 1) * HALF)
                        last = nc.vector.tensor_tensor(mg[:, c, cut], banks[4 + i][:], sga[:, cut], ALU.mult)
                    last.then_inc(m1, 1)
                    for i in range(2):
                        cut = slice(i * HALF, (i + 1) * HALF)
                        last = nc.vector.tensor_tensor(sgb[:, cut], banks[6 + i][:], sgb[:, cut], ALU.mult)
                    last.then_inc(m2, 1)
                    dve.wait_ge(m1, c + 1)
                    dve.wait_ge(m2, c + 1)
                    nc.vector.tensor_tensor(mg[:, c, :], mg[:, c, :], sgb[:], ALU.add).then_inc(m3, 1)

        wo_h, wo_l = y_hi, y_lo
        npost = sga
        xt = ab[:].rearrange("p (k t) -> p k t", k=KD)
        xt = [xt, g1[:].rearrange("p (k t) -> p k t", k=KD)]
        tmp, fin = [sq, rinv], [w_raw, sb("e_fin", [P, T])]
        rr = sb("e_rr", [P, 2])
        with nc.Block() as block:
            @block.sync
            def _(sp):
                sp.dma_start(npost[:], io["norm_post"].broadcast_to([P, T])).then_inc(cst, 16)
                for k in range(KD):
                    if k >= 1:
                        sp.wait_ge(wo_lo, k)
                    sp.dma_start(w_raw[:], io["w_out2"][k * P:(k + 1) * P, :]).then_inc(wo_in, 16)
                for t in range(NT):
                    if t >= 2:
                        sp.wait_ge(x_ready, t - 1)
                    sp.dma_start(xt[t % 2], io["x1_scr"][:, :, t * P:(t + 1) * P].rearrange("k p t -> p k t")
                                 ).then_inc(x_in[t % 2], 16)
                    if t >= 1:
                        sp.wait_ge(f_done, t)
                        sp.dma_start(io["out"][(t - 1) * P:t * P, :], fin[(t - 1) % 2][:]).then_inc(stored[(t - 1) % 2], 16)
                sp.wait_ge(f_done, NT)
                sp.dma_start(io["out"][(NT - 1) * P:, :], fin[(NT - 1) % 2][:]).then_inc(stored[(NT - 1) % 2], 16)
                for q in range(2):
                    sp.wait_ge(stored[q], 16 * NT // 2)

            @block.gpsimd
            def _(pool):
                for k in range(KD):
                    pool.wait_ge(wo_hi, k + 1)
                    nc.gpsimd.tensor_tensor(wo_l[:, k, :], w_raw[:], wo_h[:, k, :].bitcast(F32),
                                            ALU.subtract).then_inc(wo_lo, 1)

            @block.scalar
            def _(act):
                for k in range(KD):
                    nc.scalar.activation(h_hi[:, k, :], mg[:, k, :], ACT.Copy).then_inc(mg_hi, 1)
                for t in range(NT):
                    act.wait_ge(o_ready, t + 1)
                    if t >= 1:
                        act.wait_ge(t_done, 2 * t)
                    for i in range(2):
                        b = banks[2 * (t % 2) + i]
                        nc.scalar.activation(mg[:, 0, i * HALF:(i + 1) * HALF], b[:], ACT.Square,
                                             accum_out=rr[:, i:i + 1]).then_inc(r_sq, 1)
                    act.wait_ge(r_done, 2 * t + 1)
                    nc.scalar.activation(rr[:, 0:1], rr[:, 0:1], ACT.Ln, scale=1.0 / D, bias=eps[:, 0:1]).then_inc(r_ln, 1)
                    act.wait_ge(r_ln, 2 * t + 1)
                    nc.scalar.activation(rr[:, 0:1], rr[:, 0:1], ACT.Exp, scale=-0.5).then_inc(r_ln, 1)

            @block.tensor
            def _(pe):
                pe.wait_ge(mg_hi, KD)
                pe.wait_ge(mg_lo, KD)
                for t in range(NT):
                    cut = slice(t * P, (t + 1) * P)
                    if t >= 2:
                        pe.wait_ge(t_done, 2 * (t - 1))
                    for k in range(KD):
                        if t == 0:
                            pe.wait_ge(wo_lo, k + 1)
                        for i in range(2):
                            c = slice(i * HALF, (i + 1) * HALF)
                            bank = banks[2 * (t % 2) + i][:]
                            nc.tensor.matmul(bank, h_hi[:, k, cut], wo_h[:, k, c], start=(k == 0), stop=False)
                            nc.tensor.matmul(bank, h_hi[:, k, cut], wo_l[:, k, c], start=False, stop=False)
                            last = nc.tensor.matmul(bank, h_lo[:, k, cut], wo_h[:, k, c], start=False,
                                                    stop=(k == KD - 1))
                    last.then_inc(o_ready, 1)
                    pe.wait_ge(x_in[t % 2], 16 * (t // 2 + 1))
                    if t >= 2:
                        pe.wait_ge(f_done, t - 1)
                    for k in range(KD):
                        last = nc.tensor.transpose(banks[4 + 2 * (t % 2) + k // 4][:, (k % 4) * P:(k % 4 + 1) * P],
                                                   xt[t % 2][:, k, :], ident[:])
                    last.then_inc(x_ready, 1)

            @block.vector
            def _(dve):
                for k in range(KD):
                    dve.wait_ge(wo_in, 16 * (k + 1))
                    nc.vector.tensor_copy(wo_h[:, k, :], w_raw[:]).then_inc(wo_hi, 1)
                    dve.wait_ge(mg_hi, k + 1)
                    nc.vector.tensor_tensor(h_lo[:, k, :], mg[:, k, :], h_hi[:, k, :].bitcast(F32),
                                            ALU.subtract).then_inc(mg_lo, 1)
                dve.wait_ge(cst, 32)
                for t in range(NT):
                    dve.wait_ge(r_sq, 2 * t + 2)
                    nc.vector.tensor_tensor(rr[:, 0:1], rr[:, 0:1], rr[:, 1:2], ALU.add).then_inc(r_done, 1)
                    dve.wait_ge(r_ln, 2 * t + 2)
                    if t >= 2:
                        dve.wait_ge(f_done, t - 1)
                    for i in range(2):
                        c = slice(i * HALF, (i + 1) * HALF)
                        nc.vector.scalar_tensor_tensor(tmp[t % 2][:, c], banks[2 * (t % 2) + i][:], rr[:, 0:1],
                                                       npost[:, c], ALU.mult, ALU.mult).then_inc(t_done, 1)
                    dve.wait_ge(t_done, 2 * t + 2)
                    dve.wait_ge(x_ready, t + 1)
                    if t >= 2:
                        dve.wait_ge(stored[t % 2], 16 * (t // 2))
                    for i in range(2):
                        c = slice(i * HALF, (i + 1) * HALF)
                        last = nc.vector.tensor_tensor(fin[t % 2][:, c], banks[4 + 2 * (t % 2) + i][:],
                                                       tmp[t % 2][:, c], ALU.add)
                        if i == 0:
                            last.then_inc(r_done, 1)
                    last.then_inc(f_done, 1)


def _tiles(w, starts, width=P):
    k = w.shape[0] // P
    out = []
    for cols in starts:
        pieces, at = [], 0
        for place, first, n in cols:
            if place > at:
                pieces.append(np.zeros((w.shape[0], place - at), w.dtype))
            pieces.append(w[:, first:first + n])
            at = place + n
        if at < width:
            pieces.append(np.zeros((w.shape[0], width - at), w.dtype))
        t = np.concatenate(pieces, axis=1)
        out.append(t.reshape(k, P, width).transpose(1, 0, 2).reshape(P, k * width))
    return np.ascontiguousarray(np.stack(out))


def _col(v):
    return np.ascontiguousarray(v.reshape(-1, P).transpose())


def _constants():
    s, t = np.meshgrid(np.arange(P), np.arange(P), indexing="ij")
    lev = np.zeros((P, LEVELS, P), np.float32)
    for l in range(LEVELS):
        n = 2 ** l
        lev[:, l, :] = (s // (2 * n) == t // (2 * n)) & (s % (2 * n) < n) & (t % (2 * n) >= n)
    q, c = np.meshgrid(np.arange(P), np.arange(T), indexing="ij")
    dist = q - (c - (T - P))
    alibi = np.stack([np.where(dist >= 0, 2.0 ** (-8.0 * (h + 1) / HA) * dist, -NEG) for h in range(HA)], axis=1)
    return {
        "ident": np.eye(P, dtype=np.float32),
        "ones": np.ones((P, P), np.float32),
        "tri": np.where(t >= s, 0.0, NEG).astype(np.float32),
        "lev": lev,
        "alibi": alibi.astype(np.float32),
    }


def _layout(inputs):
    a = {k: np.asarray(v) for k, v in inputs.items()}
    qk, vw = QK_HEADS * DH, V_HEADS * DH
    first = [[(0, 2 * qk + 2 * vw, 16), (32, 2 * qk + 2 * vw + 16, 16)]]
    conv = []
    for g in range(QK_HEADS):
        own = [g * P, qk + g * P, 2 * qk + 2 * g * P, 2 * qk + (2 * g + 1) * P]
        conv.append(own)
        first += [[(0, c, P)] for c in own]
        first += [[(0, 2 * qk + vw + (2 * g + q) * P, P)] for q in range(2)]
    cw = a["gdn_conv_w"][0]
    wa, wb = HA * 2 * DA, HB * DH
    gates2 = 4 * wa + 5 * wb
    at2 = {"qa": 0, "ka": wa, "va": 2 * wa, "za": 3 * wa, "qb": 4 * wa, "kb": 4 * wa + wb, "vb": 4 * wa + 2 * wb,
           "ob": 4 * wa + 3 * wb, "zb": 4 * wa + 4 * wb}
    second = [[(0, gates2 + HB, HB), (32, gates2, HB)]]
    second += [[(0, at2[name] + i * P, P)] for i in range(HB) for name in MIX_JOBS]
    win2, cqk = a["w_in_2"][0], a["conv_qk_2"][0]
    gate0 = gates2 + 2 * HB
    ga = _tiles(win2, [[(0, gate0 + c * P, P)] for c in range(KD)])
    gb = _tiles(win2, [[(0, gate0 + D + c * P, P)] for c in range(KD)])
    wab = np.concatenate([_tiles(a["w_a_2"][0], [[(0, c * P, P)] for c in range(KD)]),
                          _tiles(a["w_b_2"][0], [[(0, c * P, P)] for c in range(KD)])], axis=2)
    m = {
        "xT": a["x"][0].transpose().reshape(KD, P, T).transpose(1, 0, 2),
        "c": _col(a["c"][0]),
        "ada_w": _tiles(a["ada_w"][0], [[(0, n * P, P)] for n in range(3 * KD)]),
        "ada_b": _col(a["ada_b"][0]),
        "norm_g": _col(a["norm_g"][0]),
        "w1": _tiles(a["gdn_w_in"][0], first),
        "conv_w": np.stack([np.stack([cw[:, c:c + P].transpose() for c in own], axis=1) for own in conv], axis=1),
        "norm_w": _col(a["gdn_norm_w"][0]),
        "w_out": a["gdn_w_out"][0],
        "final_g": _col(a["final_g"]),
        "norm_pre": _col(a["norm_pre_2"][0]),
        "w2": _tiles(win2, second),
        "conv_w2": np.stack([np.stack([cqk[:, i * P:(i + 1) * P].transpose(),
                                       cqk[:, wb + i * P:wb + (i + 1) * P].transpose()], axis=1)
                             for i in range(HB)], axis=1),
        "bif": np.stack([a["b_if_2"][0, HB:], a["b_if_2"][0, :HB]], axis=1),
        "lq": a["lambda_qk_2"].reshape(1, 4 * DA),
        "w3": np.stack([ga, gb, wab], axis=1).reshape(3 * KD, P, KD * P),
        "norm_y": np.concatenate([_col(a["norm_a_2"][0]), _col(a["norm_b_2"][0])], axis=1),
        "w_out2": a["w_out_2"][0],
        "norm_post": a["norm_post_2"],
        "adt": np.stack([a["gdn_a_log"][0], a["gdn_dt_bias"][0]], axis=1),
    }
    m.update(_constants())
    return {k: np.ascontiguousarray(v) for k, v in m.items()}


def build(nc, io):
    with ExitStack() as ctx:
        def sb(name, shape, dt=F32):
            return ctx.enter_context(nc.sbuf_tensor(name, shape, dt))

        keep = {
            "ident": sb("ident", [P, P]), "ones": sb("ones", [P, P]), "eps": sb("eps", [P, 1]),
            "gate": sb("gate", [P, KD]),
            "h_hi": sb("h_hi", [P, KD, T], F32R), "h_lo": sb("h_lo", [P, KD, T], F32R),
            "const_in": ctx.enter_context(nc.semaphore("const_in")),
            "eps_set": ctx.enter_context(nc.semaphore("eps_set")),
        }
        stage_norm(nc, ctx, io, keep)
        with nc.cleanup_on_exit():
            stage_deltanet(nc, ctx, io, keep)
        stage_out(nc, ctx, io, keep)
        stage_mix(nc, ctx, io, keep)
        stage_merge(nc, ctx, io, keep)


SCRATCH = {
    "grows": (2 * V_HEADS, T),
    "z_scr": (V_HEADS, P, T),
    "o_scr": (V_HEADS, P, T),
    "x1_scr": (KD, P, T),
    "mrows": (2 * HB, T),
    "g_scr": (3 * HB, P, T),
    "a_scr": (HA + HB, P, T),
}


def kernel(**inputs):
    import concourse.bacc as bacc
    from concourse.bass_utils import run_bass_kernel_spmd

    arrays = _layout(inputs)
    nc = bacc.Bacc("TRN2", target_bir_lowering=False, num_devices=1)
    io = {}
    for name, a in arrays.items():
        io[name] = nc.dram_tensor("in_" + name, a.shape, F32, kind="ExternalInput").ap()
    for name, shape in SCRATCH.items():
        io[name] = nc.dram_tensor(name, shape, F32, kind="Internal").ap()
    io["out"] = nc.dram_tensor("out_x", (T, D), F32, kind="ExternalOutput").ap()
    build(nc, io)
    r = run_bass_kernel_spmd(nc, [{"in_" + name: a for name, a in arrays.items()}], core_ids=[0])
    return r.results[0]["out_x"].reshape(1, T, D)
```

```python
from contextlib import ExitStack

import numpy as np

import concourse.bass as bass
from concourse import mybir

F32 = mybir.dt.float32
F32R = mybir.dt.float32r
ALU = mybir.AluOpType
ACT = mybir.ActivationFunctionType
AX = mybir.AxisListType.X

P = 128
D = 1024
T = 1024
KD = D // P
NT = T // P
HALF = 512
EPS = 1e-6
QK_HEADS = 8
V_HEADS = 16
DH = 128
LEVELS = 7
HA, DA = 4, 64
HB = 4
TAPS = 4
NEG = -1.0e30
EXP_LN = "natural_log_exp_and_others"


def bc(ap, axis, n):
    ap = ap.unsqueeze(axis)
    shape = list(ap.shape)
    shape[axis] = n
    return ap.broadcast_to(shape)


def stage_norm(nc, ctx, io, keep):
    def sb(name, shape, dt=F32):
        return own.enter_context(nc.sbuf_tensor(name, shape, dt))

    own = ExitStack()
    with own:
        sem = lambda name: ctx.enter_context(nc.semaphore(name))
        RING = 4
        x_sb = sb("x_sb", [P, KD, T])
        ada = sb("ada", [P, RING, 3 * D])
        acc = sb("acc", [P, 3 * D])
        c_col = sb("c_col", [P, KD])
        cond = sb("cond", [P, KD])
        ada_b = sb("ada_b", [P, 3 * KD])
        g_col = sb("g_col", [P, KD])
        mod = sb("mod", [P, 2 * KD])
        gain = sb("gain", [P, KD])
        sq = sb("sq", [P, 2, T])
        rinv = sb("rinv", [P, T])
        h = sb("h", [P, 3, T])
        ps_ss = [own.enter_context(nc.psum_tensor(f"ps_ss{i}", [P, HALF], F32)) for i in range(2)]
        ps_mod = own.enter_context(nc.psum_tensor("ps_mod", [P, HALF], F32))
        ps_gate = own.enter_context(nc.psum_tensor("ps_gate", [P, HALF], F32))
        h_hi, h_lo = keep["h_hi"], keep["h_lo"]

        small_in = sem("a_small_in")
        x_in = [sem(f"a_x_in{i}") for i in range(KD)]
        ada_in = [sem(f"a_ada_in{i}") for i in range(RING)]
        const_in = keep["const_in"]
        eps_set = keep["eps_set"]
        cond_done = sem("a_cond_done")
        sq_done = sem("a_sq_done")
        ss_done = sem("a_ss_done")
        ln_done = sem("a_ln_done")
        rinv_done = sem("a_rinv_done")
        acc_done = sem("a_acc_done")
        mod_ready = sem("a_mod_ready")
        mod_done = sem("a_mod_done")
        xn_done = sem("a_xn_done")
        h_done = sem("a_h_done")
        hi_done = sem("a_hi_done")
        lo_done = [sem("a_lo_done0"), sem("a_lo_done1")]

        with nc.Block() as block:
            @block.sync
            def _(sp):
                for dst, src in ((c_col, io["c"]), (ada_b, io["ada_b"]), (g_col, io["norm_g"])):
                    sp.dma_start(dst[:], src).then_inc(small_in, 16)
                for dst, src in ((keep["ones"], io["ones"]), (keep["ident"], io["ident"])):
                    sp.dma_start(dst[:], src).then_inc(const_in, 16)
                for k in range(KD):
                    sp.dma_start(x_sb[:, k, :], io["xT"][:, k, :]).then_inc(x_in[k], 16)
                for k in range(KD):
                    if k >= RING:
                        sp.wait_ge(acc_done, 2 * (k - RING + 1))
                    sp.dma_start(ada[:, k % RING, :], io["ada_w"][k * P:(k + 1) * P, :]).then_inc(ada_in[k % RING], 16)
                for q in range(2):
                    sp.wait_ge(lo_done[q], KD // 2)

            @block.gpsimd
            def _(pool):
                for k in range(0, KD, 2):
                    pool.wait_ge(hi_done, k + 1)
                    nc.gpsimd.tensor_tensor(h_lo[:, k, :], h[:, k % 3, :],
                                            h_hi[:, k, :].bitcast(F32), ALU.subtract).then_inc(lo_done[0], 1)

            @block.scalar
            def _(act):
                act.wait_ge(small_in, 48)
                nc.scalar.activation(cond[:], c_col[:], ACT.Silu).then_inc(cond_done, 1)
                for k in range(KD):
                    act.wait_ge(x_in[k], 16)
                    if k >= 2:
                        act.wait_ge(ss_done, k - 1)
                    nc.scalar.activation(sq[:, k % 2, :], x_sb[:, k, :], ACT.Square).then_inc(sq_done, 1)
                nc.scalar.preload_act_table_set(EXP_LN)
                act.wait_ge(ss_done, KD)
                act.wait_ge(eps_set, 1)
                for i in range(2):
                    nc.scalar.activation(rinv[:, i * HALF:(i + 1) * HALF], ps_ss[i][:], ACT.Ln,
                                         scale=1.0 / D, bias=keep["eps"][:, 0:1]).then_inc(ln_done, 1)
                act.wait_ge(ln_done, 2)
                nc.scalar.activation(rinv[:], rinv[:], ACT.Exp, scale=-0.5).then_inc(rinv_done, 1)
                act.wait_ge(mod_done, 3)
                for k in range(KD):
                    act.wait_ge(xn_done, k + 1)
                    if k >= 3:
                        act.wait_ge(lo_done[(k - 3) % 2], (k - 3) // 2 + 1)
                    nc.scalar.activation(h[:, k % 3, :], x_sb[:, k, :], ACT.Identity,
                                         scale=gain[:, k:k + 1], bias=mod[:, k:k + 1]).then_inc(h_done, 1)

            @block.tensor
            def _(pe):
                pe.wait_ge(const_in, 32)
                for k in range(KD):
                    pe.wait_ge(sq_done, k + 1)
                    for i in range(2):
                        last = nc.tensor.matmul(ps_ss[i][:], keep["ones"][:], sq[:, k % 2, i * HALF:(i + 1) * HALF],
                                                start=(k == 0), stop=(k == KD - 1))
                    last.then_inc(ss_done, 1)
                for part, (bank, n) in enumerate(((ps_mod, 2 * KD), (ps_gate, KD))):
                    pe.wait_ge(acc_done, 2 * KD - 1 + part)
                    for m in range(n):
                        at = (2 * KD * part + m) * P
                        last = nc.tensor.matmul(bank[:, m:m + 1], acc[:, at:at + P], keep["ones"][:, 0:1],
                                                start=True, stop=True)
                    last.then_inc(mod_ready, 1)

            @block.vector
            def _(dve):
                def add_up(k):
                    dve.wait_ge(ada_in[k % RING], 16 * (k // RING + 1))
                    for part, cut in enumerate((slice(0, 2 * D), slice(2 * D, 3 * D))):
                        if k == 0:
                            nc.vector.tensor_scalar(acc[:, cut], ada[:, 0, cut], cond[:, 0:1], None, ALU.mult
                                                    ).then_inc(acc_done, 1)
                        else:
                            dve.wait_ge(acc_done, 2 * (k - 1) + part + 1)
                            nc.vector.scalar_tensor_tensor(acc[:, cut], ada[:, k % RING, cut], cond[:, k:k + 1],
                                                           acc[:, cut], ALU.mult, ALU.add).then_inc(acc_done, 1)

                nc.vector.memset(keep["eps"][:], EPS).then_inc(eps_set, 1)
                dve.wait_ge(cond_done, 1)
                add_up(0)
                add_up(1)
                dve.wait_ge(rinv_done, 1)
                for k in range(KD):
                    nc.vector.tensor_tensor(x_sb[:, k, :], x_sb[:, k, :], rinv[:], ALU.mult).then_inc(xn_done, 1)
                for k in range(2, KD):
                    add_up(k)
                dve.wait_ge(mod_ready, 1)
                nc.vector.tensor_tensor(mod[:], ps_mod[:, 0:2 * KD], ada_b[:, 0:2 * KD], ALU.add).then_inc(mod_done, 1)
                dve.wait_ge(mod_done, 1)
                nc.vector.tensor_scalar_add(gain[:], mod[:, KD:2 * KD], 1.0).then_inc(mod_done, 1)
                dve.wait_ge(mod_done, 2)
                nc.vector.tensor_tensor(gain[:], gain[:], g_col[:], ALU.mult).then_inc(mod_done, 1)
                for k in range(KD):
                    dve.wait_ge(h_done, k + 1)
                    nc.vector.tensor_copy(h_hi[:, k, :], h[:, k % 3, :]).then_inc(hi_done, 1)
                    if k % 2:
                        dve.wait_ge(hi_done, k + 1)
                        nc.vector.tensor_tensor(h_lo[:, k, :], h[:, k % 3, :], h_hi[:, k, :].bitcast(F32),
                                                ALU.subtract).then_inc(lo_done[1], 1)
                dve.wait_ge(mod_ready, 2)
                nc.vector.tensor_tensor(keep["gate"][:], ps_gate[:, 0:KD], ada_b[:, 2 * KD:3 * KD], ALU.add
                                        ).then_inc(mod_done, 1)


JOBS = 6


def plan(projects, recurs):
    jobs = (list(range(4)) if projects else []) + (list(range(4, JOBS)) if recurs else [])
    slices = [("slice", j, h, k) for j in jobs for h in range(2) for k in range(KD)]
    steps = []
    if recurs:
        steps += [("edge",), ("queries",)]
        for b in range(4):
            steps += [("gram", b), ("vcols", b), ("kcols", b)]
        steps += [("bcast",)]

        def levels(pair):
            def chain(b):
                out = [[("part", b, 0), ("unit", b), ("part", b, 1), ("turn", b, 0)]]
                for l in range(1, LEVELS):
                    out.append([("right", b, l)] + ([("part", b, l + 1)] if l < LEVELS - 1 else []))
                    out.append([("left", b, l)])
                    if l < LEVELS - 1:
                        out.append([("turn", b, l)])
                return out

            first, second = (chain(b) for b in pair)
            out = list(first[0])
            for i in range(1, len(first) + 1):
                out += (first[i] if i < len(first) else []) + second[i - 1]
            return out

        def chunk(c):
            return [("read", c), ("solve", c), ("write", c)]

        steps += levels((0, 1))
        later = levels((2, 3))
        second = [s for c in range(4) for s in chunk(c)]
        n = len(later) // len(second)
        for i, s in enumerate(second):
            steps += later[i * n:(i + 1) * n] + [s]
        steps += later[len(second) * n:]
        for c in range(4, NT):
            steps += chunk(c)
            if projects:
                steps += ([("dexp", c - 5)] if c > 4 else []) + [("decay", c - 4)]
        if projects:
            steps += [("dexp", 3)]
    else:
        steps += [("bcast",)] + [(what, b) for b in range(4) for what in ("decay", "dexp")]

    def weight(s):
        if s[0] in ("read", "solve", "write"):
            return 2 if s[1] >= 4 else 1
        return 1 if s[0] in ("gram", "vcols", "kcols", "right", "left", "turn") else 0

    if not recurs:
        weight = lambda s: s[0] in ("decay", "dexp")
    total = sum(weight(s) for s in steps)
    out, behind = [], []
    sent = passed = 0

    def finish(s):
        j, h = s[1:3]
        out.append(("evac", j, h))
        if h == 0:
            return
        if j < 4:
            for q in range(TAPS):
                behind.append((1 + q, ("tap", j, q)))
            behind.append((2 + TAPS, ("silu", j)))
        if j >= 4:
            out.append(("zstore", j))
        if j == 1:
            for m in range(4):
                w = (m // 2, m % 2)
                behind.append((8 + 5 * m, ("nsquare",) + w))
                behind.append((11 + 5 * m, ("nsum",) + w))
                behind.append((12 + 5 * m, ("norm",) + w))

    def send(upto):
        nonlocal sent, behind
        while sent < min(upto, len(slices)):
            s = slices[sent]
            if s[2:] == (0, 2):
                out.append(("weights", s[1]))
            out.append(s)
            sent += 1
            behind = [(n - 1, x) for n, x in behind]
            out.extend(x for n, x in sorted(behind, key=lambda e: e[0]) if n <= 0)
            behind = [(n, x) for n, x in behind if n > 0]
            if s[3] == KD - 1:
                finish(s)

    start = 2 if recurs else 2 * 2 * KD
    send(start)
    if not recurs:
        out.append(("gcols",))
    for s in steps:
        out.append(s)
        if weight(s):
            passed += weight(s)
            send(start + passed * (len(slices) - start) // total)
    send(len(slices))
    return out + [x for n, x in sorted(behind, key=lambda e: e[0])]


def ordinals(steps):
    seen, out = {}, {}
    for s in steps:
        out[s] = seen.get(s[0], 0)
        seen[s[0]] = out[s] + 1
    return out, seen


def stage_deltanet(nc, ctx, io, keep):
    own = ExitStack()
    with own:
        def sb(name, shape, dt=F32):
            return own.enter_context(nc.sbuf_tensor(name, shape, dt))

        def ps(name):
            return own.enter_context(nc.psum_tensor(name, [P, HALF], F32))

        sem = nc.alloc_semaphore
        h_hi, h_lo, ident, ones = keep["h_hi"], keep["h_lo"], keep["ident"], keep["ones"]

        w_raw = sb("w_raw", [P, KD * P])
        w_hi = sb("w_hi", [P, 2, KD * P], F32R)
        w_lo = sb("w_lo", [P, 2, KD * P], F32R)
        pre = sb("pre", [P, TAPS - 1 + T])
        conv_w = sb("conv_w", [P, QK_HEADS, 4, TAPS])
        qv = sb("qv", [P, 3, T])
        kT = sb("kT", [P, 2, T])
        nsq = sb("nsq", [P, HALF])
        nrm = sb("nrm", [P, HALF])
        rows = sb("rows", [P, 2, 2, T])
        qd = sb("qd", [P, 2, T])
        gam = sb("gam", [P, NT, 2, P])
        at = sb("at", [P, NT, 2, P])
        vb = sb("vb", [P, NT, 2, P])
        kd = sb("kd", [P, NT, 2, P])
        U = sb("U", [P, NT, 2, P])
        Ti = sb("Ti", [P, 2, HALF])
        Pr = sb("Pr", [P, 2, HALF])
        X = sb("X", [P, 2, 2, HALF])
        S = sb("S", [P, 2, P])
        Dl = sb("Dl", [P, 2, P])
        vn = sb("vn", [P, 2, P])
        oT = sb("oT", [P, 2, 2, P])
        tri = sb("tri", [P, P])
        lev = sb("lev", [P, LEVELS, P])
        cols = sb("cols", [P, NT, 64])
        eg = sb("eg", [P, NT, V_HEADS])
        nbe = sb("nbe", [P, NT, V_HEADS])
        edl = sb("edl", [P, NT, 2])
        gl = sb("gl", [P, NT, 2])
        adt = sb("adt", [P, 2])
        qbias = sb("qbias", [P, 2])

        p_job = [ps("p_job0"), ps("p_job1")]
        p_right, p_left, p_turn, p_pre = ps("p_right"), ps("p_left"), ps("p_turn"), ps("p_pre")
        p_read, p_write = ps("p_read"), ps("p_write")

        grow = vb[:].rearrange("p a b c -> p (a b c)")[:, 0:T]
        gt0 = vb[:].rearrange("p a b c -> p (a b c)")[:, T:2 * T]
        gt1 = kd[:].rearrange("p a b c -> p (a b c)")[:, 0:T]

        N_IT = QK_HEADS + 1
        N_JOBS = 1 + JOBS * QK_HEADS
        plans = [plan(True, False)] + [plan(True, True)] * (QK_HEADS - 1) + [plan(False, True)]
        order = [ordinals(p) for p in plans]

        cst = sem("b_cst")
        w_in = sem("b_w_in"); w_hi_done = sem("b_w_hi"); w_lo_done = sem("b_w_lo")
        half_done = sem("b_half"); evac_done = sem("b_evac"); conv_step = sem("b_conv")
        pad_set = sem("b_pad"); silu_done = sem("b_silu")
        nsq_done = sem("b_nsq"); nss_done = sem("b_nss"); nln = sem("b_nln"); nexp = sem("b_nexp"); nmul = sem("b_nmul")
        z_stored = sem("b_zst")
        g_act = sem("b_gact"); g_dve = sem("b_gdve"); g_pe = sem("b_gpe"); g_out = sem("b_gout")
        rows_in = sem("b_rows")
        diff_done = sem("b_diff"); mask_done = sem("b_mask"); decay_done = sem("b_decay"); dbeta_done = sem("b_dbeta")
        edge_dve = sem("b_edged"); edge_act = sem("b_edgea"); qexp = sem("b_qexp"); qd_done = sem("b_qd")
        gram_ready = sem("b_gram"); gram_used = sem("b_gramu")
        v_ready = sem("b_vr"); vb_done = sem("b_vb"); k_ready = sem("b_kr"); kd_done = sem("b_kd")
        part_done = sem("b_part"); right_ready = sem("b_right"); right_cp = sem("b_rightc")
        left_ready = sem("b_left"); u_done = sem("b_u"); turn_ready = sem("b_turn"); turn_cp = sem("b_turnc")
        read_ready = sem("b_read"); d_done = sem("b_d"); solve_ready = sem("b_solve"); vn_done = sem("b_vn")
        write_ready = sem("b_write"); s_done = sem("b_s"); o_done = sem("b_o")
        o_stored = [sem("b_os0"), sem("b_os1")]

        N_PART, N_LVL = 4 * LEVELS, 4 * (LEVELS - 1)

        def job(i, j):
            return JOBS * i - 1 + j - (4 if i == QK_HEADS else 0) if i else 1 + j

        def conv_dst(i, j):
            return (qv[:, 0, :], kT[:, i % 2, :], qv[:, 1, :], qv[:, 2, :])[j]

        def unit(t, b):
            return t[:, 2 * b:2 * b + 2, :, :].rearrange("p a b c -> p (a b c)")

        def u_ord(b, l):
            return b // 2 * 2 * LEVELS + 2 * l + b % 2

        with nc.Block() as block:
            @block.sync
            def _(sp):
                def load(J):
                    if J >= 1:
                        sp.wait_ge(w_lo_done, J)
                    sp.dma_start(w_raw[:], io["w1"][J]).then_inc(w_in, 16)

                load(0)
                for dst, src in ((tri[:], io["tri"]), (lev[:], io["lev"]), (conv_w[:], io["conv_w"]),
                                 (adt[32:48, :], io["adt"])):
                    sp.dma_start(dst, src).then_inc(cst, 16)
                load(1)
                load(2)
                for i in range(N_IT):
                    g = i - 1
                    o, n = order[i]
                    for s in plans[i]:
                        if s[0] == "weights" and 2 < job(i, s[1]) + 1 < N_JOBS:
                            load(job(i, s[1]) + 1)
                        elif s[0] == "bcast" and i < QK_HEADS:
                            if i == 0:
                                sp.wait_ge(g_dve, 13)
                                sp.dma_start(io["grows"][0:V_HEADS, :], grow[0:V_HEADS, :]).then_inc(g_out, 16)
                                sp.dma_start(io["grows"][V_HEADS:2 * V_HEADS, :], grow[32:48, :]).then_inc(g_out, 16)
                                sp.wait_ge(g_out, 32)
                            else:
                                sp.wait_ge(dbeta_done, 4 * i)
                                sp.wait_ge(qexp, i)
                                sp.wait_ge(edge_dve, i)
                                sp.wait_ge(edge_act, 2 * i)
                            for kind in range(2):
                                for a in range(2):
                                    r = kind * V_HEADS + 2 * i + a
                                    sp.dma_start(rows[:, kind, a, :], io["grows"][r:r + 1, :].broadcast_to([P, T])
                                                 ).then_inc(rows_in, 16)
                        elif s[0] == "zstore":
                            J = job(i, s[1])
                            sp.wait_ge(evac_done, 2 * J + 2)
                            sp.dma_start(io["z_scr"][2 * g + s[1] - 4], pre[:, TAPS - 1:]).then_inc(z_stored, 16)
                        elif s[0] == "write":
                            g, c = i - 1, s[1]
                            sp.wait_ge(o_done, NT * g + c + 1)
                            sp.dma_start(io["o_scr"][2 * g:2 * g + 2, :, c * P:(c + 1) * P].rearrange("a p t -> p a t"),
                                         oT[:, c % 2]).then_inc(o_stored[c % 2], 16)
                sp.wait_ge(z_stored, 16 * V_HEADS)
                for q in range(2):
                    sp.wait_ge(o_stored[q], 16 * QK_HEADS * NT // 2)

            @block.gpsimd
            def _(pool):
                def split_lo(J):
                    pool.wait_ge(w_hi_done, J + 1)
                    nc.gpsimd.tensor_tensor(w_lo[:, J % 2, :], w_raw[:], w_hi[:, J % 2, :].bitcast(F32),
                                            ALU.subtract).then_inc(w_lo_done, 1)

                split_lo(0)
                pool.wait_ge(cst, 64)
                split_lo(1)
                split_lo(2)
                for i in range(N_IT):
                    g = i - 1
                    o, n = order[i]
                    for s in plans[i]:
                        if s[0] == "weights" and 2 < job(i, s[1]) + 1 < N_JOBS:
                            split_lo(job(i, s[1]) + 1)
                        elif s[0] == "decay":
                            b = s[1]
                            pool.wait_ge(diff_done, 4 * i + b + 1)
                            x = gam[:, 2 * b:2 * b + 2].rearrange("p a b c -> p (a b) c")
                            nc.gpsimd.tensor_tensor(x, x, bc(tri[:], 1, 4), ALU.add).then_inc(mask_done, 1)
                        elif s[0] == "dexp":
                            b = s[1]
                            pool.wait_ge(decay_done, 4 * i + b + 1)
                            if i >= 1:
                                pool.wait_ge(part_done, N_PART * g + o[("part", b, LEVELS - 1)] + 1)
                            else:
                                pool.wait_ge(rows_in, 64)
                            for a in range(2):
                                last = nc.gpsimd.tensor_tensor(
                                    at[:, 2 * b:2 * b + 2, a, :], gam[:, 2 * b:2 * b + 2, a, :],
                                    rows[:, 0, a, 2 * b * P:(2 * b + 2) * P].rearrange("p (c t) -> p c t", c=2),
                                    ALU.mult)
                                if a == 1:
                                    last.then_inc(dbeta_done, 1)
                        elif s[0] == "queries":
                            pool.wait_ge(qexp, g + 1)
                            pool.wait_ge(nmul, 4 * (g + 1))
                            nc.gpsimd.tensor_tensor(qd[:], qd[:], bc(qv[:, 0, :], 1, 2), ALU.mult).then_inc(qd_done, 1)
                        elif s[0] == "part":
                            b, l = s[1:]
                            pool.wait_ge(gram_used, 2 * (4 * g + b) + 2)
                            if l > 2:
                                pool.wait_ge(right_ready, N_LVL * g + o[("right", b, l - 2)] + 1)
                            elif l == 2:
                                pool.wait_ge(u_done, N_PART * g + u_ord(b, 0) + 1)
                            elif l == 0 and b >= 2:
                                pool.wait_ge(right_ready, N_LVL * g + o[("right", b - 2, LEVELS - 1)] + 1)
                            elif l == 0 and g >= 1:
                                pool.wait_ge(right_ready, N_LVL * g)
                            nc.gpsimd.tensor_tensor(
                                X[:, b % 2, l % 2, :].rearrange("p (u t) -> p u t", u=4),
                                unit(at, b).rearrange("p (u t) -> p u t", u=4), bc(lev[:, l, :], 1, 4),
                                ALU.mult).then_inc(part_done, 1)

            @block.scalar
            def _(act):
                def evac(J, h, func=ACT.Copy):
                    act.wait_ge(half_done, 2 * J + h + 1)
                    nc.scalar.activation(pre[:, TAPS - 1 + h * HALF:TAPS - 1 + (h + 1) * HALF], p_job[h][:],
                                         func).then_inc(evac_done, 1)

                act.wait_ge(cst, 64)
                nc.scalar.preload_act_table_set(EXP_LN)
                nc.scalar.activation(adt[32:48, 0:1], adt[32:48, 0:1], ACT.Exp).then_inc(g_act, 1)
                act.wait_ge(pad_set, 4)
                evac(0, 0)
                evac(0, 1)
                act.wait_ge(evac_done, 2)
                nc.scalar.activation(gt0[0:16, :], pre[0:16, TAPS - 1:], ACT.Exp, scale=-1.0).then_inc(g_act, 1)
                nc.scalar.activation(gt0[32:48, :], pre[32:48, TAPS - 1:], ACT.Identity,
                                     bias=adt[32:48, 1:2]).then_inc(g_act, 1)
                act.wait_ge(g_dve, 3)
                nc.scalar.activation(gt1[32:48, :], gt1[32:48, :], ACT.Exp).then_inc(g_act, 1)
                act.wait_ge(g_act, 4)
                nc.scalar.activation(gt1[32:48, :], gt1[32:48, :], ACT.Ln, bias=1.0).then_inc(g_act, 1)

                for i in range(N_IT):
                    g = i - 1
                    o, n = order[i]
                    for s in plans[i]:
                        if s[0] == "evac":
                            j, h = s[1:]
                            J = job(i, j)
                            if h == 0:
                                if i == 0 and j == 0:
                                    act.wait_ge(g_act, 3)
                                elif i >= 2 and (j == 0 or (j == 4 and i == QK_HEADS)):
                                    act.wait_ge(z_stored, 16 * 2 * g)
                                elif j <= 4:
                                    act.wait_ge(conv_step, 16 * i + 4 * j)
                                else:
                                    act.wait_ge(z_stored, 16 * (2 * g + 1))
                            evac(J, h, ACT.Silu if j >= 4 else ACT.Copy)
                        elif s[0] == "gcols":
                            act.wait_ge(g_pe, 1)
                            nc.scalar.activation(cols[:].rearrange("p a b -> p (a b)"), p_turn[:], ACT.Copy
                                                 ).then_inc(g_act, 1)
                            act.wait_ge(g_act, 6)
                            nc.scalar.activation(eg[:], cols[:, :, 32:48], ACT.Exp).then_inc(g_act, 1)
                        elif s[0] == "tap" and s[2] == 0:
                            j = s[1]
                            dst = conv_dst(i, j)
                            act.wait_ge(evac_done, 2 * job(i, j) + 2)
                            if g >= 0:
                                act.wait_ge(gram_ready, 4 * (g + 1))
                                act.wait_ge(qd_done, g + 1)
                                act.wait_ge(v_ready, 4 * (g + 1))
                            if i >= 2 and j == 1:
                                act.wait_ge(read_ready, NT * (i - 1))
                            nc.scalar.activation(dst, pre[:, 0:T], ACT.Copy, scale=conv_w[:, i, j, 0:1]
                                                 ).then_inc(conv_step, 1)
                        elif s[0] == "silu":
                            j = s[1]
                            act.wait_ge(conv_step, 16 * i + 4 * (j + 1))
                            nc.scalar.activation(conv_dst(i, j), conv_dst(i, j), ACT.Silu).then_inc(silu_done, 1)
                        elif s[0] == "nsquare":
                            w, h = s[1:]
                            m = 4 * i + 2 * w + h
                            src = (qv[:, 0, :] if w == 0 else kT[:, i % 2, :])[:, h * HALF:(h + 1) * HALF]
                            act.wait_ge(silu_done, 4 * i + w + 1)
                            if m >= 1:
                                act.wait_ge(nss_done, m)
                            nc.scalar.activation(nsq[:], src, ACT.Square).then_inc(nsq_done, 1)
                        elif s[0] == "norm":
                            w, h = s[1:]
                            m = 4 * i + 2 * w + h
                            act.wait_ge(nss_done, m + 1)
                            if m >= 1:
                                act.wait_ge(nmul, m)
                            if m % 2 == 0:
                                nc.scalar.preload_act_table_set(EXP_LN)
                            nc.scalar.activation(nrm[:], p_pre[:], ACT.Ln, bias=keep["eps"][:, 0:1]).then_inc(nln, 1)
                            act.wait_ge(nln, m + 1)
                            nc.scalar.activation(nrm[:], nrm[:], ACT.Exp, scale=-0.5,
                                                 bias=qbias[:, w:w + 1]).then_inc(nexp, 1)
                        elif s[0] == "dexp":
                            b = s[1]
                            act.wait_ge(mask_done, 4 * i + b + 1)
                            nc.scalar.activation(unit(gam, b), unit(gam, b), ACT.Exp).then_inc(decay_done, 1)
                        elif s[0] == "edge":
                            act.wait_ge(edge_dve, g + 1)
                            nc.scalar.activation(edl[:], edl[:], ACT.Exp).then_inc(edge_act, 1)
                            if g >= 1:
                                act.wait_ge(s_done, 17 * g)
                            nc.scalar.activation(gl[:], rows[:, 1, :, P - 1::P].rearrange("p a c -> p c a"),
                                                 ACT.Exp).then_inc(edge_act, 1)
                        elif s[0] == "queries":
                            if g >= 1:
                                act.wait_ge(write_ready, NT * g)
                            act.wait_ge(rows_in, 64 * (g + 1))
                            nc.scalar.activation(qd[:], rows[:, 1, :, :], ACT.Exp).then_inc(qexp, 1)
                        elif s[0] == "right":
                            m = N_LVL * g + o[s]
                            b = s[1]
                            act.wait_ge(right_ready, m + 1)
                            if m >= 2:
                                act.wait_ge(left_ready, m - 1)
                            nc.scalar.activation(Pr[:, b % 2, :], p_right[:], ACT.Copy).then_inc(right_cp, 1)
                        elif s[0] == "turn":
                            m = N_LVL * g + o[s]
                            b = s[1]
                            act.wait_ge(turn_ready, m + 1)
                            if m >= 2:
                                act.wait_ge(right_ready, m - 1)
                            nc.scalar.activation(Ti[:, b % 2, :], p_turn[:], ACT.Copy).then_inc(turn_cp, 1)
                        elif s[0] == "solve":
                            m = NT * g + s[1]
                            act.wait_ge(solve_ready, m + 1)
                            if m >= 1:
                                act.wait_ge(write_ready, m)
                            nc.scalar.activation(vn[:].rearrange("p a c -> p (a c)"), p_read[:, 256:512],
                                                 ACT.Copy).then_inc(vn_done, 1)
                        elif s[0] == "write":
                            c = s[1]
                            m = NT * g + c
                            act.wait_ge(write_ready, m + 1)
                            if m >= 2:
                                act.wait_ge(o_stored[c % 2], 16 * (m // 2))
                            nc.scalar.activation(oT[:, c % 2].rearrange("p a c -> p (a c)"), p_read[:, 0:256],
                                                 ACT.Copy).then_inc(o_done, 1)

            @block.tensor
            def _(pe):
                def piece(J, h, k):
                    if h == 0 and k == 0:
                        pe.wait_ge(w_lo_done, J + 1)
                    if k == 0 and J >= 1:
                        pe.wait_ge(evac_done, 2 * (J - 1) + h + 1)
                    cut = slice(h * HALF, (h + 1) * HALF)
                    hi, lo = w_hi[:, J % 2, k * P:(k + 1) * P], w_lo[:, J % 2, k * P:(k + 1) * P]
                    nc.tensor.matmul(p_job[h][:], hi, h_hi[:, k, cut], start=(k == 0), stop=False)
                    nc.tensor.matmul(p_job[h][:], hi, h_lo[:, k, cut], start=False, stop=False)
                    last = nc.tensor.matmul(p_job[h][:], lo, h_hi[:, k, cut], start=False, stop=(k == KD - 1))
                    if k == KD - 1:
                        last.then_inc(half_done, 1)

                for h in range(2):
                    for k in range(KD):
                        piece(0, h, k)
                for i in range(N_IT):
                    g = i - 1
                    o, n = order[i]
                    for s in plans[i]:
                        if s[0] == "slice":
                            piece(job(i, s[1]), s[2], s[3])
                        elif s[0] == "gcols":
                            pe.wait_ge(g_dve, 13)
                            for t in range(NT):
                                last = nc.tensor.transpose(p_turn[:, 64 * t:64 * (t + 1)],
                                                           grow[0:64, t * P:(t + 1) * P], ident[0:64, 0:64])
                            last.then_inc(g_pe, 1)
                        elif s[0] == "nsum":
                            m = 4 * i + 2 * s[1] + s[2]
                            pe.wait_ge(nsq_done, m + 1)
                            if m >= 1:
                                pe.wait_ge(nln, m)
                            if g >= 0:
                                pe.wait_ge(kd_done, 4 * (g + 1))
                            nc.tensor.matmul(p_pre[:], ones[:], nsq[:], start=True, stop=True).then_inc(nss_done, 1)
                        elif s[0] == "gram":
                            b = s[1]
                            pe.wait_ge(nmul, 4 * (g + 1))
                            if b >= 1:
                                pe.wait_ge(kd_done, 4 * g + b)
                            for t in range(2):
                                c = slice((2 * b + t) * P, (2 * b + t + 1) * P)
                                nc.tensor.matmul(p_pre[:, 256 * t:256 * t + P], kT[:, g % 2, c], kT[:, g % 2, c],
                                                 start=True, stop=True)
                                last = nc.tensor.matmul(p_pre[:, 256 * t + P:256 * t + 2 * P], kT[:, g % 2, c],
                                                        qv[:, 0, c], start=True, stop=True)
                            last.then_inc(gram_ready, 1)
                        elif s[0] == "vcols":
                            b = s[1]
                            pe.wait_ge(silu_done, 4 * (g + 1))
                            if b >= 1:
                                pe.wait_ge(vb_done, 4 * g + b)
                            elif g >= 1:
                                pe.wait_ge(turn_cp, N_LVL * g)
                            else:
                                pe.wait_ge(g_act, 6)
                            for t in range(2):
                                for a in range(2):
                                    last = nc.tensor.transpose(
                                        p_turn[:, (2 * t + a) * P:(2 * t + a + 1) * P],
                                        qv[:, 1 + a, (2 * b + t) * P:(2 * b + t + 1) * P], ident[:])
                            last.then_inc(v_ready, 1)
                        elif s[0] == "kcols":
                            b = s[1]
                            pe.wait_ge(gram_used, 2 * (4 * g + b) + 2)
                            for t in range(2):
                                last = nc.tensor.transpose(p_pre[:, t * P:(t + 1) * P],
                                                           kT[:, g % 2, (2 * b + t) * P:(2 * b + t + 1) * P], ident[:])
                            last.then_inc(k_ready, 1)
                        elif s[0] == "right":
                            b, l = s[1:]
                            m = N_LVL * g + o[s]
                            pe.wait_ge(part_done, N_PART * g + o[("part", b, l)] + 1)
                            pe.wait_ge(turn_cp, N_LVL * g + o[("turn", b, l - 1)] + 1)
                            if m >= 1:
                                pe.wait_ge(right_cp, m)
                            for u in range(4):
                                c = slice(u * P, (u + 1) * P)
                                last = nc.tensor.matmul(p_right[:, c], X[:, b % 2, l % 2, c], Ti[:, b % 2, c],
                                                        start=True, stop=True)
                            last.then_inc(right_ready, 1)
                        elif s[0] == "left":
                            b, l = s[1:]
                            m = N_LVL * g + o[s]
                            pe.wait_ge(right_cp, N_LVL * g + o[("right", b, l)] + 1)
                            pe.wait_ge(u_done, N_PART * g + u_ord(b, l))
                            for u in range(4):
                                c = slice(u * P, (u + 1) * P)
                                last = nc.tensor.matmul(p_left[:, c], Pr[:, b % 2, c], unit(U, b)[:, c],
                                                        start=True, stop=True)
                            last.then_inc(left_ready, 1)
                        elif s[0] == "turn":
                            b, l = s[1:]
                            m = N_LVL * g + o[s]
                            pe.wait_ge(u_done, N_PART * g + u_ord(b, l) + 1)
                            if o[s] >= 1:
                                pe.wait_ge(turn_cp, m)
                            else:
                                pe.wait_ge(vb_done, 4 * (g + 1))
                            for u in range(4):
                                c = slice(u * P, (u + 1) * P)
                                last = nc.tensor.transpose(p_turn[:, c], unit(U, b)[:, c], ident[:])
                            last.then_inc(turn_ready, 1)
                        elif s[0] == "read":
                            c = s[1]
                            m = NT * g + c
                            pe.wait_ge(s_done, 17 * g + 1 + 2 * c)
                            if m >= 1:
                                pe.wait_ge(o_done, m)
                            nc.tensor.matmul(p_read[:, 0:256], kT[:, g % 2, c * P:(c + 1) * P],
                                             S[:].rearrange("p a c -> p (a c)"), start=True, stop=True
                                             ).then_inc(read_ready, 1)
                        elif s[0] == "solve":
                            c = s[1]
                            m = NT * g + c
                            pe.wait_ge(d_done, 2 * m + 2)
                            pe.wait_ge(u_done, N_PART * g + u_ord(c // 2, LEVELS - 1) + 1)
                            for a in range(2):
                                last = nc.tensor.matmul(p_read[:, 256 + a * P:256 + (a + 1) * P], U[:, c, a, :],
                                                        Dl[:, a, :], start=True, stop=True)
                            last.then_inc(solve_ready, 1)
                        elif s[0] == "write":
                            c = s[1]
                            m = NT * g + c
                            pe.wait_ge(vn_done, m + 1)
                            pe.wait_ge(qd_done, g + 1)
                            pe.wait_ge(kd_done, 4 * (g + 1))
                            if m >= 1:
                                pe.wait_ge(s_done, 17 * g + 1 + 2 * c)
                            for a in range(2):
                                nc.tensor.matmul(p_write[:, a * P:(a + 1) * P], kd[:, c, a, :], vn[:, a, :],
                                                 start=True, stop=True)
                            for a in range(2):
                                nc.tensor.matmul(p_read[:, a * P:(a + 1) * P], S[:, a, :],
                                                 qd[:, a, c * P:(c + 1) * P], start=True, stop=False)
                                last = nc.tensor.matmul(p_read[:, a * P:(a + 1) * P], vn[:, a, :], gam[:, c, a, :],
                                                        start=False, stop=True)
                            last.then_inc(write_ready, 1)

            @block.vector
            def _(dve):
                def split_hi(J):
                    dve.wait_ge(w_in, 16 * (J + 1))
                    if J >= 2:
                        dve.wait_ge(half_done, 2 * (J - 1))
                    nc.vector.tensor_copy(w_hi[:, J % 2, :], w_raw[:]).then_inc(w_hi_done, 1)

                nc.vector.memset(pre[:, 0:TAPS - 1], 0.0).then_inc(pad_set, 1)
                nc.vector.memset(qbias[:, 0:1], float(np.log(DH ** -0.5))).then_inc(pad_set, 1)
                nc.vector.memset(qbias[:, 1:2], 0.0).then_inc(pad_set, 1)
                nc.vector.memset(grow, 0.0).then_inc(pad_set, 1)
                split_hi(0)
                dve.wait_ge(cst, 64)
                split_hi(1)

                dve.wait_ge(g_act, 2)
                nc.vector.tensor_scalar_add(gt0[0:16, :], gt0[0:16, :], 1.0).then_inc(g_dve, 1)
                dve.wait_ge(g_dve, 1)
                dve.wait_ge(pad_set, 4)
                split_hi(2)
                nc.vector.reciprocal(grow[0:16, :], gt0[0:16, :]).then_inc(g_dve, 1)
                dve.wait_ge(g_act, 3)
                nc.vector.scalar_tensor_tensor(gt1[32:48, :], gt0[32:48, :], -1.0, gt0[32:48, :],
                                               ALU.mult, ALU.min).then_inc(g_dve, 1)
                dve.wait_ge(g_act, 5)
                nc.vector.scalar_tensor_tensor(gt0[32:48, :], gt0[32:48, :], 0.0, gt1[32:48, :],
                                               ALU.max, ALU.add).then_inc(g_dve, 1)
                dve.wait_ge(g_dve, 4)
                nc.vector.tensor_scalar(gt0[32:48, :], gt0[32:48, :], adt[32:48, 0:1], -1.0,
                                        ALU.mult, ALU.mult).then_inc(g_dve, 1)
                dve.wait_ge(g_dve, 5)
                for t in range(NT):
                    c = slice(t * P, (t + 1) * P)
                    nc.vector.tensor_tensor_scan(grow[32:48, c], ones[32:48, :], gt0[32:48, c], 0.0,
                                                 ALU.mult, ALU.add).then_inc(g_dve, 1)

                for i in range(N_IT):
                    g = i - 1
                    o, n = order[i]
                    for s in plans[i]:
                        if s[0] == "weights" and 2 < job(i, s[1]) + 1 < N_JOBS:
                            split_hi(job(i, s[1]) + 1)
                        elif s[0] == "gcols":
                            dve.wait_ge(g_act, 7)
                            nc.vector.scalar_tensor_tensor(nbe[:], cols[:, :, 0:16], -1.0, eg[:],
                                                           ALU.mult, ALU.mult).then_inc(g_dve, 1)
                        elif s[0] == "tap" and s[2]:
                            j, q = s[1:]
                            dst = conv_dst(i, j)
                            dve.wait_ge(conv_step, 16 * i + 4 * j + q)
                            nc.vector.scalar_tensor_tensor(dst, pre[:, q:q + T], conv_w[:, i, j, q:q + 1], dst,
                                                           ALU.mult, ALU.add).then_inc(conv_step, 1)
                        elif s[0] == "norm":
                            w, h = s[1:]
                            m = 4 * i + 2 * w + h
                            src = (qv[:, 0, :] if w == 0 else kT[:, i % 2, :])[:, h * HALF:(h + 1) * HALF]
                            dve.wait_ge(nexp, m + 1)
                            nc.vector.tensor_tensor(src, src, nrm[:], ALU.mult).then_inc(nmul, 1)
                        elif s[0] == "decay":
                            b = s[1]
                            dve.wait_ge(rows_in, 64 * (i + 1))
                            if i >= 1:
                                dve.wait_ge(write_ready, NT * g + 2 * b + 2)
                            else:
                                dve.wait_ge(g_act, 6)
                            for a in range(2):
                                last = nc.vector.tensor_tensor(
                                    gam[:, 2 * b:2 * b + 2, a, :],
                                    rows[:, 1, a, 2 * b * P:(2 * b + 2) * P].rearrange("p (c t) -> p c t", c=2),
                                    bc(cols[:, 2 * b:2 * b + 2, 32 + 2 * i + a], 2, P), ALU.subtract)
                            last.then_inc(diff_done, 1)
                        elif s[0] == "edge":
                            if g >= 1:
                                dve.wait_ge(kd_done, 4 * g)
                                dve.wait_ge(s_done, 17 * g)
                                dve.wait_ge(write_ready, NT * g)
                            nc.vector.tensor_tensor(
                                edl[:], rows[:, 1, :, P - 1::P].rearrange("p a c -> p c a"),
                                cols[:, :, 32 + 2 * g:34 + 2 * g], ALU.subtract).then_inc(edge_dve, 1)
                            nc.vector.memset(S[:], 0.0).then_inc(s_done, 1)
                        elif s[0] == "gram":
                            b = s[1]
                            dve.wait_ge(gram_ready, 4 * g + b + 1)
                            dve.wait_ge(dbeta_done, 4 * g + b + 1)
                            pk = p_pre[:].rearrange("p (t k c) -> p t k c", t=2, k=2)
                            nc.vector.tensor_tensor(at[:, 2 * b:2 * b + 2], bc(pk[:, :, 0, :], 2, 2),
                                                    at[:, 2 * b:2 * b + 2], ALU.mult).then_inc(gram_used, 1)
                            nc.vector.tensor_tensor(gam[:, 2 * b:2 * b + 2], bc(pk[:, :, 1, :], 2, 2),
                                                    gam[:, 2 * b:2 * b + 2], ALU.mult).then_inc(gram_used, 1)
                        elif s[0] == "vcols":
                            b = s[1]
                            dve.wait_ge(v_ready, 4 * g + b + 1)
                            if g == 0:
                                dve.wait_ge(g_out, 32)
                            nc.vector.tensor_tensor(
                                vb[:, 2 * b:2 * b + 2], p_turn[:].rearrange("p (t a c) -> p t a c", t=2, a=2),
                                bc(cols[:, 2 * b:2 * b + 2, 2 * g:2 * g + 2], 3, P), ALU.mult).then_inc(vb_done, 1)
                        elif s[0] == "kcols":
                            b = s[1]
                            dve.wait_ge(k_ready, 4 * g + b + 1)
                            dve.wait_ge(edge_act, 2 * g + 1)
                            nc.vector.tensor_tensor(
                                kd[:, 2 * b:2 * b + 2],
                                bc(p_pre[:, 0:256].rearrange("p (t c) -> p t c", t=2), 2, 2),
                                bc(edl[:, 2 * b:2 * b + 2, :], 3, P), ALU.mult).then_inc(kd_done, 1)
                        elif s[0] == "unit":
                            b = s[1]
                            dve.wait_ge(part_done, N_PART * g + o[("part", b, 0)] + 1)
                            if g >= 1:
                                dve.wait_ge(solve_ready, NT * g)
                            nc.vector.tensor_tensor(unit(U, b).rearrange("p (u t) -> p u t", u=4), bc(ident[:], 1, 4),
                                                    X[:, b % 2, 0, :].rearrange("p (u t) -> p u t", u=4),
                                                    ALU.subtract).then_inc(u_done, 1)
                        elif s[0] == "left":
                            b, l = s[1:]
                            dve.wait_ge(left_ready, N_LVL * g + o[s] + 1)
                            nc.vector.tensor_tensor(unit(U, b), unit(U, b), p_left[:], ALU.subtract).then_inc(u_done, 1)
                        elif s[0] == "read":
                            c = s[1]
                            m = NT * g + c
                            dve.wait_ge(read_ready, m + 1)
                            dve.wait_ge(vb_done, 4 * (g + 1))
                            dve.wait_ge(g_dve, 14)
                            if m >= 1:
                                dve.wait_ge(solve_ready, m)
                            for a in range(2):
                                hd = 2 * g + a
                                nc.vector.scalar_tensor_tensor(Dl[:, a, :], p_read[:, a * P:(a + 1) * P],
                                                               nbe[:, c, hd:hd + 1], vb[:, c, a, :],
                                                               ALU.mult, ALU.add).then_inc(d_done, 1)
                        elif s[0] == "write":
                            c = s[1]
                            m = NT * g + c
                            dve.wait_ge(write_ready, m + 1)
                            dve.wait_ge(edge_act, 2 * g + 2)
                            dve.wait_ge(s_done, 17 * g + 1 + 2 * c)
                            for a in range(2):
                                nc.vector.scalar_tensor_tensor(S[:, a, :], S[:, a, :], gl[:, c, a:a + 1],
                                                               p_write[:, a * P:(a + 1) * P],
                                                               ALU.mult, ALU.add).then_inc(s_done, 1)


CH_PASS = (3, 3, 2)


def stage_out(nc, ctx, io, keep):
    own = ExitStack()
    with own:
        def sb(name, shape, dt=F32):
            return own.enter_context(nc.sbuf_tensor(name, shape, dt))

        sem = nc.alloc_semaphore
        h_hi, h_lo, ones, eps, ident = (keep[n] for n in ("h_hi", "h_lo", "ones", "eps", "ident"))
        y2_hi = sb("y2_hi", [P, V_HEADS - KD, T], F32R)
        y2_lo = sb("y2_lo", [P, V_HEADS - KD, T], F32R)
        x1 = sb("x1", [P, KD, T])
        W3 = 3 * P
        w_raw = sb("wo_raw", [P, 2, W3])
        w_hi = sb("wo_hi", [P, 2, W3], F32R)
        w_lo = sb("wo_lo", [P, 2, W3], F32R)
        ob = sb("ob", [P, 3, T])
        zb = sb("zb", [P, 3, T])
        sq = sb("sq3", [P, 2, T])
        rinv = sb("rinv3", [P, T])
        nw = sb("nw", [P, 1])
        fg = sb("fg", [P, KD])
        np_col = sb("np_col", [P, KD])
        fn = sb("fn", [P, KD])
        p_out = [own.enter_context(nc.psum_tensor(f"p_out{i}", [P, HALF], F32)) for i in range(6)]
        p_ss = [own.enter_context(nc.psum_tensor(f"p_ss{i}", [P, HALF], F32)) for i in range(2)]

        p_s2 = p_out[4:6]
        rin2 = ob[:, 0, :]
        total = ob[:, 1:3, :]
        hn = [zb[:, q, :] for q in range(3)]

        def y(part, n):
            low, high = ((h_hi, y2_hi), (h_lo, y2_lo))[part]
            return low[:, n, :] if n < KD else high[:, n - KD, :]

        cst = sem("c_cst"); x_in = sem("c_x"); oz_in = [sem(f"c_oz{q}") for q in range(3)]
        sq_done = sem("c_sq"); ss_done = sem("c_ss"); ln_done = sem("c_ln"); rinv_done = sem("c_rinv")
        gz_done = sem("c_gz"); y_done = sem("c_y"); yhi_done = sem("c_yhi"); ylo_done = sem("c_ylo")
        w_in = [sem("c_w0"), sem("c_w1")]; whi_done = sem("c_whi"); wlo_done = sem("c_wlo"); w_used = sem("c_wu")
        pass_done = sem("c_pass"); bank_used = sem("c_bank")
        sq2 = sem("c_sq2"); ss2 = sem("c_ss2"); ln2 = sem("c_ln2"); ri2 = sem("c_ri2"); xn2 = sem("c_xn2"); ms2 = sem("c_ms2")
        hh = sem("c_hh"); hhi = sem("c_hhi"); hlo = [sem("c_hlo0"), sem("c_hlo1")]; fn_set = sem("c_fn"); added = sem("c_add"); rt_ready = sem("c_rt"); rc_done = sem("c_rc"); x1_out = sem("c_x1o")
        steps = [(q, n) for q in range(len(CH_PASS)) for n in range(V_HEADS)]
        first_ch = [sum(CH_PASS[:q]) for q in range(len(CH_PASS))]

        with nc.Block() as block:
            @block.sync
            def _(sp):
                for dst, src in ((nw, io["norm_w"]), (fg, io["final_g"]), (np_col, io["norm_pre"])):
                    sp.dma_start(dst[:], src).then_inc(cst, 16)

                def load_w(m):
                    q, n = steps[m]
                    c0, cn = first_ch[q] * P, CH_PASS[q] * P
                    if m >= 2:
                        sp.wait_ge(wlo_done, m - 1)
                    sp.dma_start(w_raw[:, m % 2, 0:cn], io["w_out"][n * P:(n + 1) * P, c0:c0 + cn]
                                 ).then_inc(w_in[m % 2], 16)

                for m in range(len(steps)):
                    if m < V_HEADS:
                        if m >= 3:
                            sp.wait_ge(ylo_done, m - 2)
                        sp.dma_start(ob[:, m % 3, :], io["o_scr"][m]).then_inc(oz_in[m % 3], 16)
                        sp.dma_start(zb[:, m % 3, :], io["z_scr"][m]).then_inc(oz_in[m % 3], 16)
                    if m == 2:
                        sp.dma_start(x1[:], io["xT"]).then_inc(x_in, 16)
                    load_w(m)
                for k in range(KD):
                    sp.wait_ge(bank_used, 2 * (k + 1))
                    sp.dma_start(io["x1_scr"][k], x1[:, k, :]).then_inc(x1_out, 16)
                sp.wait_ge(x1_out, 16 * KD)
                for q in range(2):
                    sp.wait_ge(hlo[q], KD // 2)

            @block.gpsimd
            def _(pool):
                def add_squares(k):
                    for r in range(2):
                        pool.wait_ge(sq2, 2 * k + r + 1)
                        if k >= 2:
                            pool.wait_ge(added, 2 * (k - 2) + r + 1)
                        if k:
                            nc.gpsimd.tensor_tensor(total[:, r, :], total[:, r, :], sq[:, r, :], ALU.add
                                                    ).then_inc(added, 1)

                for m, (q, n) in enumerate(steps):
                    cn = CH_PASS[q] * P
                    if q == 2 and 4 <= n < 4 + first_ch[2]:
                        add_squares(n - 4)
                    if q == 0:
                        pool.wait_ge(yhi_done, n + 1)
                        nc.gpsimd.tensor_tensor(y(1, n), zb[:, n % 3, :], y(0, n).bitcast(F32),
                                                ALU.subtract).then_inc(ylo_done, 1)
                    pool.wait_ge(whi_done, m + 1)
                    nc.gpsimd.tensor_tensor(w_lo[:, m % 2, 0:cn], w_raw[:, m % 2, 0:cn],
                                            w_hi[:, m % 2, 0:cn].bitcast(F32), ALU.subtract).then_inc(wlo_done, 1)
                for k in range(first_ch[2], KD):
                    add_squares(k)
                for k in range(0, KD, 2):
                    pool.wait_ge(hhi, k + 1)
                    nc.gpsimd.tensor_tensor(h_lo[:, k, :], hn[k % 3], h_hi[:, k, :].bitcast(F32),
                                            ALU.subtract).then_inc(hlo[0], 1)

            @block.scalar
            def _(act):
                def squares(k):
                    act.wait_ge(bank_used, 2 * (k + 1))
                    for r in range(2):
                        if k >= 2:
                            act.wait_ge(added, 2 * (k - 2) + r + 1)
                        else:
                            act.wait_ge(ylo_done, V_HEADS)
                            act.wait_ge(ss_done, V_HEADS)
                        dst = sq[:, r, :] if k else total[:, r, :]
                        nc.scalar.activation(dst, x1[:, k, :], ACT.Square,
                                             scale=(fg[:, k:k + 1] if r else 1.0)).then_inc(sq2, 1)

                nc.scalar.preload_act_table_set(EXP_LN)
                for n in range(V_HEADS + 1):
                    if n < V_HEADS:
                        act.wait_ge(oz_in[n % 3], 32 * (n // 3 + 1))
                        if n >= 2:
                            act.wait_ge(ss_done, n - 1)
                        nc.scalar.activation(sq[:, n % 2, :], ob[:, n % 3, :], ACT.Square).then_inc(sq_done, 1)
                    if n >= 1:
                        m = n - 1
                        act.wait_ge(ss_done, m + 1)
                        if m >= 1:
                            act.wait_ge(y_done, m)
                        for i in range(2):
                            nc.scalar.activation(rinv[:, i * HALF:(i + 1) * HALF], p_ss[i][:], ACT.Ln,
                                                 scale=1.0 / DH, bias=eps[:, 0:1]).then_inc(ln_done, 1)
                        act.wait_ge(ln_done, 2 * m + 2)
                        nc.scalar.activation(rinv[:], rinv[:], ACT.Exp, scale=-0.5).then_inc(rinv_done, 1)
                for k in range(KD):
                    squares(k)
                act.wait_ge(y_done, V_HEADS)
                act.wait_ge(ss2, 2)
                for i in range(2):
                    nc.scalar.activation(rinv[:, i * HALF:(i + 1) * HALF], p_ss[i][:], ACT.Ln, scale=1.0 / D,
                                         bias=eps[:, 0:1]).then_inc(ln2, 1)
                act.wait_ge(ln2, 2)
                nc.scalar.activation(rinv[:], rinv[:], ACT.Exp, scale=-0.5).then_inc(ri2, 1)
                act.wait_ge(ms2, 3)
                nc.scalar.activation(rin2, rin2, ACT.Ln, bias=eps[:, 0:1]).then_inc(ln2, 1)
                act.wait_ge(ln2, 3)
                nc.scalar.activation(rin2, rin2, ACT.Exp, scale=-0.5).then_inc(ri2, 1)
                act.wait_ge(rt_ready, 1)
                for i in range(2):
                    nc.scalar.activation(keep["rin_col"][:, 4 * i:4 * i + 4], p_out[i][:, 0::P], ACT.Copy
                                         ).then_inc(rc_done, 1)
                for k in range(KD):
                    act.wait_ge(hh, k + 1)
                    nc.scalar.activation(h_hi[:, k, :], hn[k % 3], ACT.Copy).then_inc(hhi, 1)

            @block.tensor
            def _(pe):
                def sums(n):
                    pe.wait_ge(sq_done, n + 1)
                    if n >= 1:
                        pe.wait_ge(ln_done, 2 * n)
                    for i in range(2):
                        last = nc.tensor.matmul(p_ss[i][:], ones[:], sq[:, n % 2, i * HALF:(i + 1) * HALF],
                                                start=True, stop=True)
                    last.then_inc(ss_done, 1)

                sums(0)
                for m, (q, n) in enumerate(steps):
                    if q == 0 and n + 1 < V_HEADS:
                        sums(n + 1)
                    pe.wait_ge(ylo_done, n + 1)
                    pe.wait_ge(wlo_done, m + 1)
                    for c in range(CH_PASS[q]):
                        hi, lo = w_hi[:, m % 2, c * P:(c + 1) * P], w_lo[:, m % 2, c * P:(c + 1) * P]
                        for i in range(2):
                            bank = p_out[2 * c + i]
                            if q and n == 0:
                                pe.wait_ge(bank_used, 2 * first_ch[q - 1] + 2 * c + i + 1)
                            cut = slice(i * HALF, (i + 1) * HALF)
                            nc.tensor.matmul(bank[:], hi, y(0, n)[:, cut], start=(n == 0), stop=False)
                            nc.tensor.matmul(bank[:], hi, y(1, n)[:, cut], start=False, stop=False)
                            last = nc.tensor.matmul(bank[:], lo, y(0, n)[:, cut], start=False,
                                                    stop=(n == V_HEADS - 1))
                    last.then_inc(w_used, 1)
                for r, bank in enumerate((p_ss, p_s2)):
                    pe.wait_ge(added, 2 * (KD - 1) - 1 + r)
                    pe.wait_ge(ln_done, 2 * V_HEADS) if r == 0 else pe.wait_ge(bank_used, 2 * first_ch[2])
                    for i in range(2):
                        last = nc.tensor.matmul(bank[i][:], ones[:], total[:, r, i * HALF:(i + 1) * HALF],
                                                start=True, stop=True)
                    last.then_inc(ss2, 1)
                pe.wait_ge(ri2, 1)
                pe.wait_ge(bank_used, 2 * KD)
                for t in range(NT):
                    last = nc.tensor.transpose(p_out[t // 4][:, (t % 4) * P:(t % 4 + 1) * P],
                                               rinv[:, t * P:(t + 1) * P], ident[:])
                last.then_inc(rt_ready, 1)

            @block.vector
            def _(dve):
                def drain(q):
                    dve.wait_ge(w_used, V_HEADS * (q + 1))
                    dve.wait_ge(x_in, 16)
                    for c in range(CH_PASS[q]):
                        ch = first_ch[q] + c
                        for i in range(2):
                            cut = slice(i * HALF, (i + 1) * HALF)
                            nc.vector.scalar_tensor_tensor(x1[:, ch, cut], p_out[2 * c + i][:],
                                                           keep["gate"][:, ch:ch + 1], x1[:, ch, cut],
                                                           ALU.mult, ALU.add).then_inc(bank_used, 1)

                def low(k):
                    dve.wait_ge(hhi, k + 1)
                    nc.vector.tensor_tensor(h_lo[:, k, :], hn[k % 3], h_hi[:, k, :].bitcast(F32),
                                            ALU.subtract).then_inc(hlo[1], 1)

                def split_hi(m):
                    q = steps[m][0]
                    cn = CH_PASS[q] * P
                    dve.wait_ge(w_in[m % 2], 16 * (m // 2 + 1))
                    if m >= 2:
                        dve.wait_ge(w_used, m - 1)
                    nc.vector.tensor_copy(w_hi[:, m % 2, 0:cn], w_raw[:, m % 2, 0:cn]).then_inc(whi_done, 1)

                dve.wait_ge(cst, 48)
                nc.vector.tensor_tensor(fn[:], fg[:], np_col[:], ALU.mult).then_inc(fn_set, 1)
                dve.wait_ge(fn_set, 1)
                for m, (q, n) in enumerate(steps):
                    split_hi(m)
                    if q and n == 0:
                        drain(q - 1)
                    if q == 0:
                        z = zb[:, n % 3, :]
                        dve.wait_ge(oz_in[n % 3], 32 * (n // 3 + 1))
                        nc.vector.scalar_tensor_tensor(z, ob[:, n % 3, :], nw[:, 0:1], z,
                                                       ALU.mult, ALU.mult).then_inc(gz_done, 1)
                        dve.wait_ge(gz_done, n + 1)
                        dve.wait_ge(rinv_done, n + 1)
                        nc.vector.tensor_tensor(z, z, rinv[:], ALU.mult).then_inc(y_done, 1)
                        dve.wait_ge(y_done, n + 1)
                        nc.vector.tensor_copy(y(0, n), z).then_inc(yhi_done, 1)
                drain(len(CH_PASS) - 1)
                dve.wait_ge(ri2, 1)
                dve.wait_ge(bank_used, 2 * KD)
                dve.wait_ge(ss2, 2)
                nc.vector.tensor_tensor(rin2, rinv[:], rinv[:], ALU.mult).then_inc(ms2, 1)
                dve.wait_ge(ms2, 1)
                for i in range(2):
                    cut = slice(i * HALF, (i + 1) * HALF)
                    nc.vector.scalar_tensor_tensor(rin2[:, cut], p_s2[i][:], 1.0 / D, rin2[:, cut],
                                                   ALU.mult, ALU.mult).then_inc(ms2, 1)
                dve.wait_ge(ri2, 2)
                nc.vector.tensor_tensor(rin2, rin2, rinv[:], ALU.mult).then_inc(ms2, 1)
                dve.wait_ge(ms2, 4)
                dve.wait_ge(ylo_done, V_HEADS)
                for k in range(KD):
                    if k >= 3:
                        dve.wait_ge(hlo[(k - 3) % 2], (k - 3) // 2 + 1)
                    nc.vector.scalar_tensor_tensor(hn[k % 3], x1[:, k, :], fn[:, k:k + 1], rin2,
                                                   ALU.mult, ALU.mult).then_inc(hh, 1)
                    if k and k % 2 == 0:
                        low(k - 1)
                low(KD - 1)


MIX_JOBS = ("qa", "ka", "va", "qb", "kb", "vb", "za", "ob", "zb")


def mix_plan(projects, recurs):
    jobs = (list(range(6)) if projects else []) + (list(range(6, len(MIX_JOBS))) if recurs else [])
    slices = [("slice", j, h, k) for j in jobs for h in range(2) for k in range(KD)]
    steps = []
    if recurs:
        steps += [("edge",), ("gaps",), ("bcast",)]
        steps += [("cols", w, h) for w in range(3) for h in range(2)]
        steps += [("score", 0, 0), ("score", 0, 1), ("sim", 0)]
        for i in range(NT):
            steps += [("blend", i)]
            if i + 1 < NT:
                steps += [("score", i + 1, 0), ("score", i + 1, 1)]
            steps += [("update", i)]
            steps += [("turn", i, q) for q in range((i + 4) // 4)]
            steps += [("apply", i), ("out", i)]
            if i + 1 < NT:
                steps += [("sim", i + 1)]
            if i == NT - 2:
                steps += [("slope",)]
        steps += [("store",)]
    else:
        steps += [("bcast",)]

    def weight(s):
        if s[0] == "score":
            return 2 + s[1] // 3
        return 2 * (s[0] in ("cols", "sim", "update", "turn", "apply", "out"))

    total = sum(weight(s) for s in steps)
    out, sent, passed = [], 0, 0

    def send(upto):
        nonlocal sent
        while sent < min(upto, len(slices)):
            s = slices[sent]
            if s[2:] == (0, 2):
                out.append(("weights", s[1]))
            out.append(s)
            sent += 1
            if s[3] == KD - 1:
                out.append(("evac", s[1], s[2]))
                if s[2] == 1:
                    if MIX_JOBS[s[1]] in ("qb", "kb"):
                        out.append(("conv", s[1] - 3))
                    if MIX_JOBS[s[1]] in ("za", "ob", "zb"):
                        out.append(("gstore", s[1] - 6))
                    if MIX_JOBS[s[1]] == "vb":
                        out.append(("silu",))

    if not recurs:
        send(4 * KD)
        out.append(("gcols",))
    for s in steps:
        out.append(s)
        if weight(s):
            passed += weight(s)
            send(passed * len(slices) // total)
    send(len(slices))
    return out


def stage_mix(nc, ctx, io, keep):
    own = ExitStack()
    with own:
        def sb(name, shape, dt=F32):
            return own.enter_context(nc.sbuf_tensor(name, shape, dt))

        def ps(name, n=HALF):
            return own.enter_context(nc.psum_tensor(name, [P, n], F32))

        sem = lambda name: ctx.enter_context(nc.semaphore(name))
        h_hi, h_lo, ident, ones = keep["h_hi"], keep["h_lo"], keep["ident"], keep["ones"]
        DV = DH + 1

        w_raw = sb("m_raw", [P, KD * P])
        w_hi = sb("m_hi", [P, 2, KD * P], F32R)
        w_lo = sb("m_lo", [P, 2, KD * P], F32R)
        pre = sb("m_pre", [P, TAPS - 1 + T])
        conv_w = sb("m_conv_w", [P, HB, 2, TAPS])
        qa = sb("qa", [P, 2, T])
        ka = sb("ka", [P, 2, T])
        vaT = sb("vaT", [P, T])
        qb = sb("qb", [P, 2, T])
        kb = sb("kb", [P, 2, T])
        vbT = sb("vbT", [P, T])
        gt = sb("m_gt", [P, T])
        va = sb("va", [P, NT, P])
        v1 = sb("v1", [P, NT, DV])
        kw = sb("kw", [P, NT, P])
        alibi = sb("alibi", [P, T])
        sc = sb("sc", [P, 2, 2, T])
        mn = sb("mn", [P, 2, 2])
        ls = sb("ls", [P, 2, 2])
        rl = sb("rl", [P, 2, 2])
        r1 = sb("r1", [P, 2])
        PT = sb("PT", [P, NT, P])
        oA = sb("oA", [P, T])
        rows = sb("m_rows", [P, 2, T])
        dm = sb("dm", [P, NT, P])
        qw = sb("qw", [P, T])
        sm = sb("sm", [P, P])
        C = sb("C", [P, DV])
        hb = sb("hb", [P, P])
        hT = sb("hT", [P, T])
        tri = sb("m_tri", [P, P])
        den = sb("den", [P, 2])
        wk = sb("wk", [P, NT])
        dec = sb("dec", [P, NT])
        cols = sb("m_cols", [P, 2, NT, HB])
        bif = sb("bif", [P, 2])
        lq = sb("lq", [P, 4, DA])
        lp = sb("lp", [P, 2, DA])
        ld = sb("ld", [P, 2])
        nlam = sb("nlam", [P, 1])
        lnd = sb("lnd", [P, 1])

        p_job = [ps("m_job0"), ps("m_job1")]
        p_sc = ps("p_sc", T)
        p_t, p_a, p_s, p_u = ps("p_t"), ps("p_a"), ps("p_s"), ps("p_u")

        flat = sc[:].rearrange("p a b c -> p (a b) c")
        r_lf, r_i, r_b, r_m = (flat[:, q, :] for q in range(4))
        r_t, r_w = oA, hT

        N_IT = HB + 1
        plans = [mix_plan(True, False)] + [mix_plan(True, True)] * (HB - 1) + [mix_plan(False, True)]
        order = [ordinals(p) for p in plans]
        nj = len(MIX_JOBS)
        N_JOBS = 1 + nj * HB
        NTURN = sum((i + 4) // 4 for i in range(NT))

        cst = sem("d_cst"); lq_in = sem("d_lq")
        w_in = sem("d_w"); w_hi_done = sem("d_whi"); w_lo_done = sem("d_wlo")
        half_done = sem("d_half"); evac_done = sem("d_evac"); conv_step = sem("d_conv"); silu_done = sem("d_silu")
        set_up = sem("d_set"); g_store = sem("d_gst")
        g_act = sem("d_gact"); g_dve = sem("d_gdve"); g_pe = sem("d_gpe"); g_dma = sem("d_gdma"); i_moved = sem("d_im")
        lam = sem("d_lam"); lam_a = sem("d_lama")
        rows_in = sem("d_rows"); alibi_in = sem("d_alibi")
        edge_dve = sem("d_edged"); edge_act = sem("d_edgea")
        gap_dve = sem("d_gap"); gap_exp = sem("d_gape"); qw_done = sem("d_qw")
        cols_ready = sem("d_cr"); cols_done = sem("d_cd")
        sc_ready = sem("d_sr"); sc_used = sem("d_su"); exp_done = sem("d_exp")
        rl_done = sem("d_rl"); p1_done = sem("d_p1"); blend_done = sem("d_bl")
        turn_ready = sem("d_tr"); turn_cp = sem("d_tc"); app_ready = sem("d_ar"); app_cp = sem("d_ac")
        sim_ready = sem("d_simr"); sim_done = sem("d_simd"); up_ready = sem("d_upr"); c_done = sem("d_c")
        den_done = sem("d_den"); hb_done = sem("d_hb"); out_ready = sem("d_or"); out_cp = sem("d_oc")
        a_stored = sem("d_as")

        def job(i, j):
            return nj * i - 2 + j - (6 if i == HB else 0) if i else 1 + j

        with nc.Block() as block:
            @block.sync
            def _(sp):
                def load(J):
                    if J >= 1:
                        sp.wait_ge(w_lo_done, J)
                    sp.dma_start(w_raw[:], io["w2"][J]).then_inc(w_in, 16)

                load(0)
                for dst, src in ((tri[:], io["tri"]), (conv_w[:], io["conv_w2"]), (bif[0:4, :], io["bif"])):
                    sp.dma_start(dst, src).then_inc(cst, 16)
                sp.dma_start(lq[:].rearrange("p a d -> p (a d)"), io["lq"].broadcast_to([P, 4 * DA])).then_inc(lq_in, 16)
                sp.dma_start(alibi[:], io["alibi"][:, 0, :]).then_inc(alibi_in, 16)
                load(1)
                load(2)
                sp.wait_ge(evac_done, 2)
                sp.dma_start(r_i[0:4, :], pre[32:36, TAPS - 1:]).then_inc(i_moved, 16)
                for i in range(N_IT):
                    g = i - 1
                    for s in plans[i]:
                        if s[0] == "weights" and 2 < job(i, s[1]) + 1 < N_JOBS:
                            load(job(i, s[1]) + 1)
                        elif s[0] == "bcast" and i < HB:
                            if i == 0:
                                sp.wait_ge(g_dve, 24)
                                sp.dma_start(io["mrows"][0:4, :], r_t[0:4, :]).then_inc(g_dma, 16)
                                sp.dma_start(io["mrows"][4:8, :], r_w[0:4, :]).then_inc(g_dma, 16)
                                sp.wait_ge(g_dma, 32)
                            else:
                                sp.wait_ge(gap_dve, NT * i)
                                sp.wait_ge(edge_dve, 2 * i)
                                sp.wait_ge(edge_act, 2 * i)
                                sp.wait_ge(qw_done, 2 * i)
                            for q in range(2):
                                sp.dma_start(rows[:, q, :], io["mrows"][4 * q + i:4 * q + i + 1, :].broadcast_to([P, T])
                                             ).then_inc(rows_in, 16)
                        elif s[0] == "slope" and i < HB:
                            sp.wait_ge(sc_used, 2 * NT * i)
                            sp.dma_start(alibi[:], io["alibi"][:, i, :]).then_inc(alibi_in, 16)
                        elif s[0] == "gstore":
                            sp.wait_ge(evac_done, 2 * job(i, 6 + s[1]) + 2)
                            sp.dma_start(io["g_scr"][3 * g + s[1]], gt[:]).then_inc(g_store, 16)
                        elif s[0] == "store":
                            sp.wait_ge(app_cp, NT * i)
                            sp.dma_start(io["a_scr"][g], oA[:]).then_inc(a_stored, 16)
                            sp.wait_ge(out_cp, NT * i)
                            sp.dma_start(io["a_scr"][HA + g], hT[:]).then_inc(a_stored, 16)
                sp.wait_ge(g_store, 16 * 3 * HB)
                sp.wait_ge(a_stored, 32 * HB)

            @block.gpsimd
            def _(pool):
                def split_lo(J):
                    pool.wait_ge(w_hi_done, J + 1)
                    nc.gpsimd.tensor_tensor(w_lo[:, J % 2, :], w_raw[:], w_hi[:, J % 2, :].bitcast(F32),
                                            ALU.subtract).then_inc(w_lo_done, 1)

                for J in range(3):
                    split_lo(J)
                for i in range(N_IT):
                    g = i - 1
                    for s in plans[i]:
                        if s[0] == "weights" and 2 < job(i, s[1]) + 1 < N_JOBS:
                            split_lo(job(i, s[1]) + 1)
                        elif s[0] == "gaps":
                            pool.wait_ge(qw_done, 2 * g + 1)
                            pool.wait_ge(silu_done, 2 * (g + 1))
                            nc.gpsimd.tensor_tensor(qw[:], qw[:], qb[:, g % 2, :], ALU.mult).then_inc(qw_done, 1)

            @block.scalar
            def _(act):
                def evac(J, h, out, func=ACT.Copy, scale=1.0):
                    act.wait_ge(half_done, 2 * J + h + 1)
                    nc.scalar.activation(out[:, h * HALF:(h + 1) * HALF], p_job[h][:], func,
                                         scale=scale).then_inc(evac_done, 1)

                nc.scalar.preload_act_table_set(EXP_LN)
                evac(0, 0, pre[:, TAPS - 1:])
                evac(0, 1, pre[:, TAPS - 1:])
                act.wait_ge(g_dve, 2)
                nc.scalar.activation(r_w[0:4, :], r_w[0:4, :], ACT.Exp).then_inc(g_act, 1)
                act.wait_ge(g_act, 1)
                nc.scalar.activation(r_w[0:4, :], r_w[0:4, :], ACT.Ln, bias=1.0).then_inc(g_act, 1)
                act.wait_ge(lam, 2)
                nc.scalar.activation(ld[:], ld[:], ACT.Exp).then_inc(lam_a, 1)

                for i in range(N_IT):
                    g = i - 1
                    o, n = order[i]
                    for s in plans[i]:
                        if s[0] == "evac":
                            j, h = s[1:]
                            J = job(i, j)
                            name = MIX_JOBS[j]
                            if name == "qa":
                                if h == 0 and i >= 2:
                                    act.wait_ge(sc_ready, 2 * NT * (i - 1))
                                evac(J, h, qa[:, i % 2, :], ACT.Copy, -(DA ** -0.5))
                            elif name == "ka":
                                evac(J, h, ka[:, i % 2, :])
                            elif name == "va":
                                if h == 0 and i >= 1:
                                    act.wait_ge(cols_ready, 6 * i)
                                evac(J, h, vaT)
                            elif name == "vb":
                                evac(J, h, vbT)
                            elif name in ("qb", "kb"):
                                if h == 0:
                                    if i or name == "kb":
                                        act.wait_ge(conv_step, 8 * i + (4 if name == "kb" else 0))
                                    else:
                                        act.wait_ge(i_moved, 16)
                                        act.wait_ge(g_dve, 1)
                                evac(J, h, pre[:, TAPS - 1:])
                            else:
                                if h == 0 and (g or name != "za"):
                                    act.wait_ge(g_store, 16 * (3 * g + j - 6))
                                evac(J, h, gt, ACT.Sigmoid if name == "ob" else ACT.Silu)
                        elif s[0] == "gcols":
                            act.wait_ge(g_pe, 1)
                            nc.scalar.activation(cols[:, 0], p_t[:, 0:32].rearrange("p (t h) -> p t h", h=HB),
                                                 ACT.Copy).then_inc(g_act, 1)
                            nc.scalar.activation(cols[:, 1], p_t[:, 32:64].rearrange("p (t h) -> p t h", h=HB),
                                                 ACT.Exp, scale=-1.0).then_inc(g_act, 1)
                        elif s[0] == "silu":
                            act.wait_ge(conv_step, 8 * (i + 1))
                            nc.scalar.activation(qb[:, i % 2, :], qb[:, i % 2, :], ACT.Silu).then_inc(silu_done, 1)
                            nc.scalar.activation(kb[:, i % 2, :], kb[:, i % 2, :], ACT.Silu).then_inc(silu_done, 1)
                        elif s[0] == "edge":
                            act.wait_ge(edge_dve, 2 * g + 1)
                            nc.scalar.activation(wk[:], wk[:], ACT.Exp).then_inc(edge_act, 1)
                            if g >= 1:
                                act.wait_ge(c_done, (NT + 1) * g)
                            nc.scalar.activation(dec[:], rows[:, 1, P - 1::P], ACT.Exp).then_inc(edge_act, 1)
                        elif s[0] == "gaps":
                            if g >= 1:
                                act.wait_ge(up_ready, NT * g)
                            act.wait_ge(rows_in, 32 * (g + 1))
                            act.wait_ge(set_up, 4)
                            nc.scalar.activation(qw[:], rows[:, 1, :], ACT.Exp, bias=lnd[:, 0:1]).then_inc(qw_done, 1)
                            act.wait_ge(gap_dve, NT * (g + 1))
                            nc.scalar.activation(dm[:], dm[:], ACT.Exp, bias=lnd[:, 0:1]).then_inc(gap_exp, 1)
                        elif s[0] == "score":
                            t, c = s[1:]
                            m = 2 * NT * g + 2 * t + c
                            w = (t + 1) * P
                            act.wait_ge(sc_used, m + 1)
                            if m >= 4:
                                act.wait_ge(rl_done, 2 * (m // 2) - 2)
                            nc.scalar.activation(sc[:, t % 2, c, 0:w], sc[:, t % 2, c, 0:w], ACT.Exp, scale=-1.0,
                                                 bias=mn[:, t % 2, c:c + 1], accum_out=ls[:, t % 2, c:c + 1]
                                                 ).then_inc(exp_done, 1)
                        elif s[0] == "blend":
                            t = s[1]
                            w = (t + 1) * P
                            m = NT * g + t
                            act.wait_ge(rl_done, 2 * m + 2)
                            nc.scalar.activation(sc[:, t % 2, 1, 0:w], sc[:, t % 2, 1, 0:w], ACT.Copy,
                                                 scale=r1[:, t % 2:t % 2 + 1]).then_inc(p1_done, 1)
                        elif s[0] == "cols":
                            w, h = s[1:]
                            m = 6 * g + o[s]
                            act.wait_ge(cols_ready, m + 1)
                            src = p_t[:].rearrange("p (t c) -> p t c", c=P)
                            cut = slice(4 * h, 4 * h + 4)
                            if w == 0:
                                if g >= 1:
                                    act.wait_ge(app_ready, NT * g)
                                nc.scalar.activation(va[:, cut, :], src, ACT.Copy).then_inc(cols_done, 1)
                            elif w == 1:
                                if g >= 1:
                                    act.wait_ge(up_ready, NT * g)
                                act.wait_ge(set_up, 4)
                                nc.scalar.activation(v1[:, cut, 0:P], src, ACT.Copy).then_inc(cols_done, 1)
                            else:
                                act.wait_ge(edge_act, 2 * g + 1)
                                for t in range(4):
                                    last = nc.scalar.activation(kw[:, 4 * h + t, :], p_t[:, t * P:(t + 1) * P], ACT.Copy,
                                                                scale=wk[:, 4 * h + t:4 * h + t + 1])
                                last.then_inc(cols_done, 1)
                        elif s[0] == "turn":
                            t, q = s[1:]
                            m = NTURN * g + o[s]
                            nb = min(4, t + 1 - 4 * q)
                            act.wait_ge(turn_ready, m + 1)
                            if q == 0 and NT * g + t >= 1:
                                act.wait_ge(app_ready, NT * g + t)
                            nc.scalar.activation(PT[:, 4 * q:4 * q + nb, :].rearrange("p b c -> p (b c)"),
                                                 p_t[:, 0:nb * P], ACT.Copy).then_inc(turn_cp, 1)
                        elif s[0] == "update":
                            c = s[1]
                            m = NT * g + c
                            act.wait_ge(den_done, 3 * m + 3)
                            if m >= 1:
                                act.wait_ge(out_ready, m)
                            nc.scalar.activation(hb[:], p_u[:, 0:P], ACT.Copy, scale=den[:, 1:2]).then_inc(hb_done, 1)
                        elif s[0] == "out":
                            c = s[1]
                            m = NT * g + c
                            act.wait_ge(out_ready, m + 1)
                            if c == 0 and g >= 1:
                                act.wait_ge(a_stored, 32 * g)
                            elif g == 0 and c == 0:
                                act.wait_ge(g_dma, 32)
                            nc.scalar.activation(hT[:, c * P:(c + 1) * P], p_u[:, 256:256 + P],
                                                 ACT.Copy).then_inc(out_cp, 1)

            @block.tensor
            def _(pe):
                def piece(J, h, k):
                    if h == 0 and k == 0:
                        pe.wait_ge(w_lo_done, J + 1)
                    if k == 0 and J >= 1:
                        pe.wait_ge(evac_done, 2 * (J - 1) + h + 1)
                    cut = slice(h * HALF, (h + 1) * HALF)
                    hi, lo = w_hi[:, J % 2, k * P:(k + 1) * P], w_lo[:, J % 2, k * P:(k + 1) * P]
                    nc.tensor.matmul(p_job[h][:], hi, h_hi[:, k, cut], start=(k == 0), stop=False)
                    nc.tensor.matmul(p_job[h][:], hi, h_lo[:, k, cut], start=False, stop=False)
                    last = nc.tensor.matmul(p_job[h][:], lo, h_hi[:, k, cut], start=False, stop=(k == KD - 1))
                    if k == KD - 1:
                        last.then_inc(half_done, 1)

                for h in range(2):
                    for k in range(KD):
                        piece(0, h, k)
                for i in range(N_IT):
                    g = i - 1
                    o, n = order[i]
                    for s in plans[i]:
                        if s[0] == "slice":
                            piece(job(i, s[1]), s[2], s[3])
                        elif s[0] == "gcols":
                            pe.wait_ge(g_dve, 24)
                            for q, r in ((0, r_i), (1, r_m)):
                                for t in range(NT):
                                    at = 32 * q + HB * t
                                    last = nc.tensor.transpose(p_t[:, at:at + HB], r[0:HB, t * P:(t + 1) * P],
                                                               ident[0:HB, 0:HB])
                            last.then_inc(g_pe, 1)
                        elif s[0] == "cols":
                            w, h = s[1:]
                            m = 6 * g + o[s]
                            pe.wait_ge(evac_done, 2 * job(g, 5) + 2)
                            pe.wait_ge(silu_done, 2 * (g + 1))
                            if o[s]:
                                pe.wait_ge(cols_done, m)
                            elif g:
                                pe.wait_ge(turn_cp, NTURN * g)
                            else:
                                pe.wait_ge(g_act, 4)
                            src = (vaT[:], vbT[:], kb[:, g % 2, :])[w]
                            for t in range(4):
                                last = nc.tensor.transpose(p_t[:, t * P:(t + 1) * P],
                                                           src[:, (4 * h + t) * P:(4 * h + t + 1) * P], ident[:])
                            last.then_inc(cols_ready, 1)
                        elif s[0] == "score":
                            t, c = s[1:]
                            m = 2 * NT * g + 2 * t + c
                            pe.wait_ge(evac_done, 2 * job(g, 1) + 2)
                            if m >= 1:
                                pe.wait_ge(sc_used, m)
                            w = (t + 1) * P
                            half = slice(DA * c, DA * (c + 1))
                            for a in range(0, w, HALF):
                                e = min(a + HALF, w)
                                last = nc.tensor.matmul(p_sc[:, a:e], qa[half, g % 2, t * P:(t + 1) * P],
                                                        ka[half, g % 2, a:e], start=True, stop=True)
                            last.then_inc(sc_ready, 1)
                        elif s[0] == "turn":
                            t, q = s[1:]
                            m = NTURN * g + o[s]
                            pe.wait_ge(blend_done, NT * g + t + 1)
                            if o[s]:
                                pe.wait_ge(turn_cp, m)
                            else:
                                pe.wait_ge(cols_done, 6 * (g + 1))
                            nb = min(4, t + 1 - 4 * q)
                            for b in range(nb):
                                last = nc.tensor.transpose(p_t[:, b * P:(b + 1) * P],
                                                           sc[:, t % 2, 0, (4 * q + b) * P:(4 * q + b + 1) * P], ident[:])
                            last.then_inc(turn_ready, 1)
                        elif s[0] == "apply":
                            t = s[1]
                            m = NT * g + t
                            pe.wait_ge(turn_cp, NTURN * g + o[("turn", t, t // 4)] + 1)
                            if m >= 1:
                                pe.wait_ge(app_cp, m)
                            for b in range(t + 1):
                                last = nc.tensor.matmul(p_a[:, 0:P], va[:, b, :], PT[:, b, :], start=(b == 0), stop=(b == t))
                            last.then_inc(app_ready, 1)
                        elif s[0] == "sim":
                            c = s[1]
                            m = NT * g + c
                            if m >= 1:
                                pe.wait_ge(c_done, (NT + 1) * g + 1 + c)
                            pe.wait_ge(silu_done, 2 * (g + 1))
                            cut = slice(c * P, (c + 1) * P)
                            nc.tensor.matmul(p_s[:, 0:P], kb[:, g % 2, cut], qb[:, g % 2, cut], start=True, stop=True
                                             ).then_inc(sim_ready, 1)
                        elif s[0] == "update":
                            c = s[1]
                            m = NT * g + c
                            pe.wait_ge(sim_done, m + 1)
                            pe.wait_ge(c_done, (NT + 1) * g + 1 + c)
                            pe.wait_ge(qw_done, 2 * g + 2)
                            pe.wait_ge(cols_done, 6 * (g + 1))
                            if m >= 1:
                                pe.wait_ge(out_cp, m)
                            nc.tensor.matmul(p_u[:, 0:DV], qw[:, c * P:(c + 1) * P], C[:], start=True, stop=False)
                            nc.tensor.matmul(p_u[:, 0:DV], sm[:], v1[:, c, :], start=False, stop=True)
                            nc.tensor.matmul(p_s[:, 256:256 + DV], kw[:, c, :], v1[:, c, :], start=True, stop=True
                                             ).then_inc(up_ready, 1)
                        elif s[0] == "out":
                            c = s[1]
                            m = NT * g + c
                            pe.wait_ge(hb_done, m + 1)
                            nc.tensor.transpose(p_u[:, 256:256 + P], hb[:], ident[:]).then_inc(out_ready, 1)

            @block.vector
            def _(dve):
                def split_hi(J):
                    dve.wait_ge(w_in, 16 * (J + 1))
                    if J >= 2:
                        dve.wait_ge(half_done, 2 * (J - 1))
                    nc.vector.tensor_copy(w_hi[:, J % 2, :], w_raw[:]).then_inc(w_hi_done, 1)

                nc.vector.memset(pre[:, 0:TAPS - 1], 0.0).then_inc(set_up, 1)
                nc.vector.memset(v1[:, :, P:DV], 1.0).then_inc(set_up, 1)
                nc.vector.memset(lnd[:], float(np.log(DH ** -0.5))).then_inc(set_up, 1)
                nc.vector.memset(nlam[:], 0.0).then_inc(set_up, 1)
                split_hi(0)
                split_hi(1)
                dve.wait_ge(lq_in, 16)
                nc.vector.tensor_tensor(lp[:], lq[:, 0::2, :], lq[:, 1::2, :], ALU.mult).then_inc(lam, 1)
                dve.wait_ge(lam, 1)
                nc.vector.reduce_sum(ld[:], lp[:], axis=AX).then_inc(lam, 1)

                dve.wait_ge(cst, 48)
                dve.wait_ge(evac_done, 2)
                nc.vector.tensor_scalar(r_lf[0:4, :], pre[0:4, TAPS - 1:], bif[0:4, 0:1], None, ALU.add
                                        ).then_inc(g_dve, 1)
                dve.wait_ge(g_dve, 1)
                nc.vector.scalar_tensor_tensor(r_w[0:4, :], r_lf[0:4, :], -1.0, r_lf[0:4, :], ALU.mult, ALU.min
                                               ).then_inc(g_dve, 1)
                dve.wait_ge(g_act, 2)
                nc.vector.scalar_tensor_tensor(r_lf[0:4, :], r_lf[0:4, :], 0.0, r_w[0:4, :], ALU.min, ALU.subtract
                                               ).then_inc(g_dve, 1)
                dve.wait_ge(i_moved, 16)
                nc.vector.tensor_scalar(r_i[0:4, :], r_i[0:4, :], bif[0:4, 1:2], None, ALU.add).then_inc(g_dve, 1)
                dve.wait_ge(g_dve, 4)
                split_hi(2)
                nc.vector.tensor_tensor_scan(r_m[0:4, :], r_lf[0:4, :], r_i[0:4, :], 0.0, ALU.add, ALU.max
                                             ).then_inc(g_dve, 1)
                for t in range(NT):
                    c = slice(t * P, (t + 1) * P)
                    nc.vector.tensor_tensor_scan(r_b[0:4, c], ones[0:4, :], r_lf[0:4, c], 0.0, ALU.mult, ALU.add
                                                 ).then_inc(g_dve, 1)
                dve.wait_ge(g_dve, 13)
                nc.vector.tensor_tensor(r_t[0:4, :], r_b[0:4, :], r_m[0:4, :], ALU.subtract).then_inc(g_dve, 1)
                nc.vector.tensor_tensor(r_i[0:4, :], r_i[0:4, :], r_b[0:4, :], ALU.subtract).then_inc(g_dve, 1)
                dve.wait_ge(g_dve, 14)
                nc.vector.tensor_copy(r_w[0:4, 0:P], r_t[0:4, 0:P]).then_inc(g_dve, 1)
                for t in range(1, NT):
                    c = slice(t * P, (t + 1) * P)
                    nc.vector.tensor_scalar(r_w[0:4, c], r_t[0:4, c], r_m[0:4, t * P - 1:t * P], None, ALU.add
                                            ).then_inc(g_dve, 1)
                dve.wait_ge(g_dve, 23)
                dve.wait_ge(lam_a, 1)
                nc.vector.tensor_tensor(nlam[:], ld[:, 1:2], ld[:, 0:1], ALU.subtract).then_inc(lam, 1)
                dve.wait_ge(lam, 3)
                nc.vector.tensor_scalar_add(nlam[:], nlam[:], -0.2).then_inc(g_dve, 1)

                for i in range(N_IT):
                    g = i - 1
                    o, n = order[i]
                    for s in plans[i]:
                        if s[0] == "weights" and 2 < job(i, s[1]) + 1 < N_JOBS:
                            split_hi(job(i, s[1]) + 1)
                        elif s[0] == "conv":
                            j = s[1]
                            base = 8 * i + 4 * j
                            dst = (qb, kb)[j][:, i % 2, :]
                            dve.wait_ge(evac_done, 2 * job(i, 3 + j) + 2)
                            if i >= 2:
                                dve.wait_ge(sim_ready, NT * (i - 1))
                            nc.vector.tensor_scalar(dst, pre[:, 0:T], conv_w[:, i, j, 0:1], None,
                                                    ALU.mult).then_inc(conv_step, 1)
                            for q in range(1, TAPS):
                                dve.wait_ge(conv_step, base + q)
                                nc.vector.scalar_tensor_tensor(dst, pre[:, q:q + T], conv_w[:, i, j, q:q + 1], dst,
                                                               ALU.mult, ALU.add).then_inc(conv_step, 1)
                        elif s[0] == "edge":
                            dve.wait_ge(rows_in, 32 * (g + 1))
                            dve.wait_ge(g_act, 4)
                            if g >= 1:
                                dve.wait_ge(cols_done, 6 * g)
                                dve.wait_ge(up_ready, NT * g)
                                dve.wait_ge(c_done, (NT + 1) * g)
                            nc.vector.tensor_tensor(wk[:], rows[:, 0, P - 1::P], cols[:, 0, :, g], ALU.add
                                                    ).then_inc(edge_dve, 1)
                            nc.vector.memset(C[:], 0.0).then_inc(c_done, 1)
                            nc.vector.memset(den[:], 0.0).then_inc(edge_dve, 1)
                        elif s[0] == "gaps":
                            if g >= 1:
                                dve.wait_ge(sim_done, NT * g)
                            for t in range(NT):
                                nc.vector.scalar_tensor_tensor(dm[:, t, :], rows[:, 0, t * P:(t + 1) * P],
                                                               cols[:, 0, t, g:g + 1], tri[:], ALU.add, ALU.add
                                                               ).then_inc(gap_dve, 1)
                        elif s[0] == "score":
                            t, c = s[1:]
                            m = 2 * NT * g + 2 * t + c
                            w = (t + 1) * P
                            dve.wait_ge(sc_ready, m + 1)
                            dve.wait_ge(alibi_in, 16 * (g + 1))
                            if NT * g + t >= 2:
                                dve.wait_ge(turn_ready, NTURN * g + o[("turn", t - 2, (t - 2) // 4)] + 1 if t >= 2
                                            else NTURN * (g - 1) + o[("turn", NT - 2 + t, 1)] + 1)
                            else:
                                dve.wait_ge(g_pe, 1)
                            nc.vector.tensor_tensor_reduce(
                                out=sc[:, t % 2, c, 0:w], in0=p_sc[:, 0:w], in1=alibi[:, T - w:], scale=1.0,
                                scalar=3.0e38, op0=ALU.add, op1=ALU.min, accum_out=mn[:, t % 2, c:c + 1]
                            ).then_inc(sc_used, 1)
                        elif s[0] == "blend":
                            t = s[1]
                            w = (t + 1) * P
                            m = NT * g + t
                            dve.wait_ge(exp_done, 2 * m + 2)
                            if m >= 2:
                                dve.wait_ge(blend_done, m - 1)
                            nc.vector.reciprocal(rl[:, t % 2, :], ls[:, t % 2, :]).then_inc(rl_done, 1)
                            dve.wait_ge(rl_done, 2 * m + 1)
                            if m >= 2:
                                dve.wait_ge(p1_done, m - 1)
                            nc.vector.tensor_tensor(r1[:, t % 2:t % 2 + 1], rl[:, t % 2, 1:2], nlam[:], ALU.mult
                                                    ).then_inc(rl_done, 1)
                            dve.wait_ge(p1_done, m + 1)
                            nc.vector.scalar_tensor_tensor(sc[:, t % 2, 0, 0:w], sc[:, t % 2, 0, 0:w],
                                                           rl[:, t % 2, 0:1], sc[:, t % 2, 1, 0:w],
                                                           ALU.mult, ALU.add).then_inc(blend_done, 1)
                        elif s[0] == "apply":
                            t = s[1]
                            m = NT * g + t
                            dve.wait_ge(app_ready, m + 1)
                            if t == 0 and g >= 1:
                                dve.wait_ge(a_stored, 32 * g)
                            elif t == 0:
                                dve.wait_ge(g_dma, 32)
                            nc.vector.tensor_copy(oA[:, t * P:(t + 1) * P], p_a[:, 0:P]).then_inc(app_cp, 1)
                        elif s[0] == "sim":
                            c = s[1]
                            m = NT * g + c
                            dve.wait_ge(sim_ready, m + 1)
                            dve.wait_ge(gap_exp, g + 1)
                            if m >= 1:
                                dve.wait_ge(up_ready, m)
                            nc.vector.tensor_tensor(sm[:], p_s[:, 0:P], dm[:, c, :], ALU.mult).then_inc(sim_done, 1)
                        elif s[0] == "update":
                            c = s[1]
                            m = NT * g + c
                            dve.wait_ge(up_ready, m + 1)
                            dve.wait_ge(edge_act, 2 * g + 2)
                            if m >= 1:
                                dve.wait_ge(hb_done, m)
                            dve.wait_ge(edge_dve, 2 * g + 2)
                            nc.vector.scalar_tensor_tensor(den[:, 0:1], p_u[:, P:DV], -1.0, cols[:, 1, c, g:g + 1],
                                                           ALU.mult, ALU.max).then_inc(den_done, 1)
                            dve.wait_ge(den_done, 3 * m + 1)
                            nc.vector.tensor_tensor(den[:, 0:1], p_u[:, P:DV], den[:, 0:1], ALU.max
                                                    ).then_inc(den_done, 1)
                            dve.wait_ge(den_done, 3 * m + 2)
                            nc.vector.reciprocal(den[:, 1:2], den[:, 0:1]).then_inc(den_done, 1)
                            dve.wait_ge(c_done, (NT + 1) * g + 1 + c)
                            nc.vector.scalar_tensor_tensor(C[:], C[:], dec[:, c:c + 1], p_s[:, 256:256 + DV],
                                                           ALU.mult, ALU.add).then_inc(c_done, 1)


MERGE_JOBS = ([("ga", c) for c in range(KD)] + [("gb", 0)]
              + [job for c in range(1, KD) for job in (("gb", c), ("ab", c - 1))] + [("ab", KD - 1)])


def stage_merge(nc, ctx, io, keep):
    own = ExitStack()
    with own:
        def sb(name, shape, dt=F32):
            return own.enter_context(nc.sbuf_tensor(name, shape, dt))

        def ps(name):
            return own.enter_context(nc.psum_tensor(name, [P, HALF], F32))

        sem = lambda name: ctx.enter_context(nc.semaphore(name))
        h_hi, h_lo, ident, ones, eps = (keep[n] for n in ("h_hi", "h_lo", "ident", "ones", "eps"))
        NY = HA + HB
        y_hi = sb("y_hi", [P, NY, T], F32R)
        y_lo = sb("y_lo", [P, NY, T], F32R)
        w_raw = sb("e_raw", [P, 2, KD * P])
        w_hi = sb("e_hi", [P, 2, KD * P], F32R)
        w_lo = sb("e_lo", [P, 2, KD * P], F32R)
        mg = sb("mg", [P, KD, T])
        ab = sb("ab", [P, 2, T])
        g1 = sb("g1", [P, T])
        sq = sb("e_sq", [P, T])
        rinv = sb("e_rinv", [P, T])
        ny = sb("ny", [P, NY])
        sgb = g1
        rr = sb("e_rr", [P, 2])
        banks = [ps(f"e_b{i}") for i in range(8)]
        p_ss = banks[6:8]

        cst = sem("e_cst"); nys = sem("e_nys"); in_a = [sem("e_ina0"), sem("e_ina1")]; in_g = sem("e_ing")
        ob_done = sem("e_ob"); sq_done = sem("e_sq"); ss_done = sem("e_ss"); ln_done = sem("e_ln"); ri_done = sem("e_ri")
        gz = sem("e_gz"); yb = sem("e_y"); yh = sem("e_yh"); yl = sem("e_yl")
        w_in = [sem("e_w0"), sem("e_w1")]; w_hi_done = sem("e_whi"); w_lo_done = sem("e_wlo"); job_done = sem("e_job")
        sg_done = sem("e_sg"); m1 = sem("e_m1"); m2 = sem("e_m2"); m3 = sem("e_m3")
        wo_in = [sem(f"e_wo{k}") for k in range(KD)]; wo_hi = sem("e_wohi"); wo_lo = [sem("e_wol0"), sem("e_wol1")]
        mg_hi = sem("e_mh"); mg_lo = [sem("e_ml"), sem("e_ml7")]; np_in = sem("e_np")
        x_in = [sem("e_x0"), sem("e_x1")]; o_ready = sem("e_or"); x_ready = sem("e_xr")
        fx = sem("e_fx"); r_sq = sem("e_rsq"); r_ln = sem("e_rln"); r_done = sem("e_rd"); t_done = sem("e_t"); f_done = sem("e_f")
        stored = [sem("e_st0"), sem("e_st1")]
        NJ = len(MERGE_JOBS)
        at = {job: J for J, job in enumerate(MERGE_JOBS)}
        LAST_GATE = at[("gb", KD - 1)]

        wo_raw = [w_raw[:, 0, :], w_raw[:, 1, :], ab[:, 0, :], ab[:, 1, :], sq[:], rinv[:],
                  w_raw[:, 0, :], w_raw[:, 1, :]]
        npost, fgr = sgb, mg[:, 1, :]
        xt = [ab[:, q, :].rearrange("p (k t) -> p k t", k=KD) for q in range(2)]
        tmp, fin = [sq, rinv], [w_raw[:, 0, :], w_raw[:, 1, :]]

        with nc.Block() as block:
            @block.sync
            def _(sp):
                def load(J):
                    if J >= 2:
                        sp.wait_ge(w_lo_done, J - 1)
                    sp.dma_start(w_raw[:, J % 2, :], io["w3"][J]).then_inc(w_in[J % 2], 16)

                load(0)
                sp.dma_start(ny[:], io["norm_y"]).then_inc(cst, 16)
                load(1)
                for n in range(NY):
                    if n >= 2:
                        sp.wait_ge(yl, n - 1)
                    sp.dma_start(ab[:, n % 2, :], io["a_scr"][n]).then_inc(in_a[n % 2], 16)
                    if n == 1:
                        for m in range(NY):
                            row = 3 * m if m < HA else 3 * (m - HA) + 2
                            sp.dma_start(y_lo[:, m, :].bitcast(F32), io["g_scr"][row]).then_inc(in_g, 16)
                        for m in range(HA, NY):
                            sp.dma_start(y_hi[:, m, :].bitcast(F32), io["g_scr"][3 * (m - HA) + 1]).then_inc(in_g, 16)
                    load(n + 2)
                for J in range(NY + 2, NJ):
                    load(J)
                sp.wait_ge(yl, NY)
                for k in range(2, KD - 2):
                    sp.dma_start(wo_raw[k], io["w_out2"][k * P:(k + 1) * P, :]).then_inc(wo_in[k], 16)
                for k in range(2):
                    sp.wait_ge(w_lo_done, NJ - 1 + k)
                    sp.dma_start(wo_raw[k], io["w_out2"][k * P:(k + 1) * P, :]).then_inc(wo_in[k], 16)
                for k in range(KD - 2, KD):
                    sp.wait_ge(wo_lo[k % 2], 1)
                    sp.dma_start(wo_raw[k], io["w_out2"][k * P:(k + 1) * P, :]).then_inc(wo_in[k], 16)
                sp.wait_ge(m3, KD)
                sp.wait_ge(mg_lo[0], 2)
                sp.dma_start(fgr, io["final_row"].broadcast_to([P, T])).then_inc(np_in, 16)
                sp.dma_start(npost[:], io["norm_post"].broadcast_to([P, T])).then_inc(np_in, 16)
                for t in range(NT):
                    if t >= 2:
                        sp.wait_ge(x_ready, t - 1)
                    else:
                        sp.wait_ge(wo_lo[t], 2)
                    sp.dma_start(xt[t % 2], io["x1_scr"][:, :, t * P:(t + 1) * P].rearrange("k p t -> p k t")
                                 ).then_inc(x_in[t % 2], 16)
                    if t >= 1:
                        sp.wait_ge(f_done, t)
                        sp.dma_start(io["out"][(t - 1) * P:t * P, :], fin[(t - 1) % 2]).then_inc(stored[(t - 1) % 2], 16)
                sp.wait_ge(f_done, NT)
                sp.dma_start(io["out"][(NT - 1) * P:, :], fin[(NT - 1) % 2]).then_inc(stored[(NT - 1) % 2], 16)
                for q in range(2):
                    sp.wait_ge(stored[q], 16 * NT // 2)

            @block.gpsimd
            def _(pool):
                def split_lo(J):
                    pool.wait_ge(w_hi_done, J + 1)
                    nc.gpsimd.tensor_tensor(w_lo[:, J % 2, :], w_raw[:, J % 2, :], w_hi[:, J % 2, :].bitcast(F32),
                                            ALU.subtract).then_inc(w_lo_done, 1)

                split_lo(0)
                split_lo(1)
                for n in range(NY):
                    pool.wait_ge(yh, n + 1)
                    nc.gpsimd.tensor_tensor(y_lo[:, n, :], ab[:, n % 2, :], y_hi[:, n, :].bitcast(F32),
                                            ALU.subtract).then_inc(yl, 1)
                    split_lo(n + 2)
                for J in range(NY + 2, NJ):
                    split_lo(J)
                for k in range(KD - 1):
                    pool.wait_ge(mg_hi, k + 1)
                    nc.gpsimd.tensor_tensor(h_lo[:, k, :], mg[:, k, :], h_hi[:, k, :].bitcast(F32),
                                            ALU.subtract).then_inc(mg_lo[0], 1)
                for k in range(0, KD, 2):
                    pool.wait_ge(wo_hi, k + 1)
                    nc.gpsimd.tensor_tensor(y_lo[:, k, :], wo_raw[k], y_hi[:, k, :].bitcast(F32),
                                            ALU.subtract).then_inc(wo_lo[0], 1)

            @block.scalar
            def _(act):
                def square(n):
                    if n < HA:
                        act.wait_ge(in_a[n % 2], 16 * (n // 2 + 1))
                    else:
                        act.wait_ge(ob_done, n - HA + 1)
                    if n >= 1:
                        act.wait_ge(ss_done, n)
                    nc.scalar.activation(sq[:], ab[:, n % 2, :], ACT.Square).then_inc(sq_done, 1)

                def gate(J, dst):
                    G = J if J < KD else KD + MERGE_JOBS[J][1]
                    act.wait_ge(job_done, J + 1)
                    for i in range(2):
                        nc.scalar.activation(dst[:, i * HALF:(i + 1) * HALF], banks[2 * (G % 2) + i][:],
                                             ACT.Sigmoid).then_inc(sg_done, 1)

                def merged_hi(k):
                    act.wait_ge(m3, k + 1)
                    nc.scalar.activation(h_hi[:, k, :], mg[:, k, :], ACT.Copy).then_inc(mg_hi, 1)

                def wo_part(k):
                    act.wait_ge(wo_in[k], 16)
                    nc.scalar.activation(y_hi[:, k, :], wo_raw[k], ACT.Copy).then_inc(wo_hi, 1)

                square(0)
                for n in range(NY):
                    act.wait_ge(ss_done, n + 1)
                    if n >= 1:
                        act.wait_ge(yb, n)
                    nc.scalar.preload_act_table_set(EXP_LN)
                    for i in range(2):
                        nc.scalar.activation(rinv[:, i * HALF:(i + 1) * HALF], p_ss[i][:], ACT.Ln, scale=1.0 / P,
                                             bias=eps[:, 0:1]).then_inc(ln_done, 1)
                    act.wait_ge(ln_done, 2 * n + 2)
                    nc.scalar.activation(rinv[:], rinv[:], ACT.Exp, scale=-0.5).then_inc(ri_done, 1)
                    if n + 1 < NY:
                        square(n + 1)
                    gate(n, mg[:, n, :])
                for c in range(KD):
                    if c >= 1:
                        act.wait_ge(m3, c)
                    else:
                        act.wait_ge(yb, NY)
                    gate(at[("gb", c)], sgb)
                nc.scalar.preload_act_table_set(EXP_LN)
                act.wait_ge(job_done, LAST_GATE + 1)
                for k in range(KD - 1):
                    merged_hi(k)
                act.wait_ge(job_done, NJ)
                wo_part(0)
                wo_part(1)
                merged_hi(KD - 1)
                for k in range(2, KD):
                    wo_part(k)
                for t in range(NT):
                    act.wait_ge(o_ready, t + 1)
                    if t >= 1:
                        act.wait_ge(t_done, 2 * t)
                    else:
                        act.wait_ge(mg_lo[0], KD - 1)
                    for i in range(2):
                        b = banks[2 * (t % 2) + i]
                        nc.scalar.activation(mg[:, 0, i * HALF:(i + 1) * HALF], b[:], ACT.Square,
                                             accum_out=rr[:, i:i + 1]).then_inc(r_sq, 1)
                    act.wait_ge(r_done, t + 1)
                    nc.scalar.activation(rr[:, 0:1], rr[:, 0:1], ACT.Ln, scale=1.0 / D, bias=eps[:, 0:1]).then_inc(r_ln, 1)
                    act.wait_ge(r_ln, 2 * t + 1)
                    nc.scalar.activation(rr[:, 0:1], rr[:, 0:1], ACT.Exp, scale=-0.5).then_inc(r_ln, 1)

            @block.tensor
            def _(pe):
                def sums(n):
                    pe.wait_ge(sq_done, n + 1)
                    if n >= 1:
                        pe.wait_ge(ln_done, 2 * n)
                    for i in range(2):
                        last = nc.tensor.matmul(p_ss[i][:], ones[:], sq[:, i * HALF:(i + 1) * HALF],
                                                start=True, stop=True)
                    last.then_inc(ss_done, 1)

                def three(bank, J, k, hi_rhs, lo_rhs, first, final):
                    hi, lo = w_hi[:, J % 2, k * P:(k + 1) * P], w_lo[:, J % 2, k * P:(k + 1) * P]
                    nc.tensor.matmul(bank, hi, hi_rhs, start=first, stop=False)
                    nc.tensor.matmul(bank, hi, lo_rhs, start=False, stop=False)
                    return nc.tensor.matmul(bank, lo, hi_rhs, start=False, stop=final)

                for J, (what, c) in enumerate(MERGE_JOBS):
                    pe.wait_ge(w_lo_done, J + 1)
                    if what == "ab":
                        if c == 0:
                            pe.wait_ge(yl, NY)
                            pe.wait_ge(ln_done, 2 * NY)
                        else:
                            pe.wait_ge(m2, c)
                        for q in range(2):
                            for i in range(2):
                                cut = slice(i * HALF, (i + 1) * HALF)
                                for k in range(HA):
                                    n = HA * q + k
                                    last = three(banks[4 + 2 * q + i][:], J, n, y_hi[:, n, cut], y_lo[:, n, cut],
                                                 k == 0, k == HA - 1)
                    else:
                        G = c + KD * (what == "gb")
                        if G >= 2:
                            pe.wait_ge(sg_done, 2 * (G - 1))
                        for i in range(2):
                            cut = slice(i * HALF, (i + 1) * HALF)
                            for k in range(KD):
                                last = three(banks[2 * (G % 2) + i][:], J, k, h_hi[:, k, cut], h_lo[:, k, cut],
                                             k == 0, k == KD - 1)
                            if i == 0 and what == "ga":
                                sums(c)
                    last.then_inc(job_done, 1)

                def residual(t):
                    pe.wait_ge(x_in[t % 2], 16 * (t // 2 + 1))
                    if t >= 2:
                        pe.wait_ge(fx, t - 1)
                    else:
                        pe.wait_ge(m2, KD)
                    for k in range(KD):
                        last = nc.tensor.transpose(banks[4 + 2 * (t % 2) + k // 4][:, (k % 4) * P:(k % 4 + 1) * P],
                                                   xt[t % 2][:, k, :], ident[:])
                    last.then_inc(x_ready, 1)

                for t in range(NT):
                    cut = slice(t * P, (t + 1) * P)
                    if t >= 2:
                        pe.wait_ge(t_done, 2 * (t - 1))
                    elif t == 0:
                        pe.wait_ge(sg_done, 4 * KD)
                    for k in range(KD):
                        if t == 0:
                            pe.wait_ge(wo_lo[k % 2], k // 2 + 1)
                            pe.wait_ge(mg_lo[k // (KD - 1)], k % (KD - 1) + 1)
                        for i in range(2):
                            c = slice(i * HALF, (i + 1) * HALF)
                            bank = banks[2 * (t % 2) + i][:]
                            nc.tensor.matmul(bank, h_hi[:, k, cut], y_hi[:, k, c], start=(k == 0), stop=False)
                            nc.tensor.matmul(bank, h_hi[:, k, cut], y_lo[:, k, c], start=False, stop=False)
                            last = nc.tensor.matmul(bank, h_lo[:, k, cut], y_hi[:, k, c], start=False,
                                                    stop=(k == KD - 1))
                    last.then_inc(o_ready, 1)
                    if t == 0:
                        residual(0)
                    if t + 1 < NT:
                        residual(t + 1)

            @block.vector
            def _(dve):
                def split_hi(J):
                    dve.wait_ge(w_in[J % 2], 16 * (J // 2 + 1))
                    if J >= 2:
                        dve.wait_ge(job_done, J - 1)
                    nc.vector.tensor_copy(w_hi[:, J % 2, :], w_raw[:, J % 2, :]).then_inc(w_hi_done, 1)

                def open_out(n):
                    if HA <= n < NY:
                        dve.wait_ge(in_a[n % 2], 16 * (n // 2 + 1))
                        nc.vector.tensor_tensor(ab[:, n % 2, :], ab[:, n % 2, :], y_hi[:, n, :].bitcast(F32), ALU.mult
                                                ).then_inc(ob_done, 1)

                split_hi(0)
                split_hi(1)
                dve.wait_ge(cst, 16)
                nc.vector.tensor_scalar(ny[:, 0:HA], ny[:, 0:HA], 0.8, None, ALU.mult).then_inc(nys, 1)
                dve.wait_ge(nys, 1)
                dve.wait_ge(in_g, 16 * (NY + HB))
                for n in range(NY):
                    b = ab[:, n % 2, :]
                    if n < HA:
                        dve.wait_ge(in_a[n % 2], 16 * (n // 2 + 1))
                    else:
                        dve.wait_ge(ob_done, n - HA + 1)
                    nc.vector.scalar_tensor_tensor(g1[:], b, ny[:, n:n + 1], y_lo[:, n, :].bitcast(F32),
                                                   ALU.mult, ALU.mult).then_inc(gz, 1)
                    dve.wait_ge(gz, n + 1)
                    dve.wait_ge(ri_done, n + 1)
                    nc.vector.tensor_tensor(b, g1[:], rinv[:], ALU.mult).then_inc(yb, 1)
                    dve.wait_ge(yb, n + 1)
                    nc.vector.tensor_copy(y_hi[:, n, :], b).then_inc(yh, 1)
                    open_out(n + 1)
                    split_hi(n + 2)
                for J in range(KD, NJ):
                    if J + 2 < NJ:
                        split_hi(J + 2)
                    what, c = MERGE_JOBS[J]
                    if what == "ab":
                        dve.wait_ge(job_done, J + 1)
                        dve.wait_ge(sg_done, 2 * (KD + c + 1))
                        for i in range(2):
                            cut = slice(i * HALF, (i + 1) * HALF)
                            last = nc.vector.tensor_tensor(mg[:, c, cut], banks[4 + i][:], mg[:, c, cut], ALU.mult)
                        last.then_inc(m1, 1)
                        for i in range(2):
                            cut = slice(i * HALF, (i + 1) * HALF)
                            last = nc.vector.tensor_tensor(sgb[:, cut], banks[6 + i][:], sgb[:, cut], ALU.mult)
                        last.then_inc(m2, 1)
                        dve.wait_ge(m1, c + 1)
                        dve.wait_ge(m2, c + 1)
                        nc.vector.tensor_tensor(mg[:, c, :], mg[:, c, :], sgb[:], ALU.add).then_inc(m3, 1)

                dve.wait_ge(mg_hi, KD)
                for k in range(1, KD, 2):
                    dve.wait_ge(wo_hi, k + 1)
                    nc.vector.tensor_tensor(y_lo[:, k, :], wo_raw[k], y_hi[:, k, :].bitcast(F32),
                                            ALU.subtract).then_inc(wo_lo[1], 1)
                    if k == 1:
                        nc.vector.tensor_tensor(h_lo[:, KD - 1, :], mg[:, KD - 1, :], h_hi[:, KD - 1, :].bitcast(F32),
                                                ALU.subtract).then_inc(mg_lo[1], 1)
                dve.wait_ge(np_in, 32)
                dve.wait_ge(wo_lo[0], KD // 2)
                dve.wait_ge(wo_lo[1], KD // 2)
                for t in range(NT):
                    dve.wait_ge(x_ready, t + 1)
                    if t >= 2:
                        dve.wait_ge(stored[t % 2], 16 * (t // 2))
                    for i in range(2):
                        c = slice(i * HALF, (i + 1) * HALF)
                        last = nc.vector.scalar_tensor_tensor(fin[t % 2][:, c], banks[4 + 2 * (t % 2) + i][:],
                                                              keep["rin_col"][:, t:t + 1], fgr[:, c],
                                                              ALU.mult, ALU.mult)
                    last.then_inc(fx, 1)
                    dve.wait_ge(r_sq, 2 * t + 2)
                    nc.vector.tensor_tensor(rr[:, 0:1], rr[:, 0:1], rr[:, 1:2], ALU.add).then_inc(r_done, 1)
                    dve.wait_ge(r_ln, 2 * t + 2)
                    if t >= 2:
                        dve.wait_ge(f_done, t - 1)
                    for i in range(2):
                        c = slice(i * HALF, (i + 1) * HALF)
                        nc.vector.scalar_tensor_tensor(tmp[t % 2][:, c], banks[2 * (t % 2) + i][:], rr[:, 0:1],
                                                       npost[:, c], ALU.mult, ALU.mult).then_inc(t_done, 1)
                    dve.wait_ge(t_done, 2 * t + 2)
                    dve.wait_ge(fx, t + 1)
                    nc.vector.tensor_tensor(fin[t % 2], fin[t % 2], tmp[t % 2][:], ALU.add).then_inc(f_done, 1)


def _tiles(w, starts, width=P):
    k = w.shape[0] // P
    out = []
    for cols in starts:
        pieces, at = [], 0
        for place, first, n in cols:
            if place > at:
                pieces.append(np.zeros((w.shape[0], place - at), w.dtype))
            pieces.append(w[:, first:first + n])
            at = place + n
        if at < width:
            pieces.append(np.zeros((w.shape[0], width - at), w.dtype))
        t = np.concatenate(pieces, axis=1)
        out.append(t.reshape(k, P, width).transpose(1, 0, 2).reshape(P, k * width))
    return np.ascontiguousarray(np.stack(out))


def _col(v):
    return np.ascontiguousarray(v.reshape(-1, P).transpose())


def _constants():
    s, t = np.meshgrid(np.arange(P), np.arange(P), indexing="ij")
    lev = np.zeros((P, LEVELS, P), np.float32)
    for l in range(LEVELS):
        n = 2 ** l
        lev[:, l, :] = (s // (2 * n) == t // (2 * n)) & (s % (2 * n) < n) & (t % (2 * n) >= n)
    q, c = np.meshgrid(np.arange(P), np.arange(T), indexing="ij")
    dist = q - (c - (T - P))
    alibi = np.stack([np.where(dist >= 0, 2.0 ** (-8.0 * (h + 1) / HA) * dist, -NEG) for h in range(HA)], axis=1)
    return {
        "ident": np.eye(P, dtype=np.float32),
        "ones": np.ones((P, P), np.float32),
        "tri": np.where(t >= s, 0.0, NEG).astype(np.float32),
        "lev": lev,
        "alibi": alibi.astype(np.float32),
    }


def _layout(inputs):
    a = {k: np.asarray(v) for k, v in inputs.items()}
    qk, vw = QK_HEADS * DH, V_HEADS * DH
    first = [[(0, 2 * qk + 2 * vw, 16), (32, 2 * qk + 2 * vw + 16, 16)]]
    conv = []
    for g in range(QK_HEADS + 1):
        if g < QK_HEADS:
            own = [g * P, qk + g * P, 2 * qk + 2 * g * P, 2 * qk + (2 * g + 1) * P]
            conv.append(own)
            first += [[(0, c, P)] for c in own]
        if g:
            first += [[(0, 2 * qk + vw + (2 * (g - 1) + q) * P, P)] for q in range(2)]
    cw = a["gdn_conv_w"][0]
    wa, wb = HA * 2 * DA, HB * DH
    gates2 = 4 * wa + 5 * wb
    at2 = {"qa": 0, "ka": wa, "va": 2 * wa, "za": 3 * wa, "qb": 4 * wa, "kb": 4 * wa + wb, "vb": 4 * wa + 2 * wb,
           "ob": 4 * wa + 3 * wb, "zb": 4 * wa + 4 * wb}
    second = [[(0, gates2 + HB, HB), (32, gates2, HB)]]
    for i in range(HB + 1):
        second += [[(0, at2[name] + i * P, P)] for name in MIX_JOBS[:6] if i < HB]
        second += [[(0, at2[name] + (i - 1) * P, P)] for name in MIX_JOBS[6:] if i]
    win2, cqk = a["w_in_2"][0], a["conv_qk_2"][0]
    gate0 = gates2 + 2 * HB
    ga = _tiles(win2, [[(0, gate0 + c * P, P)] for c in range(KD)])
    gb = _tiles(win2, [[(0, gate0 + D + c * P, P)] for c in range(KD)])
    wab = np.concatenate([_tiles(a["w_a_2"][0], [[(0, c * P, P)] for c in range(KD)]),
                          _tiles(a["w_b_2"][0], [[(0, c * P, P)] for c in range(KD)])], axis=2)
    m = {
        "xT": a["x"][0].transpose().reshape(KD, P, T).transpose(1, 0, 2),
        "c": _col(a["c"][0]),
        "ada_w": a["ada_w"][0],
        "ada_b": _col(a["ada_b"][0]),
        "norm_g": _col(a["norm_g"][0]),
        "w1": _tiles(a["gdn_w_in"][0], first),
        "conv_w": np.stack([np.stack([cw[:, c:c + P].transpose() for c in own], axis=1) for own in conv], axis=1),
        "norm_w": _col(a["gdn_norm_w"][0]),
        "w_out": a["gdn_w_out"][0],
        "final_g": _col(a["final_g"]),
        "final_row": a["final_g"].reshape(1, D),
        "norm_pre": _col(a["norm_pre_2"][0]),
        "w2": _tiles(win2, second),
        "conv_w2": np.stack([np.stack([cqk[:, i * P:(i + 1) * P].transpose(),
                                       cqk[:, wb + i * P:wb + (i + 1) * P].transpose()], axis=1)
                             for i in range(HB)], axis=1),
        "bif": np.stack([a["b_if_2"][0, HB:], a["b_if_2"][0, :HB]], axis=1),
        "lq": a["lambda_qk_2"].reshape(1, 4 * DA),
        "w3": np.stack([{"ga": ga, "gb": gb, "ab": wab}[what][c] for what, c in MERGE_JOBS]),
        "norm_y": np.concatenate([_col(a["norm_a_2"][0]), _col(a["norm_b_2"][0])], axis=1),
        "w_out2": a["w_out_2"][0],
        "norm_post": a["norm_post_2"],
        "adt": np.stack([a["gdn_a_log"][0], a["gdn_dt_bias"][0]], axis=1),
    }
    m.update(_constants())
    return {k: np.ascontiguousarray(v) for k, v in m.items()}


def build(nc, io):
    with ExitStack() as ctx:
        def sb(name, shape, dt=F32):
            return ctx.enter_context(nc.sbuf_tensor(name, shape, dt))

        keep = {
            "ident": sb("ident", [P, P]), "ones": sb("ones", [P, P]), "eps": sb("eps", [P, 1]),
            "gate": sb("gate", [P, KD]), "rin_col": sb("rin_col", [P, NT]),
            "h_hi": sb("h_hi", [P, KD, T], F32R), "h_lo": sb("h_lo", [P, KD, T], F32R),
            "const_in": ctx.enter_context(nc.semaphore("const_in")),
            "eps_set": ctx.enter_context(nc.semaphore("eps_set")),
        }
        stage_norm(nc, ctx, io, keep)
        with nc.cleanup_on_exit():
            stage_deltanet(nc, ctx, io, keep)
        with nc.cleanup_on_exit():
            stage_out(nc, ctx, io, keep)
        stage_mix(nc, ctx, io, keep)
        stage_merge(nc, ctx, io, keep)


SCRATCH = {
    "grows": (2 * V_HEADS, T),
    "z_scr": (V_HEADS, P, T),
    "o_scr": (V_HEADS, P, T),
    "x1_scr": (KD, P, T),
    "mrows": (2 * HB, T),
    "g_scr": (3 * HB, P, T),
    "a_scr": (HA + HB, P, T),
}


def kernel(**inputs):
    import concourse.bacc as bacc
    from concourse.bass_utils import run_bass_kernel_spmd

    arrays = _layout(inputs)
    nc = bacc.Bacc("TRN2", target_bir_lowering=False, num_devices=1)
    io = {}
    for name, a in arrays.items():
        io[name] = nc.dram_tensor("in_" + name, a.shape, F32, kind="ExternalInput").ap()
    for name, shape in SCRATCH.items():
        io[name] = nc.dram_tensor(name, shape, F32, kind="Internal").ap()
    io["out"] = nc.dram_tensor("out_x", (T, D), F32, kind="ExternalOutput").ap()
    build(nc, io)
    r = run_bass_kernel_spmd(nc, [{"in_" + name: a for name, a in arrays.items()}], core_ids=[0])
    return r.results[0]["out_x"].reshape(1, T, D)
```
